# Optimizing a Trainium2 kernel written in Bass

```python
import jax, jax.numpy as jnp
from jax import lax
import numpy as np

D_MODEL = 1024
BATCH = 1
SEQ = 1024
DEPTH = 2

CHUNK = 64
SUB = 16
SB_BLOCK = 128
HEAD_DIM = 128
GROUP_W = D_MODEL // 2
D_MIX = 2 * GROUP_W
H_A = GROUP_W // HEAD_DIM
H_B = GROUP_W // HEAD_DIM
H_C = GROUP_W // HEAD_DIM
DH_D = 64
H_D = GROUP_W // DH_D
CONV_A = 4
FFN_CONV = 3
D_FF = 2816
N_EVEN = (DEPTH + 1) // 2
N_ODD = DEPTH // 2
EVEN_IN = 8 * GROUP_W + 2 * H_A
ODD_IN = 7 * GROUP_W
ROPE_BASE = 10000.0
EPS = 1e-6

kernel_name = 'hybrid_streaming_encoder'

def _rms(x):
    xf = x.astype(jnp.float32)
    return xf * lax.rsqrt(jnp.mean(xf * xf, axis=-1, keepdims=True) + EPS)

def rms_norm(x, w):
    return (_rms(x) * w.astype(jnp.float32)).astype(x.dtype)

def modulate(x, shift, scale):
    return x * (1 + scale) + shift

def to_heads(x, n_heads):
    b, t, _ = x.shape
    return x.reshape(b, t, n_heads, -1).transpose(0, 2, 1, 3)

def from_heads(x):
    b, h, t, d = x.shape
    return x.transpose(0, 2, 1, 3).reshape(b, t, h * d)

def causal_dwconv(x, w, b):
    k_w, t = w.shape[0], x.shape[1]
    xp = jnp.pad(x, ((0, 0), (k_w - 1, 0), (0, 0)))
    y = b
    for i in range(k_w):
        y = y + xp[:, i:i + t] * w[i]
    return y

def rotary(x):
    t, d = x.shape[2], x.shape[3]
    inv_freq = ROPE_BASE ** (-jnp.arange(0, d, 2, dtype=jnp.float32) / d)
    ang = jnp.arange(t, dtype=jnp.float32)[:, None] * inv_freq[None, :]
    cos, sin = jnp.cos(ang), jnp.sin(ang)
    x1, x2 = x[..., : d // 2], x[..., d // 2:]
    return jnp.concatenate([x1 * cos - x2 * sin, x1 * sin + x2 * cos], axis=-1)

def _to_chunks(a):
    s = a.shape
    return jnp.moveaxis(a.reshape(s[:2] + (s[2] // CHUNK, CHUNK) + s[3:]), 2, 0)

def _from_chunks(a):
    a = jnp.moveaxis(a, 0, 2)
    s = a.shape
    return a.reshape(s[:2] + (s[2] * s[3],) + s[4:])

def gated_linear_recurrence(q, k, v, log_f):
    b_, h_, _, dk = q.shape
    dv = v.shape[-1]
    n_sub = CHUNK // SUB
    u = np.arange(SUB)
    blk = np.arange(n_sub)
    diag_mask = (blk[:, None, None, None] == blk[None, None, :, None]) & (u[None, :, None, None] >= u[None, None, None, :])
    earlier_mask = blk[None, None, :, None] < blk[:, None, None, None]

    def step(state, chunk):
        qc, kc, vc, gc = chunk
        cum = jnp.cumsum(gc, axis=2)
        cum_last = cum[:, :, -1:]
        o = jnp.einsum('bhtd,bhdv->bhtv', qc * jnp.exp(cum), state)
        ref = (cum - gc)[:, :, ::SUB]
        cum_s = cum.reshape(b_, h_, n_sub, SUB, dk)
        q_s = qc.reshape(b_, h_, n_sub, SUB, dk)
        k_s = kc.reshape(b_, h_, n_sub, SUB, dk)
        q_off = q_s * jnp.exp(cum_s - ref[:, :, :, None])
        k_off = kc[:, :, None] * jnp.exp(jnp.minimum(ref[:, :, :, None] - cum[:, :, None], 0.0))
        a_off = jnp.einsum('bhnud,bhnsd->bhnus', q_off, k_off).reshape(b_, h_, n_sub, SUB, n_sub, SUB)
        dec = jnp.exp(jnp.minimum(cum_s[:, :, :, :, None] - cum_s[:, :, :, None], 0.0))
        a_diag = jnp.einsum('bhnud,bhnsd,bhnusd->bhnus', q_s, k_s, dec)
        a = jnp.where(diag_mask, a_diag[:, :, :, :, None], jnp.where(earlier_mask, a_off, 0.0))
        o = o + jnp.einsum('bhts,bhsv->bhtv', a.reshape(b_, h_, CHUNK, CHUNK), vc)
        state = jnp.exp(cum_last[:, :, 0])[..., None] * state + jnp.einsum('bhsd,bhsv->bhdv', kc * jnp.exp(cum_last - cum), vc)
        return state, o

    s0 = jnp.zeros((b_, h_, dk, dv), jnp.float32)
    _, o = lax.scan(step, s0, (_to_chunks(q), _to_chunks(k), _to_chunks(v), _to_chunks(log_f)))
    return _from_chunks(o)

def mlstm_chunkwise(q, k, v, log_i, log_f):
    b_, h_, _, dk = q.shape
    dv = v.shape[-1]
    causal = np.tril(np.ones((CHUNK, CHUNK), dtype=bool))

    def step(carry, chunk):
        c_st, n_st, m = carry
        qc, kc, vc, ic, fc = chunk
        cum = jnp.cumsum(fc, axis=-1)
        log_d = jnp.where(causal, cum[..., :, None] - cum[..., None, :] + ic[..., None, :], -jnp.inf)
        log_inter = cum + m[..., None]
        m_t = jnp.maximum(log_inter, jnp.max(log_d, axis=-1))
        d = jnp.exp(log_d - m_t[..., None])
        w_inter = jnp.exp(log_inter - m_t)
        s = jnp.einsum('bhtd,bhsd->bhts', qc, kc) * d
        num = jnp.einsum('bhts,bhsv->bhtv', s, vc) + w_inter[..., None] * jnp.einsum('bhtd,bhdv->bhtv', qc, c_st)
        den = jnp.sum(s, axis=-1) + w_inter * jnp.einsum('bhtd,bhd->bht', qc, n_st)
        h = num / jnp.maximum(jnp.abs(den), jnp.exp(-m_t))[..., None]
        cum_last = cum[..., -1]
        log_w = cum_last[..., None] - cum + ic
        m_new = jnp.maximum(cum_last + m, jnp.max(log_w, axis=-1))
        w = jnp.exp(log_w - m_new[..., None])
        decay = jnp.exp(cum_last + m - m_new)
        c_new = decay[..., None, None] * c_st + jnp.einsum('bhs,bhsd,bhsv->bhdv', w, kc, vc)
        n_new = decay[..., None] * n_st + jnp.einsum('bhs,bhsd->bhd', w, kc)
        return (c_new, n_new, m_new), h

    carry0 = (jnp.zeros((b_, h_, dk, dv), jnp.float32), jnp.zeros((b_, h_, dk), jnp.float32), jnp.zeros((b_, h_), jnp.float32))
    _, h = lax.scan(step, carry0, (_to_chunks(q), _to_chunks(k), _to_chunks(v), _to_chunks(log_i), _to_chunks(log_f)))
    return _from_chunks(h)

def stick_breaking_attention(q, k, v):
    t_len = q.shape[2]
    scale = DH_D ** -0.5
    outs = []
    for blk in range(t_len // SB_BLOCK):
        q0, q1 = blk * SB_BLOCK, (blk + 1) * SB_BLOCK
        z = jnp.einsum('bhtd,bhsd->bhts', q[:, :, q0:q1], k[:, :, :q1]) * scale
        mask = np.arange(q1)[None, :] < np.arange(q0, q1)[:, None]
        log_rest = jnp.where(mask, jax.nn.log_sigmoid(-z), 0.0)
        tail = lax.cumsum(log_rest, axis=3, reverse=True) - log_rest
        a = jnp.where(mask, jnp.exp(jax.nn.log_sigmoid(z) + tail), 0.0)
        outs.append(jnp.einsum('bhts,bhsv->bhtv', a, v[:, :, :q1]))
    return jnp.concatenate(outs, axis=2)

def mixer_even(h, w_in, b_in, conv_w, conv_b, f_bias, norm_a, lb, norm_b, w_out):
    f32 = jnp.float32
    sizes = (2 * GROUP_W, GROUP_W, GROUP_W, H_A, H_A, GROUP_W, GROUP_W, GROUP_W, GROUP_W)
    p = h @ w_in + b_in
    qk_a, v_a, o_a, i_a, f_a, q_b, f_b, i_b, g_b = jnp.split(p, np.cumsum(sizes)[:-1].tolist(), axis=-1)
    qk_a = jax.nn.silu(causal_dwconv(qk_a, conv_w, conv_b))
    q_a, k_a = jnp.split(qk_a, 2, axis=-1)
    q_a = to_heads(q_a, H_A).astype(f32)
    k_a = to_heads(k_a, H_A).astype(f32) * HEAD_DIM ** -0.5
    v_a = to_heads(v_a, H_A).astype(f32)
    log_i = i_a.astype(f32).transpose(0, 2, 1)
    log_f = jax.nn.log_sigmoid((f_a + f_bias).astype(f32)).transpose(0, 2, 1)
    h_a = mlstm_chunkwise(q_a, k_a, v_a, log_i, log_f)
    y_a = from_heads(_rms(h_a)) * norm_a * jax.nn.sigmoid(o_a.astype(f32))
    z = to_heads(f_b, H_B).astype(f32)
    lb_h = lb.astype(f32).reshape(H_B, 1, HEAD_DIM)
    log_f_b = jnp.logaddexp(jnp.log(lb_h), jnp.log1p(-lb_h) + jax.nn.log_sigmoid(z))
    k_b = (1.0 - lb_h) * jax.nn.sigmoid(-z)
    q_bh = jax.nn.silu(to_heads(q_b, H_B).astype(f32))
    v_b = to_heads(i_b, H_B).astype(f32)
    o_b = gated_linear_recurrence(q_bh, k_b, v_b, log_f_b)
    y_b = from_heads(_rms(o_b)) * norm_b * jax.nn.silu(g_b.astype(f32))
    y = jnp.concatenate([y_a, y_b], axis=-1).astype(h.dtype)
    return y @ w_out

def mixer_odd(h, w_in, b_in, norm_c, w_out):
    f32 = jnp.float32
    p = h @ w_in + b_in
    q_c, k_c, v_c, g_c, q_d, k_d, v_d = jnp.split(p, [GROUP_W * i for i in range(1, 7)], axis=-1)
    q_ch = rotary(to_heads(q_c, H_C).astype(f32))
    k_ch = rotary(to_heads(k_c, H_C).astype(f32)) * HEAD_DIM ** -0.5
    v_ch = to_heads(v_c, H_C).astype(f32)
    log_gamma = jnp.log1p(-(2.0 ** (-5.0 - jnp.arange(H_C, dtype=f32))))
    g = jnp.broadcast_to(log_gamma[None, :, None, None], q_ch.shape)
    o_c = gated_linear_recurrence(q_ch, k_ch, v_ch, g)
    y_c = from_heads(_rms(o_c)) * norm_c * jax.nn.silu(g_c.astype(f32))
    o_d = stick_breaking_attention(to_heads(q_d, H_D).astype(f32), to_heads(k_d, H_D).astype(f32), to_heads(v_d, H_D).astype(f32))
    y = jnp.concatenate([y_c, from_heads(o_d)], axis=-1).astype(h.dtype)
    return y @ w_out

def conv_ffn(h, w_up, conv_w, conv_b, w_down):
    u = causal_dwconv(h @ w_up, conv_w, conv_b)
    a, g = jnp.split(u, 2, axis=-1)
    return (a * jax.nn.silu(g)) @ w_down

def setup_inputs(seed: int = 0) -> dict:
    key = jax.random.key(seed)
    ks = jax.random.split(key, 24)
    nrm = lambda i, shape, s: jax.random.normal(ks[i], shape, jnp.float32) * s
    d = D_MODEL
    return {
        'x': nrm(0, (BATCH, SEQ, d), 1.0),
        'c': nrm(1, (BATCH, d), 1.0),
        'w_ada': nrm(2, (d, 6 * d), d ** -0.5),
        'b_ada': nrm(3, (DEPTH, 6 * d), 0.02),
        'norm_mix': 1.0 + nrm(4, (DEPTH, d), 0.02),
        'norm_ffn': 1.0 + nrm(5, (DEPTH, d), 0.02),
        'norm_final': 1.0 + nrm(6, (d,), 0.02),
        'w_in_even': nrm(7, (N_EVEN, d, EVEN_IN), d ** -0.5),
        'b_in_even': nrm(8, (N_EVEN, EVEN_IN), 0.02),
        'conv_qk_w': nrm(9, (N_EVEN, CONV_A, 2 * GROUP_W), CONV_A ** -0.5),
        'conv_qk_b': nrm(10, (N_EVEN, 2 * GROUP_W), 0.02),
        'mlstm_f_bias': jnp.linspace(3.0, 6.0, H_A, dtype=jnp.float32)[None, :] + nrm(11, (N_EVEN, H_A), 0.1),
        'mlstm_norm': 1.0 + nrm(12, (N_EVEN, GROUP_W), 0.02),
        'hgrn_lb_logits': nrm(13, (N_EVEN, GROUP_W), 0.5),
        'hgrn_norm': 1.0 + nrm(14, (N_EVEN, GROUP_W), 0.02),
        'w_in_odd': nrm(15, (N_ODD, d, ODD_IN), d ** -0.5),
        'b_in_odd': nrm(16, (N_ODD, ODD_IN), 0.02),
        'ret_norm': 1.0 + nrm(17, (N_ODD, GROUP_W), 0.02),
        'w_out': nrm(18, (DEPTH, D_MIX, d), D_MIX ** -0.5),
        'ffn_up': nrm(19, (DEPTH, d, 2 * D_FF), d ** -0.5),
        'ffn_conv_w': nrm(20, (DEPTH, FFN_CONV, 2 * D_FF), FFN_CONV ** -0.5),
        'ffn_conv_b': nrm(21, (DEPTH, 2 * D_FF), 0.02),
        'ffn_down': nrm(22, (DEPTH, D_FF, d), D_FF ** -0.5),
    }

def reference(x, c, w_ada, b_ada, norm_mix, norm_ffn, norm_final, w_in_even, b_in_even, conv_qk_w, conv_qk_b, mlstm_f_bias, mlstm_norm, hgrn_lb_logits, hgrn_norm, w_in_odd, b_in_odd, ret_norm, w_out, ffn_up, ffn_conv_w, ffn_conv_b, ffn_down):
    ada = jax.nn.silu(c) @ w_ada
    lb_all = jnp.cumsum(jax.nn.softmax(hgrn_lb_logits.astype(jnp.float32), axis=0), axis=0)
    lb_all = lb_all - lb_all[:1]
    for layer in range(DEPTH):
        mod = (ada + b_ada[layer])[:, None, :]
        sh_m, sc_m, g_m, sh_f, sc_f, g_f = jnp.split(mod, 6, axis=-1)
        h = modulate(rms_norm(x, norm_mix[layer]), sh_m, sc_m)
        if layer % 2 == 0:
            e = layer // 2
            y = mixer_even(h, w_in_even[e], b_in_even[e], conv_qk_w[e], conv_qk_b[e], mlstm_f_bias[e], mlstm_norm[e], lb_all[e], hgrn_norm[e], w_out[layer])
        else:
            o = layer // 2
            y = mixer_odd(h, w_in_odd[o], b_in_odd[o], ret_norm[o], w_out[layer])
        x = x + g_m * y
        h = modulate(rms_norm(x, norm_ffn[layer]), sh_f, sc_f)
        x = x + g_f * conv_ffn(h, ffn_up[layer], ffn_conv_w[layer], ffn_conv_b[layer], ffn_down[layer])
    return rms_norm(x, norm_final)


_drawn_inputs = setup_inputs


def setup_inputs(seed=0):
    import zlib

    import numpy as np

    out = dict(_drawn_inputs(seed))
    spreads = {}
    factors = {'norm_mix': 3.514,
     'norm_ffn': 13.26,
     'norm_final': 20.19,
     'b_in_even': 4.264,
     'conv_qk_b': 64.0,
     'mlstm_norm': 59.774,
     'hgrn_norm': 26.879,
     'b_in_odd': 3.748,
     'ret_norm': 115.508,
     'ffn_conv_b': 13.978}
    for name, (base, spread) in spreads.items():
        noise = np.random.default_rng([zlib.crc32(name.encode()), seed]).standard_normal(out[name].shape)
        drawn = base * np.exp(spread * noise) if base else spread * noise
        out[name] = __import__('jax').numpy.asarray(drawn.astype(out[name].dtype))
    for name, factor in factors.items():
        out[name] = (out[name] * factor).astype(out[name].dtype)
    return out
```

```python
from contextlib import ExitStack

import numpy as np

import concourse.bass as bass
from concourse import mybir

F32 = mybir.dt.float32
F32R = mybir.dt.float32r
ALU = mybir.AluOpType
ACT = mybir.ActivationFunctionType
AX = mybir.AxisListType

P = 128
D = 1024
T = 1024
KT = D // P
HALF = 512
HEADS = 4
DH = 128
GROUP_W = HEADS * DH
CH = 128
NCH = T // CH
D_FF = 2816
FFT = D_FF // P
GROUPS = FFT // 2
H_D = 8
DH_D = 64
EPS = 1e-6
CONV_A = 4
FFN_CONV = 3
SCALE_A = float(DH) ** -0.5
SCALE_D = float(DH_D) ** -0.5
LEVELS = [1, 2, 4, 8, 16, 32, 64]
SMALL = 6

TQ, TK, TV, TGA, TGB = 0, 4, 8, 12, 16

N_PROJ_A, N_PROJ_B, N_PROJ_D, N_PROJ_C = 17, 16, 12, 16
N_OUT, N_FFN = 8, 66


def columns():
    sizes = [("c", 8), ("b_ada", 96), ("norm_mix", 16), ("norm_ffn", 16), ("norm_final", 8),
             ("b_even", 32), ("b_gate", 1), ("f_bias", 1), ("conv_qk_w", 8 * CONV_A), ("conv_qk_b", 8),
             ("mlstm_norm", 4), ("lb_logits", 4), ("hgrn_norm", 4), ("b_odd", 28), ("ret_norm", 4),
             ("ffn_w0", 6 * FFT), ("ffn_w1", 6 * FFT), ("ffn_b", 4 * FFT), ("eps", 1)]
    out, at = {}, 0
    for name, n in sizes:
        out[name] = at
        at += n
    out["all"] = at
    return out


COL = columns()

TAB = {}
_at = 0
for _name, _n in (("ident", 128), ("ones", 128), ("causal", 128), ("levels", SMALL * 32), ("sel", 512),
                  ("strict", 128), ("loose", 128), ("swap", 128), ("decay", 512), ("gq", 512), ("gk", 4), ("gc", 4),
                  ("cos", 1024), ("sin", 1024)):
    TAB[_name] = (_at, _n)
    _at += _n
N_TAB = _at


def in_pairs(eng, start, stop, body):
    turns = (stop - start) // 2
    if turns > 0:
        with eng.Fori(0, turns) as i:
            for u in range(2):
                body(i * 2 + (start + u), u, i)
    if (stop - start) % 2:
        body(stop - 1, 0, turns)


def flat(ap):
    return ap.rearrange("p a n -> p (a n)")


class Trunk:
    def __init__(self, nc, ctx, xT, params, tables, w_ada, w_units, outT):
        self.nc, self.ctx = nc, ctx
        self.xT, self.params_d, self.tables, self.w_ada, self.w_units, self.outT = xT, params, tables, w_ada, w_units, outT
        self.x_spill = nc.dram_tensor("x_spill", (P, KT * T), F32, kind="Internal").ap()
        self.held, self.mine, self.before = ExitStack(), [], []
        self.unit = 0
        self.top = 16512
        place = self.place
        self.ident = place("ident", [P, 128], F32)
        self.ones = place("ones", [P, 128], F32)
        self.par = place("par", [P, COL["all"]], F32)
        self.mod = place("mod", [P, 2, 48], F32)
        self.modA = place("modA", [P, 4, 8], F32)
        self.lb = place("lb", [P, 3, 4], F32)
        self.silu_c = place("silu_c", [P, 8], F32)
        self.small = place("small", [P, 8, 32], F32)
        self.top = 16512 + 7680
        self.w_raw = place("w_raw", [P, 2, 1024], F32)
        self.w_hi = place("w_hi", [P, 2, 1024], F32R)
        self.w_lo = place("w_lo", [P, 2, 1024], F32R)
        self.X0 = self.top
        self.x = place("x", [P, KT, T], F32)
        self.H0 = self.top
        self.hh = place("hh", [P, KT, T], F32R)
        self.hl = place("hl", [P, KT, T], F32R)
        self.M0 = self.top
        self.m = place("m", [P, 20, T], F32)
        self.psum = ctx.enter_context(nc.psum_tensor("ps", [P, 8, HALF], F32))
        self.n_place = 0

    def place(self, name, shape, dt):
        n = 4
        for s in shape[1:]:
            n *= s
        t = self.nc.alloc_sbuf_tensor_at(name, shape, dt, offset=self.top)
        self.top += (n + 31) // 32 * 32
        assert self.top <= 229368, (name, self.top)
        return t

    def work(self, start, limit, **shapes):
        keep, self.top, out = self.top, start, []
        self.n_place += 1
        for name, shape in shapes.items():
            dt = F32
            if isinstance(shape, tuple):
                shape, dt = shape
            out.append(self.place(f"{name}_{self.n_place}", shape, dt))
        assert self.top <= start + limit, (self.top - start, limit)
        self.top = keep
        return out

    def sems(self, phase, *names):
        new = [self.held.enter_context(self.nc.semaphore(f"{phase}_{n}")) for n in names]
        self.mine += new
        return new

    def phase(self, build):
        self.before, self.mine, last = self.mine, [], self.held
        self.held = ExitStack()
        build()
        last.close()

    def clear_before(self, eng):
        for s in self.before:
            eng.sem_clear(s)

    def col(self, name, i=0):
        if isinstance(i, int):
            return self.par[:, COL[name] + i:COL[name] + i + 1]
        return self.par[:, bass.ds(i + COL[name], 1)]

    def pair(self, q):
        return self.psum[:, 2 * q:2 * q + 2, :].rearrange("p a n -> p (a n)")

    def bank(self, b, n=HALF):
        return self.psum[:, b, 0:n]

    def stream_sems(self, name):
        return self.sems(name, "loaded_even", "loaded_odd", "hi", "split", "unit_done")

    def load_units(self, eng, sems, n):
        first = self.unit
        loaded, split = sems[0:2], sems[3]
        last = min(n + 2, TOTAL_UNITS - first)

        def load(j, slot, turn):
            eng.wait_ge(split, j - 2)
            place = (first + slot) % 2
            src = self.w_units[bass.ds(j + first, 1), :, :].rearrange("a p n -> p (a n)")
            eng.dma_start(self.w_raw[:, place, :], src).then_inc(loaded[slot], 16)
        in_pairs(eng, 2, last, load)
        count = last - 2
        eng.wait_ge(loaded[0], 16 * ((count + 1) // 2))
        if count > 1:
            eng.wait_ge(loaded[1], 16 * (count // 2))

    def split_units(self, eng, sems, n):
        first = self.unit
        loaded, hi, split, done = sems[0:2], sems[2], sems[3], sems[4]
        raw, w_hi, w_lo = self.w_raw, self.w_hi, self.w_lo
        one = self.ones[:, 0:1].to_broadcast([P, 1024])

        place = (first + 1) % 2
        eng.tensor_tensor(w_hi[:, place, :], raw[:, place, :], one, ALU.mult).then_inc(hi, 1)
        eng.wait_ge(hi, 1)
        eng.tensor_tensor(w_lo[:, place, :], raw[:, place, :], w_hi[:, place, :].bitcast(F32),
                          ALU.subtract).then_inc(split, 1)
        stop = min(n + 1, TOTAL_UNITS - first)

        def rest(j, slot, turn):
            place = (first + slot) % 2
            eng.wait_ge(loaded[slot], (turn + 1) * 16)
            eng.wait_ge(done, j - 1)
            eng.tensor_tensor(w_hi[:, place, :], raw[:, place, :], one, ALU.mult).then_inc(hi, 1)
            eng.wait_ge(hi, j)
            eng.tensor_tensor(w_lo[:, place, :], raw[:, place, :], w_hi[:, place, :].bitcast(F32),
                              ALU.subtract).then_inc(split, 1)
        in_pairs(eng, 2, stop, rest)

    def multiply(self, place, psum_pair, rhs_hi, rhs_lo):
        nc = self.nc
        for k in range(KT):
            w_hi = self.w_hi[:, place, k * P:(k + 1) * P]
            w_lo = self.w_lo[:, place, k * P:(k + 1) * P]
            for n, (w, r) in enumerate(((w_hi, rhs_hi), (w_hi, rhs_lo), (w_lo, rhs_hi))):
                for half in range(2):
                    mm = nc.tensor.matmul(self.bank(2 * psum_pair + half), w,
                                          r[:, k, half * HALF:(half + 1) * HALF],
                                          start=(k == 0 and n == 0), stop=(k == KT - 1 and n == 2))
        return mm


TOTAL_UNITS = N_PROJ_A + N_PROJ_B + N_PROJ_D + N_PROJ_C + 2 * (N_OUT + N_FFN)


def start(k):
    nc = k.nc
    par_in, x_in, ring0, ring1, ring2, ring3, prime, c_ready, hi, split, ada_mm, chain = k.sems(
        "start", "par", "x", "ada_in0", "ada_in1", "ada_in2", "ada_in3", "prime", "silu_c", "hi", "split", "ada", "chain")
    ring = (ring0, ring1, ring2, ring3)
    buf, = k.work(k.H0, 131072, ada_w=[P, 4, 4, KT, P])
    n_load = 48 // 4
    lbt, = k.work(k.M0 + 8192, 8192, lbt=[P, 2, 4])

    with nc.Block() as block:
        @block.sync
        def _(sp):
            sp.dma_start(k.par[:, :], k.params_d).then_inc(par_in, 16)
            sp.dma_start(k.ident[:, :], k.tables[:, TAB["ident"][0]:TAB["ident"][0] + 128]).then_inc(par_in, 16)
            sp.dma_start(k.ones[:, :], k.tables[:, TAB["ones"][0]:TAB["ones"][0] + 128]).then_inc(par_in, 16)
            for n in range(4):
                sp.dma_start(buf[:, n], k.w_ada[n]).then_inc(ring[n], 16)
            with sp.Fori(0, n_load // 4 - 1) as i:
                for s in range(4):
                    sp.wait_ge(ada_mm, i * 4 + s + 1)
                    sp.dma_start(buf[:, s].rearrange("p a k n -> p (a k n)"),
                                 k.w_ada[bass.ds(i * 4 + (s + 4), 1)].rearrange("z p a k n -> p (z a k n)")).then_inc(ring[s], 16)
            for s in range(2):
                sp.dma_start(k.w_raw[:, s, :], k.w_units[s]).then_inc(prime, 16)
            sp.dma_start(flat(k.x[:, :, :]), k.xT).then_inc(x_in, 16)
            sp.wait_ge(x_in, 16)

        @block.scalar
        def _(act):
            act.wait_ge(par_in, 48)
            nc.scalar.activation(k.silu_c[:, :], k.par[:, COL["c"]:COL["c"] + 8], ACT.Silu).then_inc(c_ready, 1)

        @block.gpsimd
        def _(pool):
            k.clear_before(pool)
            pool.wait_ge(prime, 32)
            pool.tensor_copy(k.w_hi[:, 0, :], k.w_raw[:, 0, :]).then_inc(hi, 1)
            pool.wait_ge(hi, 1)
            pool.tensor_tensor(k.w_lo[:, 0, :], k.w_raw[:, 0, :], k.w_hi[:, 0, :].bitcast(F32), ALU.subtract).then_inc(split, 1)

        @block.tensor
        def _(pe):
            pe.wait_ge(c_ready, 1)
            for n in range(n_load):
                pe.wait_ge(ring[n % 4], 16 * (n // 4 + 1))
                for a in range(4):
                    for kk in range(KT):
                        mm = nc.tensor.matmul(k.psum[:, 0, 4 * n + a:4 * n + a + 1], buf[:, n % 4, a, kk, :],
                                              k.silu_c[:, kk:kk + 1], start=(kk == 0), stop=(kk == KT - 1))
                mm.then_inc(ada_mm, 1)

        @block.vector
        def _(dve):
            step = [0]

            def link(ins):
                ins.then_inc(chain, 1)
                step[0] += 1
                dve.wait_ge(chain, step[0])
            dve.wait_ge(ada_mm, n_load)
            dve.wait_ge(par_in, 48)
            for layer in range(2):
                b = k.par[:, COL["b_ada"] + 48 * layer:COL["b_ada"] + 48 * layer + 48]
                link(nc.vector.tensor_tensor(k.mod[:, layer, :], k.psum[:, 0, 0:48], b, ALU.add))
            for layer in range(2):
                for n, (norm, at) in enumerate((("norm_mix", 8), ("norm_ffn", 32))):
                    w = k.par[:, COL[norm] + 8 * layer:COL[norm] + 8 * layer + 8]
                    link(nc.vector.scalar_tensor_tensor(k.modA[:, 2 * layer + n, :], k.mod[:, layer, at:at + 8], 1.0, w,
                                                        ALU.add, ALU.mult))
            lg = k.par[:, COL["lb_logits"]:COL["lb_logits"] + 4]
            link(nc.vector.tensor_tensor(lbt[:, 0, :], lg, lg, ALU.subtract))
            dve.wait_ge(c_ready, 2)
            link(nc.vector.reciprocal(lbt[:, 1, :], k.lb[:, 2, :]))
            link(nc.vector.tensor_tensor(k.lb[:, 2, :], k.lb[:, 2, :], lbt[:, 1, :], ALU.mult))
            link(nc.vector.tensor_tensor(k.lb[:, 0, :], k.lb[:, 2, :], k.lb[:, 2, :], ALU.subtract))
            link(nc.vector.tensor_scalar(k.lb[:, 1, :], k.lb[:, 0, :], -1.0, 1.0, ALU.mult, ALU.add))

        @block.scalar
        def _(act):
            act.wait_ge(chain, 7)
            nc.scalar.activation(k.lb[:, 2, :], lbt[:, 0, :], ACT.Exp).then_inc(c_ready, 1)


def norm(k, name, scale, shift, spill, out=False):
    nc = k.nc
    sq_ready, sum_done, rs_ready, rs_ln, xr, hb_ready, hi_ready, lo_done, spilled = k.sems(
        name, "sq", "sum", "rs", "ln", "xr", "hb", "hi", "lo", "spilled")
    sq, rs, tmp, hb = k.work(k.M0, 81920, sq=[P, 2, T], rs=[P, T], tmp=[P, 2, T], hb=[P, 2, T])
    hb_out, = k.work(k.H0, 32768, hb_out=[P, KT, T]) if out else (None,)

    with nc.Block() as block:
        @block.sync
        def _(sp):
            if spill:
                sp.dma_start(k.x_spill, flat(k.x[:, :, :])).then_inc(spilled, 16)
                sp.wait_ge(spilled, 16)
            if out:
                for i in range(KT):
                    sp.wait_ge(hb_ready, i + 1)
                    sp.dma_start(k.outT[:, i, :], hb_out[:, i, :]).then_inc(spilled, 16)
                sp.wait_ge(spilled, 16 * KT)

        @block.gpsimd
        def _(pool):
            k.clear_before(pool)

        @block.scalar
        def _(act):
            for i in range(KT):
                if i >= 2:
                    act.wait_ge(sum_done, i - 1)
                nc.scalar.activation(sq[:, i % 2, :], k.x[:, i, :], ACT.Square).then_inc(sq_ready, 1)
            act.wait_ge(sum_done, KT)
            nc.scalar.activation(rs[:, :], k.pair(0), ACT.Ln, bias=k.col("eps"), scale=1.0 / D).then_inc(rs_ln, 1)
            act.wait_ge(rs_ln, 1)
            nc.scalar.activation(rs[:, :], rs[:, :], ACT.Exp, scale=-0.5).then_inc(rs_ready, 1)
            if not out:
                for i in range(KT):
                    act.wait_ge(hb_ready, i + 1)
                    nc.scalar.activation(k.hh[:, i, :], hb[:, i % 2, :], ACT.Copy).then_inc(hi_ready, 1)

        @block.tensor
        def _(pe):
            for i in range(KT):
                pe.wait_ge(sq_ready, i + 1)
                for half in range(2):
                    mm = nc.tensor.matmul(k.bank(half), k.ones[:, :], sq[:, i % 2, half * HALF:(half + 1) * HALF],
                                          start=(i == 0), stop=(i == KT - 1))
                mm.then_inc(sum_done, 1)

        def lo(dve, i):
            dve.wait_ge(hi_ready, i + 1)
            nc.vector.tensor_tensor(k.hl[:, i, :], hb[:, i % 2, :], k.hh[:, i, :].bitcast(F32),
                                    ALU.subtract).then_inc(lo_done, 1)

        @block.vector
        def _(dve):
            dve.wait_ge(rs_ready, 1)
            for i in range(KT):
                if out:
                    if i >= 2:
                        dve.wait_ge(hb_ready, i - 1)
                else:
                    if i >= 2:
                        dve.wait_ge(lo_done, i - 1)
                nc.vector.tensor_tensor(tmp[:, i % 2, :], k.x[:, i, :], rs[:, :], ALU.mult).then_inc(xr, 1)
                dve.wait_ge(xr, i + 1)
                if out:
                    nc.vector.tensor_scalar(hb_out[:, i, :], tmp[:, i % 2, :], scale[:, i:i + 1], None,
                                            ALU.mult).then_inc(hb_ready, 1)
                    continue
                nc.vector.tensor_scalar(hb[:, i % 2, :], tmp[:, i % 2, :], scale[:, i:i + 1], shift[:, i:i + 1],
                                        ALU.mult, ALU.add).then_inc(hb_ready, 1)
                if i >= 1:
                    lo(dve, i - 1)
            if not out:
                lo(dve, KT - 1)


def project(k, name, n_units, segments, gate_rows=None, f_tile=None):
    nc = k.nc
    S = k.stream_sems(name)
    done = S[4]
    free, p_ready, tap_done, conv_done, negated = k.sems(
        name, "psum_free", "p_ready", "tap_done", "conv_done", "negated")
    pbuf, cbuf = k.work(k.X0, 16384, p=[P, 2, T], cv=[P, 2, T]) if name.endswith("A") else (None, None)
    first = k.unit

    with nc.Block() as block:
        @block.sync
        def _(sp):
            k.load_units(sp, S, n_units)

        @block.gpsimd
        def _(pool):
            k.clear_before(pool)
            k.split_units(pool, S, n_units)

        @block.tensor
        def _(pe):
            def unit(j, slot, turn):
                pe.wait_ge(S[3], j)
                pe.wait_ge(free, j + 1)
                k.multiply((first + slot) % 2, slot, k.hh, k.hl).then_inc(done, 1)
            in_pairs(pe, 0, n_units, unit)

        @block.scalar
        def _(act):
            act.sem_inc(free, 2)
            at = 0
            for kind, tile, bias, extra, n in segments:
                def unit(j, slot, turn, kind=kind, tile=tile, bias=bias, at=at):
                    ps = k.pair((at + slot) % 2)
                    act.wait_ge(done, j + (at + 1))
                    dst = flat(k.m[:, bass.ds(j + tile, 1), :])
                    b = k.col(bias[0], j + bias[1])
                    if kind == "conv":
                        nc.scalar.activation(pbuf[:, slot, :], ps, ACT.Identity, bias=b).then_inc(p_ready, 1)
                        act.wait_ge(conv_done, j + 1)
                        nc.scalar.activation(dst, cbuf[:, slot, :], ACT.Silu).then_inc(free, 1)
                    elif kind == "copy":
                        nc.scalar.activation(dst, ps, ACT.Identity, bias=b).then_inc(free, 1)
                    elif kind == "silu":
                        nc.scalar.activation(dst, ps, ACT.Silu, bias=b).then_inc(free, 1)
                    elif kind == "gate_sigmoid":
                        nc.scalar.activation(dst, ps, ACT.Sigmoid, bias=b).then_inc(free, 1)
                    elif kind == "gate_silu":
                        nc.scalar.activation(dst, ps, ACT.Silu, bias=b).then_inc(free, 1)
                    elif kind == "forget":
                        nc.scalar.activation(flat(f_tile[:, bass.ds(j, 1), :]), ps, ACT.Sigmoid, bias=b)
                        nc.scalar.activation(dst, ps, ACT.Sigmoid, scale=-1.0,
                                             bias=k.small[:, 0, bass.ds(j, 1)]).then_inc(free, 1)
                if kind == "rows":
                    act.wait_ge(done, at + 1)
                    ps = k.pair(at % 2)
                    g0 = COL["b_gate"]
                    nc.scalar.activation(gate_rows[0], ps[0:4, :], ACT.Identity, bias=k.par[0:4, g0:g0 + 1])
                    nc.scalar.activation(gate_rows[1], ps[32:36, :], ACT.Identity, bias=k.par[32:36, g0:g0 + 1]).then_inc(free, 1)
                else:
                    if kind == "forget":
                        act.wait_ge(negated, 1)
                    in_pairs(act, 0, n, unit)
                at += n

        @block.vector
        def _(dve):
            at = 0
            for kind, tile, bias, extra, n in segments:
                if kind == "conv":
                    def conv(j, slot, turn):
                        c = cbuf[:, slot, :]
                        dve.wait_ge(p_ready, j + 1)
                        dve.wait_ge(free, j + 1)
                        nc.vector.tensor_scalar(c, pbuf[:, slot, :], k.col("conv_qk_w", j + 8 * (CONV_A - 1)),
                                                k.col("conv_qk_b", j), ALU.mult, ALU.add).then_inc(tap_done, 1)
                        for lag in range(1, CONV_A):
                            dve.wait_ge(tap_done, j * (CONV_A - 1) + lag)
                            nc.vector.scalar_tensor_tensor(
                                cbuf[:, slot, lag:T], pbuf[:, slot, 0:T - lag], k.col("conv_qk_w", j + 8 * (CONV_A - 1 - lag)),
                                cbuf[:, slot, lag:T], ALU.mult, ALU.add).then_inc(conv_done if lag == CONV_A - 1 else tap_done, 1)
                    in_pairs(dve, 0, n, conv)
                elif kind in ("gate_sigmoid", "gate_silu"):
                    def gate(j, slot, turn, tile=tile, extra=extra, at=at):
                        dst = flat(k.m[:, bass.ds(j + tile, 1), :])
                        dve.wait_ge(free, j + (at + 3))
                        nc.vector.tensor_scalar(dst, dst, k.col(extra, j), None, ALU.mult)
                    in_pairs(dve, 0, n, gate)
                elif kind == "forget":
                    b0 = COL[bias[0]] + bias[1]
                    nc.vector.tensor_scalar(k.small[:, 0, 0:4], k.par[:, b0:b0 + 4], -1.0, None, ALU.mult).then_inc(negated, 1)

                    def forget(j, slot, turn, tile=tile, at=at):
                        f = flat(f_tile[:, bass.ds(j, 1), :])
                        dst = flat(k.m[:, bass.ds(j + tile, 1), :])
                        dve.wait_ge(free, j + (at + 3))
                        nc.vector.tensor_scalar(f, f, k.lb[:, 1, bass.ds(j, 1)], k.lb[:, 0, bass.ds(j, 1)], ALU.mult, ALU.add)
                        nc.vector.tensor_scalar(dst, dst, k.lb[:, 1, bass.ds(j, 1)], None, ALU.mult)
                    in_pairs(dve, 0, n, forget)
                at += n
    k.unit += n_units


def out_project(k, name, layer):
    nc = k.nc
    S = k.stream_sems(name)
    done = S[4]
    free, hi_done, y_split, x_in = k.sems(name, "psum_free", "y_hi", "y_split", "x_back")
    first = k.unit
    gate = k.mod[:, layer, 16:24]

    with nc.Block() as block:
        @block.sync
        def _(sp):
            sp.dma_start(flat(k.x[:, :, :]), k.x_spill).then_inc(x_in, 16)
            k.load_units(sp, S, N_OUT)

        @block.gpsimd
        def _(pool):
            k.clear_before(pool)
            k.split_units(pool, S, N_OUT)

        @block.scalar
        def _(act):
            for i in range(KT):
                nc.scalar.activation(k.hh[:, i, :], k.m[:, TGA + i, :], ACT.Copy).then_inc(hi_done, 1)

        @block.tensor
        def _(pe):
            pe.wait_ge(y_split, KT)

            def unit(j, slot, turn):
                pe.wait_ge(S[3], j)
                pe.wait_ge(free, j + 1)
                k.multiply((first + slot) % 2, slot, k.hh, k.hl).then_inc(done, 1)
            in_pairs(pe, 0, N_OUT, unit)

        @block.vector
        def _(dve):
            dve.sem_inc(free, 2)
            for i in range(KT):
                dve.wait_ge(hi_done, i + 1)
                nc.vector.tensor_tensor(k.hl[:, i, :], k.m[:, TGA + i, :], k.hh[:, i, :].bitcast(F32),
                                        ALU.subtract).then_inc(y_split, 1)
            dve.wait_ge(x_in, 16)

            def unit(j, slot, turn):
                x = flat(k.x[:, bass.ds(j, 1), :])
                dve.wait_ge(done, j + 1)
                nc.vector.scalar_tensor_tensor(x, k.pair(slot), gate[:, bass.ds(j, 1)], x, ALU.mult, ALU.add).then_inc(free, 1)
            in_pairs(dve, 0, N_OUT, unit)
    k.unit += N_OUT


def ffn(k, name, layer):
    nc = k.nc
    S = k.stream_sems(name)
    done = S[4]
    newest, tap1, tap_done, silu_done, prod, hi_done, split_done, down_done, down_free = k.sems(
        name, "newest_tap", "tap1", "taps_done", "silu_done", "product", "a_hi", "a_split", "down_done", "down_free")
    a_hi, a_lo, conv, sg = k.work(k.M0, 81920, a_hi=([P, 2, 2, T], F32R), a_lo=([P, 2, 2, T], F32R),
                                  cv=[P, 4, T], sg=[P, 2, T])
    first = k.unit
    gate = k.mod[:, layer, 40:48]
    W = [("ffn_w0", 3 * FFT * layer), ("ffn_w1", 3 * FFT * layer)]

    def cols(kind, g, u):
        tile = g * 2 + (u // 2 + (u % 2) * FFT)
        if kind == 3:
            return k.col("ffn_b", tile + 2 * FFT * layer)
        at = kind * 2 * FFT + FFN_CONV * 2 * FFT * layer
        return k.col("ffn_w0", tile + at)

    with nc.Block() as block:
        @block.sync
        def _(sp):
            k.load_units(sp, S, N_FFN)

        @block.gpsimd
        def _(pool):
            k.clear_before(pool)
            k.split_units(pool, S, N_FFN)

        @block.tensor
        def _(pe):
            def up(g, unit0):
                for u in range(4):
                    pe.wait_ge(S[3], unit0 + u)
                    pe.wait_ge(tap_done, g * 4 + (u + 1))
                    k.multiply((first + u) % 2, u % 2, k.hh, k.hl).then_inc(done, 1)

            def down(g, parity, unit0):
                pe.wait_ge(split_done, g * 2 + 2)
                for u in range(2):
                    place = (first + u) % 2
                    pe.wait_ge(S[3], unit0 + u)
                    for o in range(4):
                        pe.wait_ge(down_free, g * 8 + (4 * u + o + 1))
                        for kk in range(2):
                            w_hi = k.w_hi[:, place, kk * HALF + o * P:kk * HALF + (o + 1) * P]
                            w_lo = k.w_lo[:, place, kk * HALF + o * P:kk * HALF + (o + 1) * P]
                            for n, (w, r) in enumerate(((w_hi, a_hi), (w_hi, a_lo), (w_lo, a_hi))):
                                for half in range(2):
                                    mm = nc.tensor.matmul(k.bank(4 + 2 * (o % 2) + half), w,
                                                          r[:, parity, kk, half * HALF:(half + 1) * HALF],
                                                          start=(kk == 0 and n == 0), stop=(kk == 1 and n == 2))
                        mm.then_inc(done if o == 3 else down_done, 1)

            up(0, 0)
            with pe.Fori(0, (GROUPS - 1) // 2) as i:
                for v in range(2):
                    g = i * 2 + (1 + v)
                    up(g, i * 12 + (6 * v + 4))
                    down(i * 2 + v, v, i * 12 + (6 * v + 8))
            down(GROUPS - 1, (GROUPS - 1) % 2, N_FFN - 2)

        @block.scalar
        def _(act):
            def group(g, parity, unit0):
                for u in range(4):
                    act.wait_ge(done, unit0 + (u + 1))
                    act.wait_ge(split_done, g * 2)
                    nc.scalar.activation(conv[:, u, :], k.pair(u % 2), ACT.Identity, bias=cols(3, g, u),
                                         scale=cols(2, g, u)).then_inc(newest, 1)
                    if u % 2:
                        act.wait_ge(tap_done, g * 4 + (u + 3))
                        nc.scalar.activation(sg[:, u // 2, :], conv[:, u, :], ACT.Silu).then_inc(silu_done, 1)
                        act.wait_ge(prod, g * 2 + (u // 2 + 1))
                        nc.scalar.activation(a_hi[:, parity, u // 2, :], conv[:, u - 1, :], ACT.Copy).then_inc(hi_done, 1)

            group(0, 0, 0)
            with act.Fori(0, (GROUPS - 1) // 2) as i:
                for v in range(2):
                    group(i * 2 + (1 + v), (1 + v) % 2, i * 12 + (6 * v + 4))

        @block.vector
        def _(dve):
            def up(g, parity):
                for u in range(4):
                    ps = k.pair(u % 2)
                    dve.wait_ge(newest, g * 4 + (u + 1))
                    nc.vector.scalar_tensor_tensor(conv[:, u, 1:T], ps[:, 0:T - 1], cols(1, g, u), conv[:, u, 1:T],
                                                   ALU.mult, ALU.add).then_inc(tap1, 1)
                    dve.wait_ge(tap1, g * 4 + (u + 1))
                    nc.vector.scalar_tensor_tensor(conv[:, u, 2:T], ps[:, 0:T - 2], cols(0, g, u), conv[:, u, 2:T],
                                                   ALU.mult, ALU.add).then_inc(tap_done, 1)
                    if u % 2:
                        dve.wait_ge(silu_done, g * 2 + (u // 2 + 1))
                        nc.vector.tensor_tensor(conv[:, u - 1, :], conv[:, u - 1, :], sg[:, u // 2, :],
                                                ALU.mult).then_inc(prod, 1)
                        dve.wait_ge(hi_done, g * 2 + (u // 2 + 1))
                        nc.vector.tensor_tensor(a_lo[:, parity, u // 2, :], conv[:, u - 1, :],
                                                a_hi[:, parity, u // 2, :].bitcast(F32), ALU.subtract).then_inc(split_done, 1)

            def down(g, unit0):
                for o in range(KT):
                    if o % 4 == 3:
                        dve.wait_ge(done, unit0 + (o // 4 + 1))
                    else:
                        dve.wait_ge(down_done, g * 6 + (o // 4 * 3 + o % 4 + 1))
                    nc.vector.scalar_tensor_tensor(k.x[:, o, :], k.pair(2 + o % 2), gate[:, o:o + 1], k.x[:, o, :],
                                                   ALU.mult, ALU.add).then_inc(down_free, 1)
            dve.sem_inc(tap_done, 2)
            dve.sem_inc(down_free, 2)
            up(0, 0)
            with dve.Fori(0, (GROUPS - 1) // 2) as i:
                for v in range(2):
                    up(i * 2 + (1 + v), (1 + v) % 2)
                    down(i * 2 + v, i * 12 + (6 * v + 8))
            down(GROUPS - 1, N_FFN - 2)
    k.unit += N_FFN


def chunk(ap4, c):
    return ap4[:, :, bass.ds(c * CH, CH)]


def mix_a(k):
    nc = k.nc
    q, kk, v = k.m[:, TQ:TQ + 4, :], k.m[:, TK:TK + 4, :], k.m[:, TV:TV + 4, :]
    rows = k.m[0:4, TGB:TGB + 4, :]
    (k_st, v_st, vaug, pr, qs, kw, dx, wi, state, sel, causal, lf, reset, acol, m_prev) = k.work(
        k.X0, 32768, k_st=[P, 4, CH], v_st=[P, 4, CH], vaug=[P, 4, DH + 1], pr=[P, 4, CH], qs=[P, 4, CH],
        kw=[P, 4, DH], dx=[P, 4, CH], wi=[P, 4, CH], state=[P, 4, DH + 1], sel=[4, 4, P], causal=[P, CH],
        lf=[4, T], reset=[4, T], acol=[P, NCH, 4], mprev=[P, 4, NCH])
    (tab_in, rows_f, chain, gates_done, cols_mm, cols_done, zeroed) = k.sems(
        "a_rows", "tables_in", "row_act", "chain", "gates", "cols_mm", "cols", "zeroed")
    (v_staged, vaug_ready, d_ready, wi_ready, o_stored, k_staged, x_ready, qs_ready, p_ready, kw_ready,
     st_done, g_done, tv_done, s_done, tk_done, num_done, st_mm) = k.sems(
        "a", "v_staged", "vaug", "d_ready", "wi_ready", "o_stored", "k_staged", "x_ready", "qs_ready", "p_ready",
        "kw_ready", "state_done", "g_rows", "v_turned", "scores", "k_turned", "numerator", "state_mm")
    den, em = k.small[:, 1, :], k.small[:, 2, :]
    i_row, F_row, m_row, G_row = rows[:, 0, :], rows[:, 1, :], rows[:, 2, :], rows[:, 3, :]
    bG, bS, bV, bK = 0, 1, 2, 3
    num = k.psum[:, 4:6, :].rearrange("p a (b n) -> p (a b) n", b=2)
    st = k.psum[:, 6:8, :].rearrange("p a (b n) -> p (a b) n", b=2)

    def heads(b):
        return k.psum[:, b, :].rearrange("p (h n) -> p h n", h=4)

    with nc.Block() as block:
        @block.sync
        def _(sp):
            a, n = TAB["sel"]
            sp.dma_start(sel[:, :, :].rearrange("p a n -> p (a n)"), k.tables[0:4, a:a + n]).then_inc(tab_in, 16)
            a, n = TAB["causal"]
            sp.dma_start(causal[:, :], k.tables[:, a:a + n]).then_inc(tab_in, 16)
            sp.wait_ge(tab_in, 32)

        @block.gpsimd
        def _(pool):
            k.clear_before(pool)
            pool.memset(state[:, :, :], 0.0).then_inc(zeroed, 1)
            pool.memset(vaug[:, :, DH:DH + 1], 1.0).then_inc(zeroed, 1)

        @block.scalar
        def _(act):
            act.wait_ge(chain, 1)
            nc.scalar.activation(lf[:, :], F_row, ACT.Abs).then_inc(rows_f, 1)
            act.wait_ge(rows_f, 1)
            nc.scalar.activation(lf[:, :], lf[:, :], ACT.Exp, scale=-1.0).then_inc(rows_f, 1)
            act.wait_ge(rows_f, 2)
            nc.scalar.activation(lf[:, :], lf[:, :], ACT.Ln, bias=1.0).then_inc(rows_f, 1)
            act.wait_ge(cols_mm, 1)
            nc.scalar.activation(em, k.psum[:, 1, 0:32], ACT.Exp, scale=-1.0)
            nc.scalar.activation(m_prev[:, :, 1:NCH], k.psum[:, 2, 0:32].rearrange("p (h c) -> p h c", h=4)[:, :, 0:NCH - 1],
                                 ACT.Copy).then_inc(cols_done, 1)
            with act.Fori(0, NCH) as c:
                act.wait_ge(tv_done, c)
                nc.scalar.activation(v_st[:, :, :], chunk(v, c), ACT.Copy).then_inc(v_staged, 1)
                act.wait_ge(tv_done, c + 1)
                act.wait_ge(st_mm, c)
                nc.scalar.activation(vaug[:, :, 0:DH], heads(bV), ACT.Copy).then_inc(vaug_ready, 1)
                act.wait_ge(x_ready, c + 1)
                act.wait_ge(kw_ready, c)
                nc.scalar.activation(dx[:, :, :], dx[:, :, :], ACT.Exp).then_inc(d_ready, 1)
                act.wait_ge(st_done, c)
                act.wait_ge(g_done, c + 1)
                for h in range(4):
                    ins = nc.scalar.activation(wi[:, h, :], heads(bG)[:, h, :], ACT.Exp, bias=m_prev[:, h, bass.ds(c, 1)])
                ins.then_inc(wi_ready, 1)
                act.wait_ge(num_done, c + 1)
                nc.scalar.activation(den[:, bass.ds(c * 4, 4)], num[:, :, DH:DH + 1].rearrange("p h a -> p (h a)"), ACT.Copy)
                nc.scalar.activation(chunk(v, c), num[:, :, 0:DH], ACT.Copy).then_inc(o_stored, 1)

        @block.vector
        def _(dve):
            step = [0]

            def link(ins):
                ins.then_inc(chain, 1)
                step[0] += 1
                dve.wait_ge(chain, step[0])
            fb = COL["f_bias"]
            link(nc.vector.tensor_scalar(F_row, F_row, k.par[0:4, fb:fb + 1], None, ALU.add))
            nc.vector.memset(reset[:, :], 1.0)
            link(nc.vector.memset(m_prev[:, :, :], 0.0))
            link(nc.vector.memset(reset[:, 0:T:CH], 0.0))
            dve.wait_ge(rows_f, 3)
            link(nc.vector.scalar_tensor_tensor(lf[:, :], F_row, 0.0, lf[:, :], ALU.min, ALU.subtract))
            link(nc.vector.tensor_tensor_scan(m_row, lf[:, :], i_row, 0.0, ALU.add, ALU.max))
            link(nc.vector.tensor_tensor_scan(F_row, reset[:, :], lf[:, :], 0.0, ALU.mult, ALU.add))
            link(nc.vector.tensor_tensor(i_row, i_row, F_row, ALU.subtract))
            nc.vector.tensor_tensor(G_row, F_row, m_row, ALU.subtract).then_inc(gates_done, 1)
            dve.wait_ge(cols_mm, 1)
            nc.vector.tensor_copy(acol[:, :, :], k.psum[:, 0, 0:32].rearrange("p (c h) -> p c h", h=4)).then_inc(cols_done, 1)
            dve.wait_ge(cols_done, 2)
            dve.wait_ge(zeroed, 2)
            dve.wait_ge(tab_in, 32)
            with dve.Fori(0, NCH) as c:
                dve.wait_ge(s_done, c)
                dve.wait_ge(tk_done, c)
                nc.vector.tensor_copy(k_st[:, :, :], chunk(kk, c)).then_inc(k_staged, 1)
                dve.wait_ge(g_done, c + 1)
                for h in range(4):
                    ins = nc.vector.scalar_tensor_tensor(dx[:, h, :], heads(bG)[:, h, :], acol[:, bass.ds(c, 1), h:h + 1].rearrange("p a n -> p (a n)"),
                                                         causal[:, :], ALU.add, ALU.add)
                ins.then_inc(x_ready, 1)
                dve.wait_ge(wi_ready, c + 1)
                dve.wait_ge(num_done, c)
                nc.vector.scalar_tensor_tensor(qs[:, :, :], chunk(q, c), SCALE_A, wi[:, :, :], ALU.mult, ALU.mult).then_inc(qs_ready, 1)
                dve.wait_ge(d_ready, c + 1)
                dve.wait_ge(s_done, c + 1)
                nc.vector.scalar_tensor_tensor(pr[:, :, :], heads(bS), SCALE_A, dx[:, :, :], ALU.mult, ALU.mult).then_inc(p_ready, 1)
                dve.wait_ge(tk_done, c + 1)
                dve.wait_ge(st_mm, c)
                nc.vector.tensor_tensor(kw[:, :, :], heads(bK), dx[:, :, CH - 1:CH].to_broadcast([P, 4, DH]), ALU.mult).then_inc(kw_ready, 1)
                dve.wait_ge(num_done, c + 1)
                dve.wait_ge(st_mm, c + 1)
                for h in range(4):
                    ins = nc.vector.scalar_tensor_tensor(state[:, h, :], state[:, h, :], wi[:, h, CH - 1:CH], st[:, h, 0:DH + 1],
                                                         ALU.mult, ALU.add)
                ins.then_inc(st_done, 1)

        @block.tensor
        def _(pe):
            pe.wait_ge(gates_done, 1)
            pe.wait_ge(tab_in, 32)
            for c in range(NCH):
                nc.tensor.matmul(k.psum[:, 0, 4 * c:4 * c + 4], i_row[:, c * CH:(c + 1) * CH], k.ident[0:4, 0:4], start=True, stop=True)
                nc.tensor.matmul(k.psum[:, 1, 4 * c:4 * c + 4], m_row[:, c * CH:(c + 1) * CH], k.ident[0:4, 0:4], start=True, stop=True)
            for h in range(4):
                mm = nc.tensor.matmul(k.psum[:, 2, NCH * h:NCH * (h + 1)], sel[:, h, :], m_row[:, CH - 1:T:CH], start=True, stop=True)
            mm.then_inc(cols_mm, 1)
            pe.wait_ge(cols_done, 2)
            pe.wait_ge(zeroed, 2)
            with pe.Fori(0, NCH) as c:
                pe.wait_ge(x_ready, c)
                pe.wait_ge(wi_ready, c)
                for h in range(4):
                    mm = nc.tensor.matmul(heads(bG)[:, h, :], sel[:, h, :], G_row[:, bass.ds(c * CH, CH)], start=True, stop=True)
                mm.then_inc(g_done, 1)
                pe.wait_ge(v_staged, c + 1)
                pe.wait_ge(vaug_ready, c)
                for h in range(4):
                    mm = nc.tensor.transpose(heads(bV)[:, h, :], v_st[:, h, :], k.ident[:, :])
                mm.then_inc(tv_done, 1)
                pe.wait_ge(k_staged, c + 1)
                pe.wait_ge(p_ready, c)
                for h in range(4):
                    mm = nc.tensor.matmul(heads(bS)[:, h, :], k_st[:, h, :], q[:, h, bass.ds(c * CH, CH)], start=True, stop=True)
                mm.then_inc(s_done, 1)
                pe.wait_ge(kw_ready, c)
                for h in range(4):
                    mm = nc.tensor.transpose(heads(bK)[:, h, :], k_st[:, h, :], k.ident[:, :])
                mm.then_inc(tk_done, 1)
                pe.wait_ge(vaug_ready, c + 1)
                pe.wait_ge(qs_ready, c + 1)
                pe.wait_ge(p_ready, c + 1)
                pe.wait_ge(st_done, c)
                pe.wait_ge(o_stored, c)
                for h in range(4):
                    nc.tensor.matmul(num[:, h, 0:DH + 1], pr[:, h, :], vaug[:, h, :], start=True, stop=False)
                    mm = nc.tensor.matmul(num[:, h, 0:DH + 1], qs[:, h, :], state[:, h, :], start=False, stop=True)
                mm.then_inc(num_done, 1)
                pe.wait_ge(kw_ready, c + 1)
                for h in range(4):
                    mm = nc.tensor.matmul(st[:, h, 0:DH + 1], kw[:, h, :], vaug[:, h, :], start=True, stop=True)
                mm.then_inc(st_mm, 1)


def finish_heads(k, name, gate_tile, mlstm=False, plain=None):
    nc = k.nc
    o = k.m[:, TV:TV + 4, :] if plain is None else k.m[:, plain:plain + 4, :]
    y = k.m[:, gate_tile:gate_tile + 4, :]
    sq, = k.work(k.X0, 8192, sq=[P, 2, NCH, DH])
    sq_ready, reduced, fac_ready, scaled, turned, stored, chain, ln = k.sems(
        name, "sq", "reduced", "factor", "scaled", "turned", "stored", "chain", "ln")
    ss, fac, r = k.small[:, 3, :], k.small[:, 4, :], k.small[:, 5, :]
    den, em = k.small[:, 1, :], k.small[:, 2, :]

    with nc.Block() as block:
        @block.gpsimd
        def _(pool):
            k.clear_before(pool)

        @block.scalar
        def _(act):
            if plain is None:
                for h in range(4):
                    if h >= 2:
                        act.wait_ge(reduced, h - 1)
                    nc.scalar.activation(sq[:, h % 2], o[:, h, :].rearrange("p (c n) -> p c n", c=NCH), ACT.Square).then_inc(sq_ready, 1)
                act.wait_ge(chain, 5 if mlstm else 1)
                nc.scalar.activation(fac, ss, ACT.Ln, bias=k.col("eps"), scale=1.0 / DH).then_inc(ln, 1)
                act.wait_ge(ln, 1)
                nc.scalar.activation(fac, fac, ACT.Exp, scale=-0.5).then_inc(fac_ready, 1)
            else:
                for n in range(0, 8, 2):
                    act.wait_ge(turned, n + 1)
                    h, g = n // 2, n % 2
                    nc.scalar.activation(y[:, h, g * HALF:(g + 1) * HALF], k.bank(n % 4), ACT.Copy).then_inc(stored, 1)

        @block.vector
        def _(dve):
            if plain is None:
                step = [0]

                def link(ins):
                    ins.then_inc(chain, 1)
                    step[0] += 1
                    dve.wait_ge(chain, step[0])
                for h in range(4):
                    dve.wait_ge(sq_ready, h + 1)
                    ins = nc.vector.tensor_reduce(ss[:, h * NCH:(h + 1) * NCH], sq[:, h % 2], axis=AX.X, op=ALU.add)
                    ins.then_inc(reduced, 1)
                dve.wait_ge(reduced, 4)
                if mlstm:
                    link(nc.vector.scalar_tensor_tensor(den, den, -1.0, den, ALU.mult, ALU.max))
                    link(nc.vector.tensor_tensor(r.rearrange("p (h c) -> p c h", h=4), den.rearrange("p (c h) -> p c h", h=4),
                                                 em.rearrange("p (c h) -> p c h", h=4), ALU.max))
                    link(nc.vector.reciprocal(r, r))
                    link(nc.vector.tensor_tensor(ss, ss, r, ALU.mult))
                    link(nc.vector.tensor_tensor(ss, ss, r, ALU.mult))
                else:
                    dve.sem_inc(chain, 1)
                dve.wait_ge(fac_ready, 1)
                if mlstm:
                    link(nc.vector.tensor_tensor(fac, fac, r, ALU.mult))
                for h in range(4):
                    oh = o[:, h, :].rearrange("p (c n) -> p c n", c=NCH)
                    f = fac[:, h * NCH:(h + 1) * NCH].rearrange("p (c n) -> p c n", n=1).to_broadcast([P, NCH, DH])
                    nc.vector.tensor_tensor(oh, oh, f, ALU.mult).then_inc(scaled, 1)
                for n in range(8):
                    dve.wait_ge(turned, n + 1)
                    h, g = n // 2, n % 2
                    yh = y[:, h, g * HALF:(g + 1) * HALF]
                    nc.vector.tensor_tensor(yh, k.bank(n % 4), yh, ALU.mult).then_inc(stored, 1)
            else:
                for n in range(1, 8, 2):
                    dve.wait_ge(turned, n + 1)
                    h, g = n // 2, n % 2
                    nc.vector.tensor_copy(y[:, h, g * HALF:(g + 1) * HALF], k.bank(n % 4)).then_inc(scaled, 1)

        @block.tensor
        def _(pe):
            for n in range(8):
                h, g = n // 2, n % 2
                if plain is None:
                    pe.wait_ge(scaled, h + 1)
                    if n >= 4:
                        pe.wait_ge(stored, n - 3)
                elif n >= 4:
                    pe.wait_ge(scaled if n % 2 else stored, n // 2 - 1)
                for c in range(4):
                    at = (g * 4 + c) * CH
                    mm = nc.tensor.transpose(k.bank(n % 4)[:, c * P:(c + 1) * P], o[:, h, at:at + CH], k.ident[:, :])
                mm.then_inc(turned, 1)


def mix_b(k, f_slot):
    nc = k.nc
    q, kk, v = k.m[:, TQ:TQ + 4, :], k.m[:, TK:TK + 4, :], k.m[:, TV:TV + 4, :]
    NL = len(LEVELS)
    Q, K, B, v_st, v_tok, kw, pr, state, levels, picked, diag = k.work(
        k.H0, 65536, Q=[P, NL + 2, 4, CH], K=[P, NL + 1, 4, CH], B=[P, NL + 1, 2 * CH], v_st=[P, 4, CH], v_tok=[P, 4, DH],
        kw=[P, 4, DH], pr=[P, 4, CH], state=[P, 4, DH], levels=[P, SMALL, 32], picked=[P, SMALL, 4, 32], diag=[P, 4, 32])
    (tab_in, zeroed, v_staged, v_turned, v_ready, base_in, q_lower, q_upper, k_upper, k_lower, blocks, small_mm, big_mm,
     pick, diag_ready, placed, big_stored, k_turned, kw_ready, num_done, o_stored, st_mm, st_done) = k.sems(
        "b", "tables_in", "zeroed", "v_staged", "v_turned", "v_ready", "base_in", "q_lower", "q_upper", "k_upper", "k_lower",
        "blocks", "small_mm", "big_mm", "picked", "diag_ready", "placed", "big_stored", "k_turned", "kw_ready", "num_done",
        "o_stored", "state_mm", "state_done")
    bSm, bBig, bV, bK, bN, bC = 0, 2, 3, 4, 5, 6

    def heads(b):
        return k.psum[:, b, :].rearrange("p (h n) -> p h n", h=4)

    def halves(ap, n, L):
        x = ap[:, n].rearrange("p h t -> p (h t)").rearrange("p (b u l) -> p b u l", u=2, l=L)
        return x[:, :, 0, :], x[:, :, 1, :]

    def decays(c, n, L):
        if n == 0:
            f = chunk(f_slot, c).rearrange("p h (b u) -> p h b u", u=2)
            return f[:, :, :, 0:1], f[:, :, :, 1:2]
        x = B[:, n, 0:4 * CH // L].rearrange("p (b u l) -> p b u l", u=2, l=1)
        return x[:, :, 0, :], x[:, :, 1, :]

    def spread(d, n, L):
        return d if n == 0 else d.to_broadcast([P, 2 * CH // L, L])

    def shaped(x, n):
        return x.rearrange("p (h b) l -> p h b l", h=4) if n == 0 else x

    with nc.Block() as block:
        @block.sync
        def _(sp):
            a, n = TAB["levels"]
            sp.dma_start(levels[:, :, :].rearrange("p a n -> p (a n)"), k.tables[:, a:a + n]).then_inc(tab_in, 16)
            sp.wait_ge(tab_in, 16)

        @block.gpsimd
        def _(pool):
            k.clear_before(pool)
            pool.memset(state[:, :, :], 0.0).then_inc(zeroed, 1)
            pool.memset(pr[:, :, :], 0.0).then_inc(zeroed, 1)
            with pool.Fori(0, NCH) as c:
                for n, L in enumerate(LEVELS):
                    if n == 0:
                        pool.wait_ge(base_in, c + 1)
                        pool.wait_ge(k_turned, c)
                    else:
                        pool.wait_ge(k_lower, c * NL + n)
                        pool.wait_ge(k_upper, c * NL + n)
                        pool.wait_ge(blocks, c * NL + n)
                    lo, _ = halves(K, n, L)
                    to, _ = halves(K, n + 1, L)
                    _, d = decays(c, n, L)
                    pool.tensor_tensor(shaped(to, n), shaped(lo, n), spread(d, n, L), ALU.mult).then_inc(k_lower, 1)

        @block.vector
        def _(dve):
            dve.wait_ge(tab_in, 16)
            dve.wait_ge(zeroed, 2)
            with dve.Fori(0, NCH) as c:
                dve.wait_ge(num_done, c)
                dve.wait_ge(k_lower, c * NL)
                nc.vector.tensor_tensor(Q[:, 1], chunk(q, c), chunk(f_slot, c), ALU.mult).then_inc(q_upper, 1)
                for n, L in enumerate(LEVELS):
                    dve.wait_ge(q_upper, c * (NL + 1) + (n + 1))
                    if n:
                        dve.wait_ge(q_lower, c * NL + n)
                        dve.wait_ge(blocks, c * NL + n)
                    _, up = halves(Q, n + 1, L)
                    _, to = halves(Q, n + 2, L)
                    d, d2 = decays(c, n, L)
                    nc.vector.tensor_tensor(shaped(to, n), shaped(up, n), spread(d, n, L), ALU.mult).then_inc(q_upper, 1)
                    out = B[:, n + 1, 0:2 * CH // L].rearrange("p (b l) -> p b l", l=1)
                    nc.vector.tensor_tensor(shaped(out, n), d, d2, ALU.mult).then_inc(blocks, 1)
                dve.wait_ge(small_mm, c + 1)
                ps = k.psum[:, 0:2, :].rearrange("p a n -> p (a n)")
                for a, b in ((0, 4), (4, SMALL)):
                    ins = nc.vector.tensor_tensor(
                        picked[:, a:b], ps[:, a * 128:b * 128].rearrange("p (l h t) -> p l h t", h=4, t=32),
                        levels[:, a:b].rearrange("p l (h t) -> p l h t", h=1).to_broadcast([P, b - a, 4, 32]), ALU.mult)
                ins.then_inc(pick, 1)
                dve.wait_ge(pick, c + 1)
                dve.wait_ge(placed, c)
                nc.vector.tensor_reduce(diag[:, :, :].rearrange("p h t -> p (h t)"),
                                        picked[:, :, :, :].rearrange("p l h t -> p (h t) l"), axis=AX.X, op=ALU.add).then_inc(diag_ready, 1)
                dve.wait_ge(big_mm, c + 1)
                for j in range(3):
                    ins = nc.vector.tensor_copy(pr[32 * j:32 * j + 32, :, 32 * (j + 1):CH], heads(bBig)[32 * j:32 * j + 32, :, 32 * (j + 1):CH])
                ins.then_inc(big_stored, 1)
                dve.wait_ge(k_turned, c + 1)
                dve.wait_ge(st_mm, c)
                nc.vector.tensor_copy(kw[:, :, :], heads(bK)).then_inc(kw_ready, 1)
                dve.wait_ge(num_done, c + 1)
                nc.vector.tensor_scalar(chunk(v, c), heads(bN), 1.0, None, ALU.mult).then_inc(o_stored, 1)
                for h in range(4):
                    ins = nc.vector.scalar_tensor_tensor(state[:, h, :], state[:, h, :], B[:, NL, h:h + 1], heads(bC)[:, h, :],
                                                         ALU.mult, ALU.add)
                ins.then_inc(st_done, 1)

        @block.scalar
        def _(act):
            with act.Fori(0, NCH) as c:
                act.wait_ge(num_done, c)
                act.wait_ge(k_lower, c * NL)
                nc.scalar.activation(K[:, 0], chunk(kk, c), ACT.Copy)
                nc.scalar.activation(Q[:, 0], chunk(q, c), ACT.Copy).then_inc(base_in, 1)
                act.wait_ge(v_turned, c)
                nc.scalar.activation(v_st[:, :, :], chunk(v, c), ACT.Copy).then_inc(v_staged, 1)
                act.wait_ge(k_turned, c)
                for n, L in enumerate(LEVELS):
                    act.wait_ge(q_upper, c * (NL + 1) + (n + 1))
                    if n:
                        act.wait_ge(q_lower, c * NL + n)
                        act.wait_ge(k_upper, c * NL + n)
                        act.wait_ge(k_lower, c * NL + n)
                    else:
                        act.wait_ge(base_in, c + 1)
                    lo, _ = halves(Q, n + 1, L)
                    to, _ = halves(Q, n + 2, L)
                    nc.scalar.activation(to, lo, ACT.Copy).then_inc(q_lower, 1)
                    _, up = halves(K, n, L)
                    _, to = halves(K, n + 1, L)
                    nc.scalar.activation(to, up, ACT.Copy).then_inc(k_upper, 1)
                    if n == 1:
                        act.wait_ge(v_turned, c + 1)
                        act.wait_ge(st_mm, c)
                        nc.scalar.activation(v_tok[:, :, :], heads(bV), ACT.Copy).then_inc(v_ready, 1)
                act.wait_ge(diag_ready, c + 1)
                act.wait_ge(num_done, c)
                for j in range(4):
                    ins = nc.scalar.activation(pr[32 * j:32 * j + 32, :, 32 * j:32 * j + 32], diag[32 * j:32 * j + 32, :, :], ACT.Copy)
                ins.then_inc(placed, 1)

        @block.tensor
        def _(pe):
            pe.wait_ge(zeroed, 2)
            with pe.Fori(0, NCH) as c:
                pe.wait_ge(v_staged, c + 1)
                pe.wait_ge(v_ready, c)
                for h in range(4):
                    mm = nc.tensor.transpose(heads(bV)[:, h, :], v_st[:, h, :], k.ident[:, :])
                mm.then_inc(v_turned, 1)
                pe.wait_ge(pick, c)
                for n in range(SMALL):
                    qi, ki = n, max(n - 1, 0)
                    if n == 0:
                        pe.wait_ge(base_in, c + 1)
                    else:
                        pe.wait_ge(q_upper, c * (NL + 1) + n)
                    if n >= 2:
                        pe.wait_ge(q_lower, c * NL + (n - 1))
                        pe.wait_ge(k_lower, c * NL + (n - 1))
                        pe.wait_ge(k_upper, c * NL + (n - 1))
                    for h in range(4):
                        for j in range(4):
                            out = k.psum[32 * j:32 * j + 32, n // 4, (n % 4) * 128 + h * 32:(n % 4) * 128 + h * 32 + 32]
                            mm = nc.tensor.matmul(out, K[:, ki, h, 32 * j:32 * j + 32], Q[:, qi, h, 32 * j:32 * j + 32],
                                                  start=True, stop=True)
                mm.then_inc(small_mm, 1)
                pe.wait_ge(big_stored, c)
                pe.wait_ge(q_lower, c * NL + 5)
                pe.wait_ge(q_upper, c * (NL + 1) + 6)
                pe.wait_ge(k_lower, c * NL + 5)
                pe.wait_ge(k_upper, c * NL + 5)
                for h in range(4):
                    for s0 in (0, 64):
                        nc.tensor.matmul(heads(bBig)[s0:s0 + 32, h, s0 + 32:s0 + 64], K[:, 5, h, s0:s0 + 32], Q[:, 6, h, s0 + 32:s0 + 64],
                                         start=True, stop=True)
                pe.wait_ge(q_lower, c * NL + 6)
                pe.wait_ge(q_upper, c * (NL + 1) + 7)
                pe.wait_ge(k_lower, c * NL + 6)
                pe.wait_ge(k_upper, c * NL + 6)
                for h in range(4):
                    mm = nc.tensor.matmul(heads(bBig)[0:64, h, 64:128], K[:, 6, h, 0:64], Q[:, 7, h, 64:128], start=True, stop=True)
                mm.then_inc(big_mm, 1)
                pe.wait_ge(kw_ready, c)
                pe.wait_ge(k_lower, c * NL + 7)
                pe.wait_ge(k_upper, c * NL + 7)
                for h in range(4):
                    mm = nc.tensor.transpose(heads(bK)[:, h, :], K[:, NL, h, :], k.ident[:, :])
                mm.then_inc(k_turned, 1)
                pe.wait_ge(v_ready, c + 1)
                pe.wait_ge(kw_ready, c + 1)
                pe.wait_ge(st_done, c)
                for h in range(4):
                    mm = nc.tensor.matmul(heads(bC)[:, h, :], kw[:, h, :], v_tok[:, h, :], start=True, stop=True)
                mm.then_inc(st_mm, 1)
                pe.wait_ge(q_upper, c * (NL + 1) + 8)
                pe.wait_ge(q_lower, c * NL + 7)
                pe.wait_ge(placed, c + 1)
                pe.wait_ge(big_stored, c + 1)
                pe.wait_ge(o_stored, c)
                for h in range(4):
                    nc.tensor.matmul(heads(bN)[:, h, :], pr[:, h, :], v_tok[:, h, :], start=True, stop=False)
                    mm = nc.tensor.matmul(heads(bN)[:, h, :], Q[:, NL + 1, h, :], state[:, h, :], start=False, stop=True)
                mm.then_inc(num_done, 1)


def rotate(k):
    nc = k.nc
    cos, sin, swap, a, b = k.work(k.X0, 32768, cos=[P, T], sin=[P, T], swap=[P, P], a=[P, 2, T], b=[P, 2, T])
    tab_in, swapped, with_cos, with_sin, done = k.sems("rotary", "tables_in", "swapped", "with_cos", "with_sin", "done")
    n_tiles = 2 * HEADS

    with nc.Block() as block:
        @block.sync
        def _(sp):
            for buf, name in ((swap, "swap"), (cos, "cos"), (sin, "sin")):
                at, n = TAB[name]
                sp.dma_start(buf[:, :], k.tables[:, at:at + n]).then_inc(tab_in, 16)
            sp.wait_ge(tab_in, 48)

        @block.tensor
        def _(pe):
            pe.wait_ge(tab_in, 48)

            def one(j, slot, turn):
                pe.wait_ge(with_sin, j + 1)
                for half in range(2):
                    mm = nc.tensor.matmul(k.bank(2 * slot + half), swap[:, :], k.m[:, bass.ds(j, 1), half * HALF:(half + 1) * HALF].rearrange("p a n -> p (a n)"),
                                          start=True, stop=True)
                mm.then_inc(swapped, 1)
            in_pairs(pe, 0, n_tiles, one)

        @block.gpsimd
        def _(pool):
            k.clear_before(pool)
            pool.wait_ge(tab_in, 48)
            pool.sem_inc(done, 2)

            def one(j, slot, turn):
                pool.wait_ge(done, j + 1)
                pool.tensor_tensor(a[:, slot, :], flat(k.m[:, bass.ds(j, 1), :]), cos[:, :], ALU.mult).then_inc(with_cos, 1)
            in_pairs(pool, 0, n_tiles, one)

        @block.vector
        def _(dve):
            dve.wait_ge(tab_in, 48)
            dve.sem_inc(with_sin, 2)

            def one(j, slot, turn):
                dve.wait_ge(swapped, j + 1)
                nc.vector.tensor_tensor(b[:, slot, :], k.pair(slot), sin[:, :], ALU.mult).then_inc(with_sin, 1)
                dve.wait_ge(with_sin, j + 3)
                dve.wait_ge(with_cos, j + 1)
                nc.vector.tensor_tensor(flat(k.m[:, bass.ds(j, 1), :]), a[:, slot, :], b[:, slot, :], ALU.add).then_inc(done, 1)
            in_pairs(dve, 0, n_tiles, one)


def mix_c(k):
    nc = k.nc
    q, kk, v = k.m[:, TQ:TQ + 4, :], k.m[:, TK:TK + 4, :], k.m[:, TV:TV + 4, :]
    (k_st, v_st, v_tok, pr, qs, kw, state, decay, gq, gk, gc) = k.work(
        k.X0, 32768, k_st=[P, 4, CH], v_st=[P, 4, CH], v_tok=[P, 4, DH], pr=[P, 4, CH], qs=[P, 4, CH],
        kw=[P, 4, DH], state=[P, 4, DH], decay=[P, 4, CH], gq=[P, 4, CH], gk=[P, 4, 1], gc=[P, 4, 1])
    (tab_in, zeroed, v_staged, v_ready, o_stored, k_staged, qs_ready, p_ready, kw_ready, decayed, st_done, tv_done, s_done,
     tk_done, num_done, st_mm) = k.sems(
        "c", "tables_in", "zeroed", "v_staged", "v_ready", "o_stored", "k_staged", "qs_ready", "p_ready", "kw_ready",
        "decayed", "state_done", "v_turned", "scores", "k_turned", "numerator", "state_mm")
    bS, bV, bK, bN, bC = 0, 1, 2, 3, 4

    def heads(b):
        return k.psum[:, b, :].rearrange("p (h n) -> p h n", h=4)

    with nc.Block() as block:
        @block.sync
        def _(sp):
            for buf, name in ((decay, "decay"), (gq, "gq"), (gk, "gk"), (gc, "gc")):
                at, n = TAB[name]
                sp.dma_start(buf[:, :, :].rearrange("p a n -> p (a n)"), k.tables[:, at:at + n]).then_inc(tab_in, 16)
            sp.wait_ge(tab_in, 64)

        @block.gpsimd
        def _(pool):
            k.clear_before(pool)
            pool.memset(state[:, :, :], 0.0).then_inc(zeroed, 1)
            pool.wait_ge(tab_in, 64)
            with pool.Fori(0, NCH) as c:
                pool.wait_ge(num_done, c)
                pool.tensor_tensor(qs[:, :, :], chunk(q, c), gq[:, :, :], ALU.mult).then_inc(qs_ready, 1)

        @block.scalar
        def _(act):
            with act.Fori(0, NCH) as c:
                act.wait_ge(tv_done, c)
                nc.scalar.activation(v_st[:, :, :], chunk(v, c), ACT.Copy).then_inc(v_staged, 1)
                act.wait_ge(tv_done, c + 1)
                act.wait_ge(num_done, c)
                act.wait_ge(st_mm, c)
                nc.scalar.activation(v_tok[:, :, :], heads(bV), ACT.Copy).then_inc(v_ready, 1)

        @block.vector
        def _(dve):
            dve.wait_ge(zeroed, 1)
            dve.wait_ge(tab_in, 64)
            with dve.Fori(0, NCH) as c:
                dve.wait_ge(s_done, c)
                dve.wait_ge(tk_done, c)
                nc.vector.tensor_copy(k_st[:, :, :], chunk(kk, c)).then_inc(k_staged, 1)
                dve.wait_ge(s_done, c + 1)
                dve.wait_ge(num_done, c)
                nc.vector.tensor_tensor(pr[:, :, :], heads(bS), decay[:, :, :], ALU.mult).then_inc(p_ready, 1)
                dve.wait_ge(tk_done, c + 1)
                dve.wait_ge(st_mm, c)
                nc.vector.tensor_tensor(kw[:, :, :], heads(bK), gk[:, :, :].to_broadcast([P, 4, DH]), ALU.mult).then_inc(kw_ready, 1)
                dve.wait_ge(num_done, c + 1)
                nc.vector.tensor_scalar(chunk(v, c), heads(bN), 1.0, None, ALU.mult).then_inc(o_stored, 1)
                nc.vector.tensor_tensor(state[:, :, :], state[:, :, :], gc[:, :, :].to_broadcast([P, 4, DH]), ALU.mult).then_inc(decayed, 1)
                dve.wait_ge(decayed, c + 1)
                dve.wait_ge(st_mm, c + 1)
                nc.vector.tensor_tensor(state[:, :, :], heads(bC), state[:, :, :], ALU.add).then_inc(st_done, 1)

        @block.tensor
        def _(pe):
            pe.wait_ge(zeroed, 1)
            with pe.Fori(0, NCH) as c:
                pe.wait_ge(v_staged, c + 1)
                pe.wait_ge(v_ready, c)
                for h in range(4):
                    mm = nc.tensor.transpose(heads(bV)[:, h, :], v_st[:, h, :], k.ident[:, :])
                mm.then_inc(tv_done, 1)
                pe.wait_ge(k_staged, c + 1)
                pe.wait_ge(p_ready, c)
                for h in range(4):
                    mm = nc.tensor.matmul(heads(bS)[:, h, :], k_st[:, h, :], q[:, h, bass.ds(c * CH, CH)], start=True, stop=True)
                mm.then_inc(s_done, 1)
                pe.wait_ge(kw_ready, c)
                for h in range(4):
                    mm = nc.tensor.transpose(heads(bK)[:, h, :], k_st[:, h, :], k.ident[:, :])
                mm.then_inc(tk_done, 1)
                pe.wait_ge(v_ready, c + 1)
                pe.wait_ge(qs_ready, c + 1)
                pe.wait_ge(p_ready, c + 1)
                pe.wait_ge(st_done, c)
                pe.wait_ge(o_stored, c)
                for h in range(4):
                    nc.tensor.matmul(heads(bN)[:, h, :], pr[:, h, :], v_tok[:, h, :], start=True, stop=False)
                    mm = nc.tensor.matmul(heads(bN)[:, h, :], qs[:, h, :], state[:, h, :], start=False, stop=True)
                mm.then_inc(num_done, 1)
                pe.wait_ge(kw_ready, c + 1)
                for h in range(4):
                    mm = nc.tensor.matmul(heads(bC)[:, h, :], kw[:, h, :], v_tok[:, h, :], start=True, stop=True)
                mm.then_inc(st_mm, 1)


def mix_d(k):
    nc = k.nc
    v = k.m[:, TV:TV + 4, :]
    o = k.m[:, TGA:TGA + 4, :]
    q_st, k_st, u, beta, prod, strict, loose = k.work(
        k.X0, 32768, q_st=[P, T], k_st=[P, T], u=[P, 2, T], beta=[P, 2, T], prod=[P, T + 8], strict=[P, P], loose=[P, P])
    (tab_in, v_turned, v_back, staged, z_done, sig_done, cleared, masked, ready, scanned, a_done, a_turned, at_stored, av_done, o_stored) = k.sems(
        "d", "tables_in", "v_turned", "v_back", "staged", "z", "sigmoids", "cleared", "masked", "ready", "scanned", "weights",
        "weights_turned", "weights_back", "av", "o_stored")
    NB = T // P
    PER = 2 * NB

    def z_pair(par):
        return k.pair(par)

    with nc.Block() as block:
        @block.sync
        def _(sp):
            for buf, name in ((strict, "strict"), (loose, "loose")):
                at, n = TAB[name]
                sp.dma_start(buf[:, :], k.tables[:, at:at + n]).then_inc(tab_in, 16)
            sp.wait_ge(tab_in, 32)

        def free(act, hp, n):
            if n >= 2:
                act.wait_ge(av_done, hp * PER + (n - 1))

        def store(act, hp, n):
            tb, hh = n % NB, n // NB
            act.wait_ge(av_done, hp * PER + (n + 1))
            nc.scalar.activation(flat(o[:, bass.ds(hp, 1), tb * P + hh * DH_D:tb * P + (hh + 1) * DH_D]),
                                 k.psum[:, 6 + 0, 0:DH_D], ACT.Copy).then_inc(o_stored, 1)

        @block.scalar
        def _(act):
            for n in range(8):
                act.wait_ge(v_turned, n + 1)
                ft, g = n // 2, n % 2
                nc.scalar.activation(v[:, ft, g * HALF:(g + 1) * HALF], k.bank(n % 4), ACT.Copy).then_inc(v_back, 1)
            with act.Fori(0, HEADS) as hp:
                act.wait_ge(z_done, hp * PER)
                nc.scalar.activation(q_st[:, :], flat(k.m[:, bass.ds(hp + TQ, 1), :]), ACT.Copy).then_inc(staged, 1)
                for n in range(PER):
                    tb, w, par = n % NB, P * (n % NB + 1), n % 2
                    hh = n // NB
                    act.wait_ge(z_done, hp * PER + (n + 1))
                    free(act, hp, n)
                    nc.scalar.activation(u[:, par, 0:w], z_pair(par)[:, 0:w], ACT.Sigmoid, scale=-SCALE_D)
                    nc.scalar.activation(beta[:, par, 0:w], z_pair(par)[:, 0:w], ACT.Sigmoid, scale=SCALE_D).then_inc(sig_done, 1)
                    if n:
                        store(act, hp, n - 1)
                store(act, hp, PER - 1)

        @block.gpsimd
        def _(pool):
            k.clear_before(pool)
            pool.wait_ge(tab_in, 32)
            with pool.Fori(0, HEADS) as hp:
                for n in range(PER):
                    par = n % 2
                    pool.wait_ge(sig_done, hp * PER + (n + 1))
                    pool.tensor_tensor(u[:, par, 0:P], u[:, par, 0:P], strict[:, :], ALU.mult).then_inc(cleared, 1)
                    pool.wait_ge(cleared, hp * PER + (n + 1))
                    pool.tensor_tensor(u[:, par, 0:P], u[:, par, 0:P], loose[:, :], ALU.add)
                    pool.tensor_tensor(beta[:, par, 0:P], beta[:, par, 0:P], strict[:, :], ALU.mult).then_inc(masked, 1)

        @block.vector
        def _(dve):
            nc.vector.memset(prod[:, 0:1], 1.0).then_inc(ready, 1)
            dve.wait_ge(ready, 1)
            with dve.Fori(0, HEADS) as hp:
                dve.wait_ge(z_done, hp * PER)
                nc.vector.tensor_copy(k_st[:, ::-1], flat(k.m[:, bass.ds(hp + TK, 1), :])).then_inc(staged, 1)
                for n in range(PER):
                    w, par = P * (n % NB + 1), n % 2
                    dve.wait_ge(masked, hp * PER + (n + 1))
                    nc.vector.tensor_tensor_scan(prod[:, 1:w + 1], u[:, par, 0:w], u[:, par, 0:w], 1.0, ALU.mult, ALU.bypass).then_inc(scanned, 1)
                    dve.wait_ge(scanned, hp * PER + (n + 1))
                    nc.vector.tensor_tensor(u[:, par, 0:w][:, ::-1], beta[:, par, 0:w], prod[:, 0:w], ALU.mult).then_inc(a_done, 1)
                    dve.wait_ge(a_turned, hp * PER + (n + 1))
                    nc.vector.tensor_copy(beta[:, par, 0:w], k.pair(2)[:, 0:w]).then_inc(at_stored, 1)

        @block.tensor
        def _(pe):
            for n in range(8):
                ft, g = n // 2, n % 2
                if n >= 4:
                    pe.wait_ge(v_back, n - 3)
                for c in range(4):
                    at = g * HALF + c * P
                    mm = nc.tensor.transpose(k.bank(n % 4)[:, c * P:(c + 1) * P], v[:, ft, at:at + P], k.ident[:, :])
                mm.then_inc(v_turned, 1)
            pe.wait_ge(v_back, 8)

            def scores(hp, n):
                tb, hh, par = n % NB, n // NB, n % 2
                w = P * (tb + 1)
                rows = slice(DH_D * hh, DH_D * (hh + 1))
                if n >= 2:
                    pe.wait_ge(sig_done, hp * PER + (n - 1))
                for a in range(0, w, HALF):
                    b = min(w, a + HALF)
                    mm = nc.tensor.matmul(z_pair(par)[:, a:b], q_st[rows, tb * P:(tb + 1) * P], k_st[rows, T - w + a:T - w + b],
                                          start=True, stop=True)
                mm.then_inc(z_done, 1)

            with pe.Fori(0, HEADS) as hp:
                pe.wait_ge(staged, hp * 2 + 2)
                pe.wait_ge(sig_done, hp * PER)
                scores(hp, 0)
                for n in range(PER):
                    tb, hh, par = n % NB, n // NB, n % 2
                    if n + 1 < PER:
                        scores(hp, n + 1)
                    pe.wait_ge(a_done, hp * PER + (n + 1))
                    pe.wait_ge(at_stored, hp * PER + n)
                    for c in range(tb + 1):
                        mm = nc.tensor.transpose(k.pair(2)[:, c * P:(c + 1) * P], u[:, par, c * P:(c + 1) * P], k.ident[:, :])
                    mm.then_inc(a_turned, 1)
                    pe.wait_ge(at_stored, hp * PER + (n + 1))
                    pe.wait_ge(o_stored, hp * PER + n)
                    for c in range(tb + 1):
                        at = c * P
                        mm = nc.tensor.matmul(k.psum[:, 6, 0:DH_D], beta[:, par, c * P:(c + 1) * P],
                                              v[:, bass.ds(hp, 1), at + hh * DH_D:at + (hh + 1) * DH_D].rearrange("p a n -> p (a n)"),
                                              start=(c == 0), stop=(c == tb))
                    mm.then_inc(av_done, 1)


def hybrid_trunk(nc, xT, params, tables, w_ada, w_units, outT, stop=None, dump=None):
    with ExitStack() as ctx:
        k = Trunk(nc, ctx, xT, params, tables, w_ada, w_units, outT)
        steps = [
            ("start", lambda: start(k)),
            ("norm0", lambda: norm(k, "norm0", k.modA[:, 0, :], k.mod[:, 0, 0:8], spill=True)),
            ("projA", lambda: project(k, "projA", N_PROJ_A, [
                ("conv", TQ, ("b_even", 0), None, 8),
                ("rows", None, None, None, 1),
                ("gate_sigmoid", TGA, ("b_even", 8), "mlstm_norm", 4),
                ("copy", TV, ("b_even", 12), None, 4)],
                gate_rows=(k.m[0:4, TGB, :], k.m[0:4, TGB + 1, :]))),
            ("mixA", lambda: mix_a(k)),
            ("finA", lambda: finish_heads(k, "finA", TGA, mlstm=True)),
            ("projB", lambda: project(k, "projB", N_PROJ_B, [
                ("silu", TQ, ("b_even", 16), None, 4),
                ("forget", TK, ("b_even", 20), None, 4),
                ("gate_silu", TGB, ("b_even", 28), "hgrn_norm", 4),
                ("copy", TV, ("b_even", 24), None, 4)], f_tile=k.x[:, 0:4, :])),
            ("mixB", lambda: mix_b(k, k.x[:, 0:4, :])),
            ("finB", lambda: finish_heads(k, "finB", TGB)),
            ("out0", lambda: out_project(k, "out0", 0)),
            ("normf0", lambda: norm(k, "normf0", k.modA[:, 1, :], k.mod[:, 0, 24:32], spill=False)),
            ("ffn0", lambda: ffn(k, "ffn0", 0)),
            ("norm1", lambda: norm(k, "norm1", k.modA[:, 2, :], k.mod[:, 1, 0:8], spill=True)),
            ("projD", lambda: project(k, "projD", N_PROJ_D, [
                ("copy", TQ, ("b_odd", 16), None, 4),
                ("copy", TK, ("b_odd", 20), None, 4),
                ("copy", TV, ("b_odd", 24), None, 4)])),
            ("mixD", lambda: mix_d(k)),
            ("finD", lambda: finish_heads(k, "finD", TGB, plain=TGA)),
            ("projC", lambda: project(k, "projC", N_PROJ_C, [
                ("copy", TQ, ("b_odd", 0), None, 8),
                ("gate_silu", TGA, ("b_odd", 12), "ret_norm", 4),
                ("copy", TV, ("b_odd", 8), None, 4)])),
            ("rotary", lambda: rotate(k)),
            ("mixC", lambda: mix_c(k)),
            ("finC", lambda: finish_heads(k, "finC", TGA)),
            ("out1", lambda: out_project(k, "out1", 1)),
            ("normf1", lambda: norm(k, "normf1", k.modA[:, 3, :], k.mod[:, 1, 24:32], spill=False)),
            ("ffn1", lambda: ffn(k, "ffn1", 1)),
            ("final", lambda: norm(k, "final", k.par[:, COL["norm_final"]:COL["norm_final"] + 8], None, spill=False, out=True)),
        ]
        for name, step in steps:
            k.phase(step)
            if name == stop:
                k.phase(lambda: dump(k))
                break
        k.held.close()


def make_tables():
    t = np.zeros((P, N_TAB), np.float64)

    def put(name, a):
        at, n = TAB[name]
        t[0:a.shape[0], at:at + n] = a.reshape(a.shape[0], n)
    i = np.arange(P)
    put("ident", np.eye(P))
    put("ones", np.ones((P, P)))
    put("causal", np.where(i[:, None] <= i[None, :], 0.0, -1e30))
    lv = np.zeros((P, SMALL, 32))
    s, u = (i % 32)[:, None], np.arange(32)[None, :]
    lv[:, 0] = s == u
    for n in range(1, SMALL):
        L = 2 ** (n - 1)
        lv[:, n] = (s // (2 * L) == u // (2 * L)) & (s % (2 * L) < L) & (u % (2 * L) >= L)
    put("levels", lv)
    put("sel", np.repeat(np.eye(4)[:, :, None], P, axis=2))
    strict = (i[:, None] + i[None, :]) > P - 1
    put("strict", strict)
    put("loose", ~strict)
    swap = np.zeros((P, P))
    swap[i[64:], i[64:] - 64] = -1.0
    swap[i[:64], i[:64] + 64] = 1.0
    put("swap", swap)
    gamma = np.log1p(-(2.0 ** (-5.0 - np.arange(HEADS))))
    lag = i[None, :] - i[:, None]
    put("decay", np.where(lag[:, None, :] >= 0, np.exp(np.maximum(lag, 0)[:, None, :] * gamma[None, :, None]), 0.0) * SCALE_A)
    put("gq", np.broadcast_to(np.exp((i + 1)[None, None, :] * gamma[None, :, None]), (P, HEADS, P)) * SCALE_A)
    put("gk", np.exp((P - 1 - i)[:, None] * gamma[None, :]))
    put("gc", np.broadcast_to(np.exp(P * gamma)[None, :], (P, HEADS)))
    inv = (np.float32(10000.0) ** (-np.arange(0, DH, 2, dtype=np.float32) / np.float32(DH))).astype(np.float32)
    ang = (np.arange(T, dtype=np.float32)[None, :] * inv[:, None]).astype(np.float64)
    put("cos", np.tile(np.cos(ang), (2, 1)))
    put("sin", np.tile(np.sin(ang), (2, 1)))
    return t.astype(np.float32)


def lay_out(x, c, w_ada, b_ada, norm_mix, norm_ffn, norm_final, w_in_even, b_in_even, conv_qk_w, conv_qk_b, mlstm_f_bias,
            mlstm_norm, hgrn_lb_logits, hgrn_norm, w_in_odd, b_in_odd, ret_norm, w_out, ffn_up, ffn_conv_w, ffn_conv_b, ffn_down):
    def feature_columns(a):
        a = np.asarray(a)
        return np.moveaxis(a.reshape(-1, P), 0, 1)

    def units(w):
        return w.reshape(KT, P, -1, P).transpose(2, 1, 0, 3).reshape(-1, P, KT * P)

    G = GROUP_W
    be, bo = b_in_even[0], b_in_odd[0]
    even = w_in_even[0]
    qk, va, oa = slice(0, 2 * G), slice(2 * G, 3 * G), slice(3 * G, 4 * G)
    ia, fa = slice(4 * G, 4 * G + 4), slice(4 * G + 4, 4 * G + 8)
    rest = 4 * G + 8
    qb, fb, ib, gb = (slice(rest + i * G, rest + (i + 1) * G) for i in range(4))
    rows = np.zeros((D, P), np.float32)
    rows[:, 0:4] = even[:, ia]
    rows[:, 32:36] = even[:, fa]
    odd = w_in_odd[0]
    qc, kc, vc, gc, qd, kd, vd = (slice(i * G, (i + 1) * G) for i in range(7))

    def ffn_units(layer):
        up = units(ffn_up[layer])
        dn = ffn_down[layer].reshape(GROUPS, 2, P, 2, HALF).transpose(0, 3, 2, 1, 4).reshape(GROUPS, 2, P, 2 * HALF)
        out = []
        for g in range(GROUPS + 1):
            if g < GROUPS:
                out += [up[2 * g], up[FFT + 2 * g], up[2 * g + 1], up[FFT + 2 * g + 1]]
            if g:
                out += [dn[g - 1, 0], dn[g - 1, 1]]
        return np.stack(out)

    w_units = np.concatenate([
        units(even[:, qk]), units(rows), units(even[:, oa]), units(even[:, va]),
        units(even[:, qb]), units(even[:, fb]), units(even[:, gb]), units(even[:, ib]),
        units(w_out[0]), ffn_units(0),
        units(odd[:, qd]), units(odd[:, kd]), units(odd[:, vd]),
        units(odd[:, qc]), units(odd[:, kc]), units(odd[:, gc]), units(odd[:, vc]),
        units(w_out[1]), ffn_units(1)])

    par = np.zeros((P, COL["all"]), np.float32)

    def put(name, a):
        par[0:a.shape[0], COL[name]:COL[name] + a.shape[1]] = a
    put("c", feature_columns(c))
    put("b_ada", feature_columns(b_ada))
    put("norm_mix", feature_columns(norm_mix))
    put("norm_ffn", feature_columns(norm_ffn))
    put("norm_final", feature_columns(norm_final))
    put("b_even", feature_columns(np.concatenate([be[qk], be[oa], be[va], be[qb], be[fb], be[ib], be[gb]])))
    gate = np.zeros((P, 1), np.float32)
    gate[0:4, 0] = be[ia]
    gate[32:36, 0] = be[fa]
    put("b_gate", gate)
    put("f_bias", mlstm_f_bias[0][:, None])
    put("conv_qk_w", feature_columns(conv_qk_w[0]))
    put("conv_qk_b", feature_columns(conv_qk_b))
    put("mlstm_norm", feature_columns(mlstm_norm))
    put("lb_logits", feature_columns(hgrn_lb_logits))
    put("hgrn_norm", feature_columns(hgrn_norm))
    put("b_odd", feature_columns(bo))
    put("ret_norm", feature_columns(ret_norm))
    fw = feature_columns(ffn_conv_w)
    n = 6 * FFT
    put("ffn_w0", fw[:, :n])
    put("ffn_w1", fw[:, n:])
    put("ffn_b", feature_columns(ffn_conv_b))
    put("eps", np.full((P, 1), EPS, np.float32))

    return {
        "xT": np.ascontiguousarray(x[0].T.reshape(KT, P, T).transpose(1, 0, 2).reshape(P, KT * T)),
        "params": par,
        "tables": make_tables(),
        "w_ada": np.ascontiguousarray(w_ada.reshape(KT, P, 12, 4, P).transpose(2, 1, 3, 0, 4)),
        "w_units": np.ascontiguousarray(w_units),
    }


def kernel(**inputs):
    import concourse.bacc as bacc
    from concourse.bass_utils import run_bass_kernel_spmd

    arrays = lay_out(**{n: np.asarray(a) for n, a in inputs.items()})
    nc = bacc.Bacc("TRN2", target_bir_lowering=False, num_devices=1)
    args = [nc.dram_tensor(n, a.shape, mybir.dt.from_np(a.dtype), kind="ExternalInput").ap() for n, a in arrays.items()]
    out = nc.dram_tensor("outT", (P, KT, T), F32, kind="ExternalOutput").ap()
    hybrid_trunk(nc, *args, out)
    got = run_bass_kernel_spmd(nc, [arrays], core_ids=[0]).results[0]["outT"]
    return np.ascontiguousarray(got.transpose(1, 0, 2).reshape(D, T).T).reshape(1, T, D)
```

```python
from contextlib import ExitStack

import numpy as np

import concourse.bass as bass
from concourse import mybir

F32 = mybir.dt.float32
F32R = mybir.dt.float32r
ALU = mybir.AluOpType
ACT = mybir.ActivationFunctionType
AX = mybir.AxisListType

P = 128
D = 1024
T = 1024
KT = D // P
HALF = 512
HEADS = 4
DH = 128
GROUP_W = HEADS * DH
CH = 128
NCH = T // CH
D_FF = 2816
FFT = D_FF // P
GROUPS = FFT // 2
H_D = 8
DH_D = 64
EPS = 1e-6
CONV_A = 4
FFN_CONV = 3
SCALE_A = float(DH) ** -0.5
SCALE_D = float(DH_D) ** -0.5
LEVELS = [1, 2, 4, 8, 16, 32, 64]
SMALL = 6

TQ, TK, TV, TGA, TGB = 0, 4, 8, 12, 16

N_PROJ_A, N_PROJ_B, N_PROJ_D, N_PROJ_C = 17, 16, 12, 16
N_OUT, N_FFN = 8, 66


def columns():
    sizes = [("b_ada", 96), ("norm_mix", 16), ("norm_ffn", 16), ("norm_final", 8),
             ("b_even", 32), ("b_gate", 1), ("f_bias", 1), ("conv_qk_w", 8 * CONV_A), ("conv_qk_b", 8),
             ("mlstm_norm", 4), ("lb_logits", 4), ("hgrn_norm", 4), ("b_odd", 28), ("ret_norm", 4),
             ("ffn_w0", 6 * FFT), ("ffn_w1", 6 * FFT), ("ffn_b", 4 * FFT), ("eps", 1)]
    out, at = {}, 0
    for name, n in sizes:
        out[name] = at
        at += n
    out["all"] = at
    return out


COL = columns()

TAB = {}
_at = 0
for _name, _n in (("ident", 128), ("ones", 128), ("causal", 128), ("levels", SMALL * 32), ("sel", 512),
                  ("barrier", 128), ("swap", 128), ("decay", 512), ("gq", 512), ("gk", 4), ("gc", 4),
                  ("cos", 1024), ("sin", 1024)):
    TAB[_name] = (_at, _n)
    _at += _n
N_TAB = _at


def in_pairs(eng, start, stop, body):
    turns = (stop - start) // 2
    if turns > 0:
        with eng.Fori(0, turns) as i:
            for u in range(2):
                body(i * 2 + (start + u), u, i)
    if (stop - start) % 2:
        body(stop - 1, 0, turns)


def flat(ap):
    return ap.rearrange("p a n -> p (a n)")


class Trunk:
    def __init__(self, nc, ctx, xT, params, tables, w_ada, c_rows, w_units, outT):
        self.nc, self.ctx = nc, ctx
        self.xT, self.params_d, self.tables, self.w_ada, self.c_rows, self.w_units, self.outT = xT, params, tables, w_ada, c_rows, w_units, outT
        self.x_spill = nc.dram_tensor("x_spill", (P, KT * T), F32, kind="Internal").ap()
        self.held, self.mine, self.before = ExitStack(), [], []
        self.unit = 0
        self.top = 16512
        place = self.place
        self.ident = place("ident", [P, 128], F32)
        self.ones = place("ones", [P, 128], F32)
        self.par = place("par", [P, COL["all"]], F32)
        self.mod = place("mod", [P, 2, 48], F32)
        self.modA = place("modA", [P, 4, 8], F32)
        self.lb = place("lb", [P, 3, 4], F32)
        self.small = place("small", [P, 8, 32], F32)
        self.top = 16512 + 7680
        self.w_raw = place("w_raw", [P, 2, 1024], F32)
        self.w_hi = place("w_hi", [P, 2, 1024], F32R)
        self.w_lo = place("w_lo", [P, 2, 1024], F32R)
        self.X0 = self.top
        self.x = place("x", [P, KT, T], F32)
        self.H0 = self.top
        self.hh = place("hh", [P, KT, T], F32R)
        self.hl = place("hl", [P, KT, T], F32R)
        self.M0 = self.top
        self.m = place("m", [P, 20, T], F32)
        self.psum = ctx.enter_context(nc.psum_tensor("ps", [P, 8, HALF], F32))
        self.n_place = 0
        self.acc, self.sq = self.work(self.M0 + 14 * T * 4, 12288, acc=[P, T], sq=[P, 2, T])
        self.rs, self.xr, self.hb = self.work(self.M0 + 15 * T * 4, 20480, rs=[P, T], xr=[P, 2, T], hb=[P, 2, T])

    def place(self, name, shape, dt):
        n = 4
        for s in shape[1:]:
            n *= s
        t = self.nc.alloc_sbuf_tensor_at(name, shape, dt, offset=self.top)
        self.top += (n + 31) // 32 * 32
        assert self.top <= 229368, (name, self.top)
        return t

    def work(self, start, limit, **shapes):
        keep, self.top, out = self.top, start, []
        self.n_place += 1
        for name, shape in shapes.items():
            dt = F32
            if isinstance(shape, tuple):
                shape, dt = shape
            out.append(self.place(f"{name}_{self.n_place}", shape, dt))
        assert self.top <= start + limit, (self.top - start, limit)
        self.top = keep
        return out

    def sems(self, phase, *names):
        new = [self.held.enter_context(self.nc.semaphore(f"{phase}_{n}")) for n in names]
        self.mine += new
        return new

    def phase(self, build):
        self.before, self.mine, last = self.mine, [], self.held
        self.held = ExitStack()
        build()
        last.close()

    def credit(self, eng, *sems):
        for s in sems:
            eng.sem_inc(s, 1)

    def clear_before(self, eng):
        for s in self.before:
            eng.sem_clear(s)

    def col(self, name, i=0):
        if isinstance(i, int):
            return self.par[:, COL[name] + i:COL[name] + i + 1]
        return self.par[:, bass.ds(i + COL[name], 1)]

    def pair(self, q):
        return self.psum[:, 2 * q:2 * q + 2, :].rearrange("p a n -> p (a n)")

    def bank(self, b, n=HALF):
        return self.psum[:, b, 0:n]

    def stream_sems(self, name):
        return self.sems(name, "loaded_even", "loaded_odd", "hi", "split", "unit_done")

    def load_units(self, eng, sems, n, beside=None):
        first = self.unit
        loaded, split = sems[0:2], sems[3]
        last = min(n + 2, TOTAL_UNITS - first)

        def load(j, slot, turn):
            eng.wait_ge(split, j - 1)
            place = (first + slot) % 2
            src = self.w_units[bass.ds(j + first, 1), :, :].rearrange("a p n -> p (a n)")
            eng.dma_start(self.w_raw[:, place, :], src).then_inc(loaded[slot], 16)
            if beside is not None and turn is not None:
                beside(j, slot)
        if beside is None:
            in_pairs(eng, 2, last, load)
        else:
            in_pairs(eng, 2, 10, load)
            in_pairs(eng, 10, last, lambda j, slot, turn: load(j, slot, None))
        count = last - 2
        eng.wait_ge(loaded[0], 16 * ((count + 1) // 2))
        if count > 1:
            eng.wait_ge(loaded[1], 16 * (count // 2))

    def split_units(self, eng, sems, n):
        first = self.unit
        loaded, hi, split, done = sems[0:2], sems[2], sems[3], sems[4]
        raw, w_hi, w_lo = self.w_raw, self.w_hi, self.w_lo
        one = self.ones[:, 0:1].to_broadcast([P, 1024])

        self.credit(eng, split)
        place = (first + 1) % 2
        eng.tensor_tensor(w_hi[:, place, :], raw[:, place, :], one, ALU.mult).then_inc(hi, 1)
        eng.wait_ge(hi, 1)
        eng.tensor_tensor(w_lo[:, place, :], raw[:, place, :], w_hi[:, place, :].bitcast(F32),
                          ALU.subtract).then_inc(split, 1)
        stop = min(n + 1, TOTAL_UNITS - first)

        def rest(j, slot, turn):
            place = (first + slot) % 2
            eng.wait_ge(loaded[slot], (turn + 1) * 16)
            eng.wait_ge(done, j - 1)
            eng.tensor_tensor(w_hi[:, place, :], raw[:, place, :], one, ALU.mult).then_inc(hi, 1)
            eng.wait_ge(hi, j)
            eng.tensor_tensor(w_lo[:, place, :], raw[:, place, :], w_hi[:, place, :].bitcast(F32),
                              ALU.subtract).then_inc(split, 1)
        in_pairs(eng, 2, stop, rest)

    def multiply(self, place, psum_pair, rhs_hi, rhs_lo):
        nc = self.nc
        for k in range(KT):
            w_hi = self.w_hi[:, place, k * P:(k + 1) * P]
            w_lo = self.w_lo[:, place, k * P:(k + 1) * P]
            for n, (w, r) in enumerate(((w_hi, rhs_hi), (w_hi, rhs_lo), (w_lo, rhs_hi))):
                for half in range(2):
                    mm = nc.tensor.matmul(self.bank(2 * psum_pair + half), w,
                                          r[:, k, half * HALF:(half + 1) * HALF],
                                          start=(k == 0 and n == 0), stop=(k == KT - 1 and n == 2))
        return mm


    def multiply_first(self, first, rhs_ready, split, done):
        nc = self.nc
        nc.tensor.wait_ge(split, 2)
        for k in range(KT):
            nc.tensor.wait_ge(rhs_ready, k + 1)
            for u in range(2):
                place = (first + u) % 2
                w_hi = self.w_hi[:, place, k * P:(k + 1) * P]
                w_lo = self.w_lo[:, place, k * P:(k + 1) * P]
                for n, (w, r) in enumerate(((w_hi, self.hh), (w_hi, self.hl), (w_lo, self.hh))):
                    for half in range(2):
                        mm = nc.tensor.matmul(self.bank(2 * u + half), w, r[:, k, half * HALF:(half + 1) * HALF],
                                              start=(k == 0 and n == 0), stop=(k == KT - 1 and n == 2))
                if k == KT - 1:
                    mm.then_inc(done, 1)

    def square_sems(self, name):
        return self.sems(name, "squared", "summed")

    def square(self, act, S, i, x):
        if not isinstance(i, int) or i >= 3:
            act.wait_ge(S[1], i - 1)
        dst = self.acc[:, :] if isinstance(i, int) and i == 0 else self.sq[:, x[1], :]
        self.nc.scalar.activation(dst, x[0], ACT.Square).then_inc(S[0], 1)

    def add_square(self, dve, S, i, slot):
        dve.wait_ge(S[0], i + 1)
        dve.wait_ge(S[1], i)
        self.nc.vector.tensor_tensor(self.acc[:, :], self.acc[:, :], self.sq[:, slot, :], ALU.add).then_inc(S[1], 1)

    def norm_sems(self, name):
        return self.sems(name, "mean", "ln", "rstd", "x_rstd", "h_hi", "h_ready")

    def norm_mean(self, N):
        for half in range(2):
            mm = self.nc.tensor.matmul(self.bank(6 + half), self.ones[:, :], self.acc[:, half * HALF:(half + 1) * HALF],
                                       start=True, stop=True)
        mm.then_inc(N[0], 1)

    def norm_rstd(self, act, N):
        act.wait_ge(N[0], 1)
        self.nc.scalar.activation(self.rs[:, :], self.pair(3), ACT.Ln, bias=self.col("eps"), scale=1.0 / D).then_inc(N[1], 1)
        act.wait_ge(N[1], 1)
        self.nc.scalar.activation(self.rs[:, :], self.rs[:, :], ACT.Exp, scale=-0.5).then_inc(N[2], 1)

    def norm_act(self, act, N, scale, shift):
        self.norm_rstd(act, N)
        for i in range(KT):
            act.wait_ge(N[3], i + 1)
            if i >= 2:
                act.wait_ge(N[5], i - 1)
            args = dict(scale=scale[:, i:i + 1], bias=shift[:, i:i + 1])
            self.nc.scalar.activation(self.hb[:, i % 2, :], self.xr[:, i % 2, :], ACT.Identity, **args)
            self.nc.scalar.activation(self.hh[:, i, :], self.xr[:, i % 2, :], ACT.Identity, **args).then_inc(N[4], 1)

    def norm_dve(self, dve, N):
        nc = self.nc

        def lo(i):
            dve.wait_ge(N[4], i + 1)
            nc.vector.tensor_tensor(self.hl[:, i, :], self.hb[:, i % 2, :], self.hh[:, i, :].bitcast(F32),
                                    ALU.subtract).then_inc(N[5], 1)
        dve.wait_ge(N[2], 1)
        for i in range(KT):
            if i >= 2:
                dve.wait_ge(N[4], i - 1)
            nc.vector.tensor_tensor(self.xr[:, i % 2, :], self.x[:, i, :], self.rs[:, :], ALU.mult).then_inc(N[3], 1)
            if i:
                lo(i - 1)
        lo(KT - 1)


TOTAL_UNITS = N_PROJ_A + N_PROJ_B + N_PROJ_D + N_PROJ_C + 2 * (N_OUT + N_FFN)


def ada_tile(k, junk, w, silu_c, out):
    return k.nc.vector.scalar_tensor_tensor(junk, w, 1.0, silu_c, ALU.mult, ALU.mult, accum_out=out)


def start(k):
    nc = k.nc
    par_in, c_in, x_in0, x_in1, ring0, ring1, ring2, ring3, prime, c_ready, hi, split, chain = k.sems(
        "start", "par", "c", "x_in0", "x_in1", "ada_in0", "ada_in1", "ada_in2", "ada_in3", "prime", "silu_c", "hi", "split", "chain")
    Q = k.square_sems("start")
    ring = (ring0, ring1, ring2, ring3)
    ada_w, = k.work(k.H0, 65536, ada_w=[P, 4, 4, D])
    junk, silu_c = k.work(k.M0, 12288, junk=[P, 2, D], silu_c=[P, D])
    lbt, = k.work(k.M0 + 12288, 1024, lbt=[P, 2, 4])

    with nc.Block() as block:
        @block.sync
        def _(sp):
            sp.dma_start(silu_c[:, :], k.c_rows).then_inc(c_in, 16)
            sp.dma_start(flat(k.x[:, 0:4, :]), k.xT[:, 0:4 * T]).then_inc(x_in0, 16)
            sp.dma_start(k.par[:, :], k.params_d).then_inc(par_in, 16)
            sp.dma_start(k.ident[:, :], k.tables[:, TAB["ident"][0]:TAB["ident"][0] + 128]).then_inc(par_in, 16)
            sp.dma_start(k.ones[:, :], k.tables[:, TAB["ones"][0]:TAB["ones"][0] + 128]).then_inc(par_in, 16)
            sp.dma_start(ada_w[:, 0], k.w_ada[0]).then_inc(ring[0], 16)
            sp.dma_start(flat(k.x[:, 4:8, :]), k.xT[:, 4 * T:]).then_inc(x_in1, 16)
            for n in range(1, 4):
                sp.dma_start(ada_w[:, n], k.w_ada[n]).then_inc(ring[n], 16)
            for s in range(2):
                sp.dma_start(k.w_raw[:, s, :], k.w_units[s]).then_inc(prime, 16)

        @block.gpsimd
        def _(pool):
            k.clear_before(pool)
            pool.wait_ge(prime, 32)
            pool.tensor_copy(k.w_hi[:, 0, :], k.w_raw[:, 0, :]).then_inc(hi, 1)
            pool.wait_ge(hi, 1)
            pool.tensor_tensor(k.w_lo[:, 0, :], k.w_raw[:, 0, :], k.w_hi[:, 0, :].bitcast(F32), ALU.subtract).then_inc(split, 1)

        @block.vector
        def _(dve):
            k.credit(dve, Q[1])
            step = [0]

            def link(ins):
                ins.then_inc(chain, 1)
                step[0] += 1
                dve.wait_ge(chain, step[0])
            dve.wait_ge(par_in, 48)
            lg = k.par[:, COL["lb_logits"]:COL["lb_logits"] + 4]
            link(nc.vector.tensor_tensor(lbt[:, 0, :], lg, lg, ALU.subtract))
            dve.wait_ge(c_ready, 2)
            link(nc.vector.reciprocal(lbt[:, 1, :], k.lb[:, 2, :]))
            link(nc.vector.tensor_tensor(k.lb[:, 2, :], k.lb[:, 2, :], lbt[:, 1, :], ALU.mult))
            link(nc.vector.tensor_tensor(k.lb[:, 0, :], k.lb[:, 2, :], k.lb[:, 2, :], ALU.subtract))
            link(nc.vector.tensor_scalar(k.lb[:, 1, :], k.lb[:, 0, :], -1.0, 1.0, ALU.mult, ALU.add))
            for n in range(16):
                dve.wait_ge(ring[n // 4], 16)
                if n >= 2:
                    dve.wait_ge(chain, step[0] - 1)
                ada_tile(k, junk[:, n % 2, :], ada_w[:, n // 4, n % 4, :], silu_c[:, :], k.mod[:, 1, n:n + 1]).then_inc(chain, 1)
                step[0] += 1
                if n % 2:
                    if n // 2:
                        k.add_square(dve, Q, n // 2, n // 2 % 2)
            dve.wait_ge(chain, step[0])
            link(nc.vector.tensor_tensor(k.mod[:, 0, 0:16], k.mod[:, 1, 0:16], k.par[:, COL["b_ada"]:COL["b_ada"] + 16], ALU.add))
            link(nc.vector.tensor_tensor(k.mod[:, 1, 0:16], k.mod[:, 1, 0:16], k.par[:, COL["b_ada"] + 48:COL["b_ada"] + 64], ALU.add))
            for layer in range(2):
                w = k.par[:, COL["norm_mix"] + 8 * layer:COL["norm_mix"] + 8 * layer + 8]
                link(nc.vector.scalar_tensor_tensor(k.modA[:, 2 * layer, :], k.mod[:, layer, 8:16], 1.0, w, ALU.add, ALU.mult))

        @block.scalar
        def _(act):
            act.wait_ge(c_in, 16)
            nc.scalar.activation(silu_c[:, :], silu_c[:, :], ACT.Silu).then_inc(c_ready, 1)
            act.wait_ge(chain, 1)
            nc.scalar.activation(k.lb[:, 2, :], lbt[:, 0, :], ACT.Exp).then_inc(c_ready, 1)
            for i in range(KT):
                act.wait_ge(x_in0 if i < 4 else x_in1, 16)
                k.square(act, Q, i, (k.x[:, i, :], i % 2))


def final_norm(k, weight):
    nc = k.nc
    N = k.norm_sems("final")
    y_ready, stored = k.sems("final", "y", "stored")
    y, = k.work(k.H0, 32768, y=[P, KT, T])

    with nc.Block() as block:
        @block.sync
        def _(sp):
            for i in range(KT):
                sp.wait_ge(y_ready, i + 1)
                sp.dma_start(k.outT[:, i, :], y[:, i, :]).then_inc(stored, 16)
            sp.wait_ge(stored, 16 * KT)

        @block.gpsimd
        def _(pool):
            k.clear_before(pool)

        @block.tensor
        def _(pe):
            k.norm_mean(N)

        @block.scalar
        def _(act):
            k.norm_rstd(act, N)
            for i in range(KT):
                act.wait_ge(N[3], i + 1)
                nc.scalar.activation(y[:, i, :], k.xr[:, i % 2, :], ACT.Copy, scale=weight[:, i:i + 1]).then_inc(y_ready, 1)

        @block.vector
        def _(dve):
            dve.wait_ge(N[2], 1)
            for i in range(KT):
                if i >= 2:
                    dve.wait_ge(y_ready, i - 1)
                nc.vector.tensor_tensor(k.xr[:, i % 2, :], k.x[:, i, :], k.rs[:, :], ALU.mult).then_inc(N[3], 1)


def project(k, name, n_units, segments, gate_rows=None, f_tile=None, norm=None, spill=False, rest_of_ada=False):
    nc = k.nc
    S = k.stream_sems(name)
    done = S[4]
    free, p_ready, tap_done, conv_done, negated = k.sems(
        name, "psum_free", "p_ready", "tap_done", "conv_done", "negated")
    N = k.norm_sems(name) if norm else None
    spilled, ada_in0, ada_in1, ada_read, ada_prod, ada_done = k.sems(name, "x_spilled", "ada_in0", "ada_in1", "ada_read", "ada_prod", "ada_done")
    c_in, c_ready = k.sems(name, "c_in", "silu_c")
    silu_c = k.m[:, TGB, :]
    ada_in = (ada_in0, ada_in1)
    ada_w = (k.x[:, 4:8, :], k.m[:, TV:TV + 4, :])
    pbuf, cbuf = k.work(k.X0, 16384, p=[P, 2, T], cv=[P, 2, T]) if name.endswith("A") else (None, None)
    first = k.unit

    with nc.Block() as block:
        @block.sync
        def _(sp):
            if spill:
                sp.dma_start(k.x_spill, flat(k.x[:, :, :])).then_inc(spilled, 16)

            if rest_of_ada:
                sp.dma_start(silu_c, k.c_rows).then_inc(c_in, 16)

            def ada_load(j, slot):
                sp.wait_ge(ada_read, j - 1)
                sp.dma_start(ada_w[slot].rearrange("p a n -> p (a n)"),
                             k.w_ada[bass.ds(j + 2, 1)].rearrange("z p a n -> p (z a n)")).then_inc(ada_in[slot], 16)
            k.load_units(sp, S, n_units, ada_load if rest_of_ada else None)
            if spill:
                sp.wait_ge(spilled, 16)

        @block.gpsimd
        def _(pool):
            k.clear_before(pool)
            k.split_units(pool, S, n_units)

        @block.tensor
        def _(pe):
            if norm:
                k.norm_mean(N)
                k.multiply_first(first, N[5], S[3], done)

            def unit(j, slot, turn):
                pe.wait_ge(S[3], j + 1)
                pe.wait_ge(free, j + 1)
                k.multiply((first + slot) % 2, slot, k.hh, k.hl).then_inc(done, 1)
            in_pairs(pe, 2 if norm else 0, n_units, unit)

        @block.scalar
        def _(act):
            if norm:
                k.norm_act(act, N, *norm)
            if rest_of_ada:
                act.wait_ge(c_in, 16)
                nc.scalar.activation(silu_c, silu_c, ACT.Silu).then_inc(c_ready, 1)
            act.sem_inc(free, 2)
            at = 0
            for kind, tile, bias, extra, n in segments:
                def unit(j, slot, turn, kind=kind, tile=tile, bias=bias, at=at):
                    ps = k.pair((at + slot) % 2)
                    act.wait_ge(done, j + (at + 1))
                    dst = flat(k.m[:, bass.ds(j + tile, 1), :])
                    b = k.col(bias[0], j + bias[1])
                    if kind == "conv":
                        nc.scalar.activation(pbuf[:, slot, :], ps, ACT.Identity, bias=b).then_inc(p_ready, 1)
                        act.wait_ge(conv_done, j + 1)
                        nc.scalar.activation(dst, cbuf[:, slot, :], ACT.Silu).then_inc(free, 1)
                    elif kind == "copy":
                        nc.scalar.activation(dst, ps, ACT.Identity, bias=b).then_inc(free, 1)
                    elif kind == "silu":
                        nc.scalar.activation(dst, ps, ACT.Silu, bias=b).then_inc(free, 1)
                    elif kind == "gate_sigmoid":
                        nc.scalar.activation(dst, ps, ACT.Sigmoid, bias=b).then_inc(free, 1)
                    elif kind == "gate_silu":
                        nc.scalar.activation(dst, ps, ACT.Silu, bias=b).then_inc(free, 1)
                    elif kind == "forget":
                        nc.scalar.activation(flat(f_tile[:, bass.ds(j, 1), :]), ps, ACT.Sigmoid, bias=b)
                        nc.scalar.activation(dst, ps, ACT.Sigmoid, scale=-1.0,
                                             bias=k.small[:, 0, bass.ds(j, 1)]).then_inc(free, 1)
                if kind == "rows":
                    act.wait_ge(done, at + 1)
                    ps = k.pair(at % 2)
                    g0 = COL["b_gate"]
                    nc.scalar.activation(gate_rows[0], ps[0:4, :], ACT.Identity, bias=k.par[0:4, g0:g0 + 1])
                    nc.scalar.activation(gate_rows[1], ps[32:36, :], ACT.Identity, bias=k.par[32:36, g0:g0 + 1]).then_inc(free, 1)
                else:
                    if kind == "forget":
                        act.wait_ge(negated, 1)
                    if tile in (TGB, TV) and rest_of_ada:
                        act.wait_ge(ada_read, 10)
                    in_pairs(act, 0, n, unit)
                at += n

        @block.vector
        def _(dve):
            if norm:
                k.norm_dve(dve, N)
            if rest_of_ada:
                dve.wait_ge(c_ready, 1)
                dve.sem_inc(ada_read, 2)
                dve.sem_inc(ada_prod, 2)
                with dve.Fori(0, 4) as i:
                    for slot in range(2):
                        dve.wait_ge(ada_in[slot], i * 16 + 16)
                        for a in range(4):
                            n = i * 8 + (4 * slot + a)
                            dve.wait_ge(ada_prod, n + 1)
                            ada_tile(k, k.pair(2 + a % 2), ada_w[slot][:, a, :], silu_c, k.mod[:, 1, bass.ds(n + 16, 1)]).then_inc(ada_prod, 1)
                        dve.wait_ge(ada_prod, i * 8 + (4 * slot + 6))
                        dve.sem_inc(ada_read, 1)
                for layer in range(2):
                    b = COL["b_ada"] + 48 * layer
                    nc.vector.tensor_tensor(k.mod[:, layer, 16:48], k.mod[:, 1, 16:48], k.par[:, b + 16:b + 48], ALU.add).then_inc(ada_done, 1)
                    dve.wait_ge(ada_done, layer * 2 + 1)
                    w = k.par[:, COL["norm_ffn"] + 8 * layer:COL["norm_ffn"] + 8 * layer + 8]
                    nc.vector.scalar_tensor_tensor(k.modA[:, 2 * layer + 1, :], k.mod[:, layer, 32:40], 1.0, w, ALU.add, ALU.mult).then_inc(ada_done, 1)
                    dve.wait_ge(ada_done, layer * 2 + 2)
            at = 0
            for kind, tile, bias, extra, n in segments:
                if kind == "conv":
                    def conv(j, slot, turn):
                        c = cbuf[:, slot, :]
                        dve.wait_ge(p_ready, j + 1)
                        dve.wait_ge(free, j + 1)
                        nc.vector.tensor_scalar(c, pbuf[:, slot, :], k.col("conv_qk_w", j + 8 * (CONV_A - 1)),
                                                k.col("conv_qk_b", j), ALU.mult, ALU.add).then_inc(tap_done, 1)
                        for lag in range(1, CONV_A):
                            dve.wait_ge(tap_done, j * (CONV_A - 1) + lag)
                            nc.vector.scalar_tensor_tensor(
                                cbuf[:, slot, lag:T], pbuf[:, slot, 0:T - lag], k.col("conv_qk_w", j + 8 * (CONV_A - 1 - lag)),
                                cbuf[:, slot, lag:T], ALU.mult, ALU.add).then_inc(conv_done if lag == CONV_A - 1 else tap_done, 1)
                    in_pairs(dve, 0, n, conv)
                elif kind in ("gate_sigmoid", "gate_silu"):
                    def gate(j, slot, turn, tile=tile, extra=extra, at=at):
                        dst = flat(k.m[:, bass.ds(j + tile, 1), :])
                        dve.wait_ge(free, j + (at + 3))
                        nc.vector.tensor_scalar(dst, dst, k.col(extra, j), None, ALU.mult)
                    in_pairs(dve, 0, n, gate)
                elif kind == "forget":
                    b0 = COL[bias[0]] + bias[1]
                    nc.vector.tensor_scalar(k.small[:, 0, 0:4], k.par[:, b0:b0 + 4], -1.0, None, ALU.mult).then_inc(negated, 1)

                    def forget(j, slot, turn, tile=tile, at=at):
                        f = flat(f_tile[:, bass.ds(j, 1), :])
                        dst = flat(k.m[:, bass.ds(j + tile, 1), :])
                        dve.wait_ge(free, j + (at + 3))
                        nc.vector.tensor_scalar(f, f, k.lb[:, 1, bass.ds(j, 1)], k.lb[:, 0, bass.ds(j, 1)], ALU.mult, ALU.add)
                        nc.vector.tensor_scalar(dst, dst, k.lb[:, 1, bass.ds(j, 1)], None, ALU.mult)
                    in_pairs(dve, 0, n, forget)
                at += n
    k.unit += n_units


def out_project(k, name, layer):
    nc = k.nc
    S = k.stream_sems(name)
    done = S[4]
    free, hi_done, y_split, x_in = k.sems(name, "psum_free", "y_hi", "y_split", "x_back")
    Q = k.square_sems(name)
    x_home = k.xT if layer == 0 else k.x_spill
    first = k.unit
    gate = k.mod[:, layer, 16:24]

    with nc.Block() as block:
        @block.sync
        def _(sp):
            sp.dma_start(flat(k.x[:, :, :]), x_home).then_inc(x_in, 16)
            k.load_units(sp, S, N_OUT)

        @block.gpsimd
        def _(pool):
            k.clear_before(pool)
            k.split_units(pool, S, N_OUT)

        @block.scalar
        def _(act):
            for i in range(KT):
                nc.scalar.activation(k.hh[:, i, :], k.m[:, TGA + i, :], ACT.Copy).then_inc(hi_done, 1)
            act.wait_ge(y_split, KT)

            def unit(j, slot, turn):
                act.wait_ge(free, j + 3)
                x = k.x[:, j, :] if isinstance(j, int) else flat(k.x[:, bass.ds(j, 1), :])
                k.square(act, Q, j, (x, slot))
            unit(0, 0, 0)
            unit(1, 1, 0)
            in_pairs(act, 2, N_OUT, unit)

        @block.tensor
        def _(pe):
            k.multiply_first(first, y_split, S[3], done)

            def unit(j, slot, turn):
                pe.wait_ge(S[3], j + 1)
                pe.wait_ge(free, j + 1)
                k.multiply((first + slot) % 2, slot, k.hh, k.hl).then_inc(done, 1)
            in_pairs(pe, 2, N_OUT, unit)

        @block.vector
        def _(dve):
            dve.sem_inc(free, 2)
            k.credit(dve, Q[1])
            for i in range(KT):
                dve.wait_ge(hi_done, i + 1)
                nc.vector.tensor_tensor(k.hl[:, i, :], k.m[:, TGA + i, :], k.hh[:, i, :].bitcast(F32),
                                        ALU.subtract).then_inc(y_split, 1)
            dve.wait_ge(x_in, 16)

            def unit(j, slot, turn):
                x = flat(k.x[:, bass.ds(j, 1), :])
                dve.wait_ge(done, j + 1)
                nc.vector.scalar_tensor_tensor(x, k.pair(slot), gate[:, bass.ds(j, 1)], x, ALU.mult, ALU.add).then_inc(free, 1)
                k.add_square(dve, Q, j, slot)
            dve.wait_ge(done, 1)
            nc.vector.scalar_tensor_tensor(k.x[:, 0, :], k.pair(0), gate[:, 0:1], k.x[:, 0, :], ALU.mult, ALU.add).then_inc(free, 1)
            dve.wait_ge(done, 2)
            nc.vector.scalar_tensor_tensor(k.x[:, 1, :], k.pair(1), gate[:, 1:2], k.x[:, 1, :], ALU.mult, ALU.add).then_inc(free, 1)
            k.add_square(dve, Q, 1, 1)
            in_pairs(dve, 2, N_OUT, unit)
    k.unit += N_OUT


def ffn(k, name, layer, norm):
    nc = k.nc
    S = k.stream_sems(name)
    done = S[4]
    newest, tap1, tap_done, silu_done, prod, hi_done, split_done, down_done, down_free = k.sems(
        name, "newest_tap", "tap1", "taps_done", "silu_done", "product", "a_hi", "a_split", "down_done", "down_free")
    N, Q = k.norm_sems(name), k.square_sems(name)
    a_hi, a_lo, conv, sg = k.work(k.M0, 14 * T * 4, a_hi=([P, 2, 2, T], F32R), a_lo=([P, 2, 2, T], F32R),
                                  cv=[P, 4, T], sg=[P, 2, T])
    first = k.unit
    gate = k.mod[:, layer, 40:48]

    def cols(kind, g, u):
        tile = g * 2 + (u // 2 + (u % 2) * FFT)
        if kind == 3:
            return k.col("ffn_b", tile + 2 * FFT * layer)
        at = kind * 2 * FFT + FFN_CONV * 2 * FFT * layer
        return k.col("ffn_w0", tile + at)

    with nc.Block() as block:
        @block.sync
        def _(sp):
            k.load_units(sp, S, N_FFN)

        @block.gpsimd
        def _(pool):
            k.clear_before(pool)
            k.split_units(pool, S, N_FFN)

        @block.tensor
        def _(pe):
            def up(g, unit0, units=range(4)):
                for u in units:
                    pe.wait_ge(S[3], unit0 + (u + 1))
                    pe.wait_ge(tap_done, g * 4 + (u + 1))
                    k.multiply((first + u) % 2, u % 2, k.hh, k.hl).then_inc(done, 1)

            def down(g, parity, unit0):
                pe.wait_ge(split_done, g * 2 + 2)
                for u in range(2):
                    place = (first + u) % 2
                    pe.wait_ge(S[3], unit0 + (u + 1))
                    for o in range(4):
                        pe.wait_ge(down_free, g * 8 + (4 * u + o + 1))
                        for kk in range(2):
                            w_hi = k.w_hi[:, place, kk * HALF + o * P:kk * HALF + (o + 1) * P]
                            w_lo = k.w_lo[:, place, kk * HALF + o * P:kk * HALF + (o + 1) * P]
                            for n, (w, r) in enumerate(((w_hi, a_hi), (w_hi, a_lo), (w_lo, a_hi))):
                                for half in range(2):
                                    mm = nc.tensor.matmul(k.bank(4 + 2 * (o % 2) + half), w,
                                                          r[:, parity, kk, half * HALF:(half + 1) * HALF],
                                                          start=(kk == 0 and n == 0), stop=(kk == 1 and n == 2))
                        mm.then_inc(done if o == 3 else down_done, 1)

            k.norm_mean(N)
            k.multiply_first(first, N[5], S[3], done)
            up(0, 0, (2, 3))
            with pe.Fori(0, (GROUPS - 1) // 2) as i:
                for v in range(2):
                    g = i * 2 + (1 + v)
                    up(g, i * 12 + (6 * v + 4))
                    down(i * 2 + v, v, i * 12 + (6 * v + 8))
            down(GROUPS - 1, (GROUPS - 1) % 2, N_FFN - 2)

        @block.scalar
        def _(act):
            def group(g, parity, unit0):
                for u in range(4):
                    act.wait_ge(done, unit0 + (u + 1))
                    act.wait_ge(split_done, g * 2)
                    nc.scalar.activation(conv[:, u, :], k.pair(u % 2), ACT.Identity, bias=cols(3, g, u),
                                         scale=cols(2, g, u)).then_inc(newest, 1)
                    if u % 2:
                        act.wait_ge(tap_done, g * 4 + (u + 3))
                        nc.scalar.activation(sg[:, u // 2, :], conv[:, u, :], ACT.Silu).then_inc(silu_done, 1)
                        act.wait_ge(prod, g * 2 + (u // 2 + 1))
                        nc.scalar.activation(a_hi[:, parity, u // 2, :], conv[:, u - 1, :], ACT.Copy).then_inc(hi_done, 1)

            k.norm_act(act, N, *norm)
            group(0, 0, 0)
            with act.Fori(0, (GROUPS - 1) // 2) as i:
                for v in range(2):
                    group(i * 2 + (1 + v), (1 + v) % 2, i * 12 + (6 * v + 4))
            for o in range(KT):
                act.wait_ge(down_free, 2 + (GROUPS - 1) * KT + o + 1)
                k.square(act, Q, o, (k.x[:, o, :], o % 2))

        @block.vector
        def _(dve):
            def up(g, parity):
                for u in range(4):
                    ps = k.pair(u % 2)
                    dve.wait_ge(newest, g * 4 + (u + 1))
                    nc.vector.scalar_tensor_tensor(conv[:, u, 1:T], ps[:, 0:T - 1], cols(1, g, u), conv[:, u, 1:T],
                                                   ALU.mult, ALU.add).then_inc(tap1, 1)
                    dve.wait_ge(tap1, g * 4 + (u + 1))
                    nc.vector.scalar_tensor_tensor(conv[:, u, 2:T], ps[:, 0:T - 2], cols(0, g, u), conv[:, u, 2:T],
                                                   ALU.mult, ALU.add).then_inc(tap_done, 1)
                    if u % 2:
                        dve.wait_ge(silu_done, g * 2 + (u // 2 + 1))
                        nc.vector.tensor_tensor(conv[:, u - 1, :], conv[:, u - 1, :], sg[:, u // 2, :],
                                                ALU.mult).then_inc(prod, 1)
                        dve.wait_ge(hi_done, g * 2 + (u // 2 + 1))
                        nc.vector.tensor_tensor(a_lo[:, parity, u // 2, :], conv[:, u - 1, :],
                                                a_hi[:, parity, u // 2, :].bitcast(F32), ALU.subtract).then_inc(split_done, 1)

            def down(g, unit0, last=False):
                for o in range(KT):
                    if o % 4 == 3:
                        dve.wait_ge(done, unit0 + (o // 4 + 1))
                    else:
                        dve.wait_ge(down_done, g * 6 + (o // 4 * 3 + o % 4 + 1))
                    nc.vector.scalar_tensor_tensor(k.x[:, o, :], k.pair(2 + o % 2), gate[:, o:o + 1], k.x[:, o, :],
                                                   ALU.mult, ALU.add).then_inc(down_free, 1)
                    if last and o >= 2:
                        k.add_square(dve, Q, o - 1, (o - 1) % 2)
                if last:
                    k.add_square(dve, Q, KT - 1, (KT - 1) % 2)
            k.norm_dve(dve, N)
            k.credit(dve, Q[1])
            dve.sem_inc(tap_done, 2)
            dve.sem_inc(down_free, 2)
            up(0, 0)
            with dve.Fori(0, (GROUPS - 1) // 2) as i:
                for v in range(2):
                    up(i * 2 + (1 + v), (1 + v) % 2)
                    down(i * 2 + v, i * 12 + (6 * v + 8))
            down(GROUPS - 1, N_FFN - 2, last=True)
    k.unit += N_FFN


def chunk(ap4, c):
    return ap4[:, :, bass.ds(c * CH, CH)]


def mix_a(k):
    nc = k.nc
    q, kk, v = k.m[:, TQ:TQ + 4, :], k.m[:, TK:TK + 4, :], k.m[:, TV:TV + 4, :]
    rows = k.m[0:4, TGB:TGB + 4, :]
    (k_st, v_st, vaug, pr, qs, kw, dx, wi, state, sel, causal, lf, reset, acol, m_prev) = k.work(
        k.X0, 32768, k_st=[P, 4, CH], v_st=[P, 4, CH], vaug=[P, 4, DH + 1], pr=[P, 4, CH], qs=[P, 4, CH],
        kw=[P, 4, DH], dx=[P, 4, CH], wi=[P, 4, CH], state=[P, 4, DH + 1], sel=[4, 4, P], causal=[P, CH],
        lf=[4, T], reset=[4, T], acol=[P, NCH, 4], mprev=[P, 4, NCH])
    (tab_in, rows_f, chain, gates_done, cols_mm, cols_done, zeroed) = k.sems(
        "a_rows", "tables_in", "row_act", "chain", "gates", "cols_mm", "cols", "zeroed")
    (v_staged, vaug_ready, d_ready, wi_ready, o_stored, k_staged, x_ready, qs_ready, p_ready, kw_ready,
     st_done, g_done, tv_done, s_done, tk_done, num_done, st_mm) = k.sems(
        "a", "v_staged", "vaug", "d_ready", "wi_ready", "o_stored", "k_staged", "x_ready", "qs_ready", "p_ready",
        "kw_ready", "state_done", "g_rows", "v_turned", "scores", "k_turned", "numerator", "state_mm")
    den, em = k.small[:, 1, :], k.small[:, 2, :]
    i_row, F_row, m_row, G_row = rows[:, 0, :], rows[:, 1, :], rows[:, 2, :], rows[:, 3, :]
    bG, bS, bV, bK = 0, 1, 2, 3
    num = k.psum[:, 4:6, :].rearrange("p a (b n) -> p (a b) n", b=2)
    st = k.psum[:, 6:8, :].rearrange("p a (b n) -> p (a b) n", b=2)

    def heads(b):
        return k.psum[:, b, :].rearrange("p (h n) -> p h n", h=4)

    with nc.Block() as block:
        @block.sync
        def _(sp):
            a, n = TAB["sel"]
            sp.dma_start(sel[:, :, :].rearrange("p a n -> p (a n)"), k.tables[0:4, a:a + n]).then_inc(tab_in, 16)
            a, n = TAB["causal"]
            sp.dma_start(causal[:, :], k.tables[:, a:a + n]).then_inc(tab_in, 16)
            sp.wait_ge(tab_in, 32)

        @block.gpsimd
        def _(pool):
            k.clear_before(pool)
            pool.memset(state[:, :, :], 0.0).then_inc(zeroed, 1)
            pool.memset(vaug[:, :, DH:DH + 1], 1.0).then_inc(zeroed, 1)

        @block.scalar
        def _(act):
            k.credit(act, v_staged, vaug_ready, d_ready, wi_ready, o_stored)
            act.wait_ge(chain, 1)
            nc.scalar.activation(lf[:, :], F_row, ACT.Abs).then_inc(rows_f, 1)
            act.wait_ge(rows_f, 1)
            nc.scalar.activation(lf[:, :], lf[:, :], ACT.Exp, scale=-1.0).then_inc(rows_f, 1)
            act.wait_ge(rows_f, 2)
            nc.scalar.activation(lf[:, :], lf[:, :], ACT.Ln, bias=1.0).then_inc(rows_f, 1)
            act.wait_ge(cols_mm, 1)
            nc.scalar.activation(em, k.psum[:, 1, 0:32], ACT.Exp, scale=-1.0)
            nc.scalar.activation(m_prev[:, :, 1:NCH], k.psum[:, 2, 0:32].rearrange("p (h c) -> p h c", h=4)[:, :, 0:NCH - 1],
                                 ACT.Copy).then_inc(cols_done, 1)
            with act.Fori(0, NCH) as c:
                act.wait_ge(tv_done, c + 1)
                nc.scalar.activation(v_st[:, :, :], chunk(v, c), ACT.Copy).then_inc(v_staged, 1)
                act.wait_ge(tv_done, c + 2)
                act.wait_ge(st_mm, c + 1)
                nc.scalar.activation(vaug[:, :, 0:DH], heads(bV), ACT.Copy).then_inc(vaug_ready, 1)
                act.wait_ge(x_ready, c + 2)
                act.wait_ge(kw_ready, c + 1)
                nc.scalar.activation(dx[:, :, :], dx[:, :, :], ACT.Exp).then_inc(d_ready, 1)
                act.wait_ge(st_done, c + 1)
                act.wait_ge(g_done, c + 2)
                for h in range(4):
                    ins = nc.scalar.activation(wi[:, h, :], heads(bG)[:, h, :], ACT.Exp, bias=m_prev[:, h, bass.ds(c, 1)])
                ins.then_inc(wi_ready, 1)
                act.wait_ge(num_done, c + 2)
                nc.scalar.activation(den[:, bass.ds(c * 4, 4)], num[:, :, DH:DH + 1].rearrange("p h a -> p (h a)"), ACT.Copy)
                nc.scalar.activation(chunk(v, c), num[:, :, 0:DH], ACT.Copy).then_inc(o_stored, 1)

        @block.vector
        def _(dve):
            k.credit(dve, k_staged, x_ready, qs_ready, p_ready, kw_ready, st_done)
            step = [0]

            def link(ins):
                ins.then_inc(chain, 1)
                step[0] += 1
                dve.wait_ge(chain, step[0])
            fb = COL["f_bias"]
            link(nc.vector.tensor_scalar(F_row, F_row, k.par[0:4, fb:fb + 1], None, ALU.add))
            nc.vector.memset(reset[:, :], 1.0)
            link(nc.vector.memset(m_prev[:, :, :], 0.0))
            link(nc.vector.memset(reset[:, 0:T:CH], 0.0))
            dve.wait_ge(rows_f, 3)
            link(nc.vector.scalar_tensor_tensor(lf[:, :], F_row, 0.0, lf[:, :], ALU.min, ALU.subtract))
            link(nc.vector.tensor_tensor_scan(m_row, lf[:, :], i_row, 0.0, ALU.add, ALU.max))
            link(nc.vector.tensor_tensor_scan(F_row, reset[:, :], lf[:, :], 0.0, ALU.mult, ALU.add))
            link(nc.vector.tensor_tensor(i_row, i_row, F_row, ALU.subtract))
            nc.vector.tensor_tensor(G_row, F_row, m_row, ALU.subtract).then_inc(gates_done, 1)
            dve.wait_ge(cols_mm, 1)
            nc.vector.tensor_copy(acol[:, :, :], k.psum[:, 0, 0:32].rearrange("p (c h) -> p c h", h=4)).then_inc(cols_done, 1)
            dve.wait_ge(cols_done, 2)
            dve.wait_ge(zeroed, 2)
            dve.wait_ge(tab_in, 32)
            with dve.Fori(0, NCH) as c:
                dve.wait_ge(s_done, c + 1)
                dve.wait_ge(tk_done, c + 1)
                nc.vector.tensor_copy(k_st[:, :, :], chunk(kk, c)).then_inc(k_staged, 1)
                dve.wait_ge(g_done, c + 2)
                for h in range(4):
                    ins = nc.vector.scalar_tensor_tensor(dx[:, h, :], heads(bG)[:, h, :], acol[:, bass.ds(c, 1), h:h + 1].rearrange("p a n -> p (a n)"),
                                                         causal[:, :], ALU.add, ALU.add)
                ins.then_inc(x_ready, 1)
                dve.wait_ge(wi_ready, c + 2)
                dve.wait_ge(num_done, c + 1)
                nc.vector.scalar_tensor_tensor(qs[:, :, :], chunk(q, c), SCALE_A, wi[:, :, :], ALU.mult, ALU.mult).then_inc(qs_ready, 1)
                dve.wait_ge(d_ready, c + 2)
                dve.wait_ge(s_done, c + 2)
                nc.vector.scalar_tensor_tensor(pr[:, :, :], heads(bS), SCALE_A, dx[:, :, :], ALU.mult, ALU.mult).then_inc(p_ready, 1)
                dve.wait_ge(tk_done, c + 2)
                dve.wait_ge(st_mm, c + 1)
                nc.vector.tensor_tensor(kw[:, :, :], heads(bK), dx[:, :, CH - 1:CH].to_broadcast([P, 4, DH]), ALU.mult).then_inc(kw_ready, 1)
                dve.wait_ge(num_done, c + 2)
                dve.wait_ge(st_mm, c + 2)
                for h in range(4):
                    ins = nc.vector.scalar_tensor_tensor(state[:, h, :], state[:, h, :], wi[:, h, CH - 1:CH], st[:, h, 0:DH + 1],
                                                         ALU.mult, ALU.add)
                ins.then_inc(st_done, 1)

        @block.tensor
        def _(pe):
            k.credit(pe, g_done, tv_done, s_done, tk_done, num_done, st_mm)
            pe.wait_ge(gates_done, 1)
            pe.wait_ge(tab_in, 32)
            for c in range(NCH):
                nc.tensor.matmul(k.psum[:, 0, 4 * c:4 * c + 4], i_row[:, c * CH:(c + 1) * CH], k.ident[0:4, 0:4], start=True, stop=True)
                nc.tensor.matmul(k.psum[:, 1, 4 * c:4 * c + 4], m_row[:, c * CH:(c + 1) * CH], k.ident[0:4, 0:4], start=True, stop=True)
            for h in range(4):
                mm = nc.tensor.matmul(k.psum[:, 2, NCH * h:NCH * (h + 1)], sel[:, h, :], m_row[:, CH - 1:T:CH], start=True, stop=True)
            mm.then_inc(cols_mm, 1)
            pe.wait_ge(cols_done, 2)
            pe.wait_ge(zeroed, 2)
            with pe.Fori(0, NCH) as c:
                pe.wait_ge(x_ready, c + 1)
                pe.wait_ge(wi_ready, c + 1)
                for h in range(4):
                    mm = nc.tensor.matmul(heads(bG)[:, h, :], sel[:, h, :], G_row[:, bass.ds(c * CH, CH)], start=True, stop=True)
                mm.then_inc(g_done, 1)
                pe.wait_ge(v_staged, c + 2)
                pe.wait_ge(vaug_ready, c + 1)
                for h in range(4):
                    mm = nc.tensor.transpose(heads(bV)[:, h, :], v_st[:, h, :], k.ident[:, :])
                mm.then_inc(tv_done, 1)
                pe.wait_ge(k_staged, c + 2)
                pe.wait_ge(p_ready, c + 1)
                for h in range(4):
                    mm = nc.tensor.matmul(heads(bS)[:, h, :], k_st[:, h, :], q[:, h, bass.ds(c * CH, CH)], start=True, stop=True)
                mm.then_inc(s_done, 1)
                pe.wait_ge(kw_ready, c + 1)
                for h in range(4):
                    mm = nc.tensor.transpose(heads(bK)[:, h, :], k_st[:, h, :], k.ident[:, :])
                mm.then_inc(tk_done, 1)
                pe.wait_ge(vaug_ready, c + 2)
                pe.wait_ge(qs_ready, c + 2)
                pe.wait_ge(p_ready, c + 2)
                pe.wait_ge(st_done, c + 1)
                pe.wait_ge(o_stored, c + 1)
                for h in range(4):
                    nc.tensor.matmul(num[:, h, 0:DH + 1], pr[:, h, :], vaug[:, h, :], start=True, stop=False)
                    mm = nc.tensor.matmul(num[:, h, 0:DH + 1], qs[:, h, :], state[:, h, :], start=False, stop=True)
                mm.then_inc(num_done, 1)
                pe.wait_ge(kw_ready, c + 2)
                for h in range(4):
                    mm = nc.tensor.matmul(st[:, h, 0:DH + 1], kw[:, h, :], vaug[:, h, :], start=True, stop=True)
                mm.then_inc(st_mm, 1)


def finish_heads(k, name, gate_tile, mlstm=False, plain=None):
    nc = k.nc
    o = k.m[:, TV:TV + 4, :] if plain is None else k.m[:, plain:plain + 4, :]
    y = k.m[:, gate_tile:gate_tile + 4, :]
    sq, = k.work(k.X0, 8192, sq=[P, 2, NCH, DH])
    sq_ready, reduced, fac_ready, scaled, turned, stored, chain, ln = k.sems(
        name, "sq", "reduced", "factor", "scaled", "turned", "stored", "chain", "ln")
    ss, fac, r = k.small[:, 3, :], k.small[:, 4, :], k.small[:, 5, :]
    den, em = k.small[:, 1, :], k.small[:, 2, :]

    with nc.Block() as block:
        @block.gpsimd
        def _(pool):
            k.clear_before(pool)

        @block.scalar
        def _(act):
            if plain is None:
                for h in range(4):
                    if h >= 2:
                        act.wait_ge(reduced, h - 1)
                    nc.scalar.activation(sq[:, h % 2], o[:, h, :].rearrange("p (c n) -> p c n", c=NCH), ACT.Square).then_inc(sq_ready, 1)
                act.wait_ge(chain, 5 if mlstm else 1)
                nc.scalar.activation(fac, ss, ACT.Ln, bias=k.col("eps"), scale=1.0 / DH).then_inc(ln, 1)
                act.wait_ge(ln, 1)
                nc.scalar.activation(fac, fac, ACT.Exp, scale=-0.5).then_inc(fac_ready, 1)
            else:
                for n in range(0, 8, 2):
                    act.wait_ge(turned, n + 1)
                    h, g = n // 2, n % 2
                    nc.scalar.activation(y[:, h, g * HALF:(g + 1) * HALF], k.bank(n % 4), ACT.Copy).then_inc(stored, 1)

        @block.vector
        def _(dve):
            if plain is None:
                step = [0]

                def link(ins):
                    ins.then_inc(chain, 1)
                    step[0] += 1
                    dve.wait_ge(chain, step[0])
                for h in range(4):
                    dve.wait_ge(sq_ready, h + 1)
                    ins = nc.vector.tensor_reduce(ss[:, h * NCH:(h + 1) * NCH], sq[:, h % 2], axis=AX.X, op=ALU.add)
                    ins.then_inc(reduced, 1)
                dve.wait_ge(reduced, 4)
                if mlstm:
                    link(nc.vector.scalar_tensor_tensor(den, den, -1.0, den, ALU.mult, ALU.max))
                    link(nc.vector.tensor_tensor(r.rearrange("p (h c) -> p c h", h=4), den.rearrange("p (c h) -> p c h", h=4),
                                                 em.rearrange("p (c h) -> p c h", h=4), ALU.max))
                    link(nc.vector.reciprocal(r, r))
                    link(nc.vector.tensor_tensor(ss, ss, r, ALU.mult))
                    link(nc.vector.tensor_tensor(ss, ss, r, ALU.mult))
                else:
                    dve.sem_inc(chain, 1)
                dve.wait_ge(fac_ready, 1)
                if mlstm:
                    link(nc.vector.tensor_tensor(fac, fac, r, ALU.mult))
                for h in range(4):
                    oh = o[:, h, :].rearrange("p (c n) -> p c n", c=NCH)
                    f = fac[:, h * NCH:(h + 1) * NCH].rearrange("p (c n) -> p c n", n=1).to_broadcast([P, NCH, DH])
                    nc.vector.tensor_tensor(oh, oh, f, ALU.mult).then_inc(scaled, 1)
                for n in range(8):
                    dve.wait_ge(turned, n + 1)
                    h, g = n // 2, n % 2
                    yh = y[:, h, g * HALF:(g + 1) * HALF]
                    nc.vector.tensor_tensor(yh, k.bank(n % 4), yh, ALU.mult).then_inc(stored, 1)
            else:
                for n in range(1, 8, 2):
                    dve.wait_ge(turned, n + 1)
                    h, g = n // 2, n % 2
                    nc.vector.tensor_copy(y[:, h, g * HALF:(g + 1) * HALF], k.bank(n % 4)).then_inc(scaled, 1)

        @block.tensor
        def _(pe):
            for n in range(8):
                h, g = n // 2, n % 2
                if plain is None:
                    pe.wait_ge(scaled, h + 1)
                    if n >= 4:
                        pe.wait_ge(stored, n - 3)
                elif n >= 4:
                    pe.wait_ge(scaled if n % 2 else stored, n // 2 - 1)
                for c in range(4):
                    at = (g * 4 + c) * CH
                    mm = nc.tensor.transpose(k.bank(n % 4)[:, c * P:(c + 1) * P], o[:, h, at:at + CH], k.ident[:, :])
                mm.then_inc(turned, 1)


def mix_b(k, f_slot):
    nc = k.nc
    q, kk, v = k.m[:, TQ:TQ + 4, :], k.m[:, TK:TK + 4, :], k.m[:, TV:TV + 4, :]
    NL = len(LEVELS)
    Q, K, B, v_st, v_tok, kw, pr, state, levels, picked, diag = k.work(
        k.H0, 65536, Q=[P, NL + 2, 4, CH], K=[P, NL + 1, 4, CH], B=[P, NL + 1, 2 * CH], v_st=[P, 4, CH], v_tok=[P, 4, DH],
        kw=[P, 4, DH], pr=[P, 4, CH], state=[P, 4, DH], levels=[P, SMALL, 32], picked=[P, SMALL, 4, 32], diag=[P, 4, 32])
    (tab_in, zeroed, v_staged, v_turned, v_ready, base_in, q_lower, q_upper, k_upper, k_lower, blocks, small_mm, big_mm,
     pick, diag_ready, placed, big_stored, k_turned, kw_ready, num_done, o_stored, st_mm, st_done) = k.sems(
        "b", "tables_in", "zeroed", "v_staged", "v_turned", "v_ready", "base_in", "q_lower", "q_upper", "k_upper", "k_lower",
        "blocks", "small_mm", "big_mm", "picked", "diag_ready", "placed", "big_stored", "k_turned", "kw_ready", "num_done",
        "o_stored", "state_mm", "state_done")
    bSm, bBig, bV, bK, bN, bC = 0, 2, 3, 4, 5, 6

    def heads(b):
        return k.psum[:, b, :].rearrange("p (h n) -> p h n", h=4)

    def halves(ap, n, L):
        x = ap[:, n].rearrange("p h t -> p (h t)").rearrange("p (b u l) -> p b u l", u=2, l=L)
        return x[:, :, 0, :], x[:, :, 1, :]

    def decays(c, n, L):
        if n == 0:
            f = chunk(f_slot, c).rearrange("p h (b u) -> p h b u", u=2)
            return f[:, :, :, 0:1], f[:, :, :, 1:2]
        x = B[:, n, 0:4 * CH // L].rearrange("p (b u l) -> p b u l", u=2, l=1)
        return x[:, :, 0, :], x[:, :, 1, :]

    def spread(d, n, L):
        return d if n == 0 else d.to_broadcast([P, 2 * CH // L, L])

    def shaped(x, n):
        return x.rearrange("p (h b) l -> p h b l", h=4) if n == 0 else x

    with nc.Block() as block:
        @block.sync
        def _(sp):
            a, n = TAB["levels"]
            sp.dma_start(levels[:, :, :].rearrange("p a n -> p (a n)"), k.tables[:, a:a + n]).then_inc(tab_in, 16)
            sp.wait_ge(tab_in, 16)

        @block.gpsimd
        def _(pool):
            k.clear_before(pool)
            k.credit(pool, k_lower)
            pool.memset(state[:, :, :], 0.0).then_inc(zeroed, 1)
            pool.memset(pr[:, :, :], 0.0).then_inc(zeroed, 1)
            with pool.Fori(0, NCH) as c:
                for n, L in enumerate(LEVELS):
                    if n == 0:
                        pool.wait_ge(base_in, c + 2)
                        pool.wait_ge(k_turned, c + 1)
                    else:
                        pool.wait_ge(k_lower, c * NL + (n + 1))
                        pool.wait_ge(k_upper, c * NL + (n + 1))
                        pool.wait_ge(blocks, c * NL + (n + 1))
                    lo, _ = halves(K, n, L)
                    to, _ = halves(K, n + 1, L)
                    _, d = decays(c, n, L)
                    pool.tensor_tensor(shaped(to, n), shaped(lo, n), spread(d, n, L), ALU.mult).then_inc(k_lower, 1)

        @block.vector
        def _(dve):
            k.credit(dve, q_upper, blocks, pick, diag_ready, big_stored, kw_ready, o_stored, st_done)
            dve.wait_ge(tab_in, 16)
            dve.wait_ge(zeroed, 2)
            with dve.Fori(0, NCH) as c:
                dve.wait_ge(num_done, c + 1)
                dve.wait_ge(k_lower, c * NL + 1)
                nc.vector.tensor_tensor(Q[:, 1], chunk(q, c), chunk(f_slot, c), ALU.mult).then_inc(q_upper, 1)
                for n, L in enumerate(LEVELS):
                    dve.wait_ge(q_upper, c * (NL + 1) + (n + 2))
                    if n:
                        dve.wait_ge(q_lower, c * NL + (n + 1))
                        dve.wait_ge(blocks, c * NL + (n + 1))
                    _, up = halves(Q, n + 1, L)
                    _, to = halves(Q, n + 2, L)
                    d, d2 = decays(c, n, L)
                    nc.vector.tensor_tensor(shaped(to, n), shaped(up, n), spread(d, n, L), ALU.mult).then_inc(q_upper, 1)
                    out = B[:, n + 1, 0:2 * CH // L].rearrange("p (b l) -> p b l", l=1)
                    nc.vector.tensor_tensor(shaped(out, n), d, d2, ALU.mult).then_inc(blocks, 1)
                dve.wait_ge(small_mm, c + 2)
                ps = k.psum[:, 0:2, :].rearrange("p a n -> p (a n)")
                for a, b in ((0, 4), (4, SMALL)):
                    ins = nc.vector.tensor_tensor(
                        picked[:, a:b], ps[:, a * 128:b * 128].rearrange("p (l h t) -> p l h t", h=4, t=32),
                        levels[:, a:b].rearrange("p l (h t) -> p l h t", h=1).to_broadcast([P, b - a, 4, 32]), ALU.mult)
                ins.then_inc(pick, 1)
                dve.wait_ge(pick, c + 2)
                dve.wait_ge(placed, c + 1)
                nc.vector.tensor_reduce(diag[:, :, :].rearrange("p h t -> p (h t)"),
                                        picked[:, :, :, :].rearrange("p l h t -> p (h t) l"), axis=AX.X, op=ALU.add).then_inc(diag_ready, 1)
                dve.wait_ge(big_mm, c + 2)
                for j in range(3):
                    ins = nc.vector.tensor_copy(pr[32 * j:32 * j + 32, :, 32 * (j + 1):CH], heads(bBig)[32 * j:32 * j + 32, :, 32 * (j + 1):CH])
                ins.then_inc(big_stored, 1)
                dve.wait_ge(k_turned, c + 2)
                dve.wait_ge(st_mm, c + 1)
                nc.vector.tensor_copy(kw[:, :, :], heads(bK)).then_inc(kw_ready, 1)
                dve.wait_ge(num_done, c + 2)
                nc.vector.tensor_scalar(chunk(v, c), heads(bN), 1.0, None, ALU.mult).then_inc(o_stored, 1)
                for h in range(4):
                    ins = nc.vector.scalar_tensor_tensor(state[:, h, :], state[:, h, :], B[:, NL, h:h + 1], heads(bC)[:, h, :],
                                                         ALU.mult, ALU.add)
                ins.then_inc(st_done, 1)

        @block.scalar
        def _(act):
            k.credit(act, base_in, v_staged, q_lower, k_upper, v_ready, placed)
            with act.Fori(0, NCH) as c:
                act.wait_ge(num_done, c + 1)
                act.wait_ge(k_lower, c * NL + 1)
                nc.scalar.activation(K[:, 0], chunk(kk, c), ACT.Copy)
                nc.scalar.activation(Q[:, 0], chunk(q, c), ACT.Copy).then_inc(base_in, 1)
                act.wait_ge(v_turned, c + 1)
                nc.scalar.activation(v_st[:, :, :], chunk(v, c), ACT.Copy).then_inc(v_staged, 1)
                act.wait_ge(k_turned, c + 1)
                for n, L in enumerate(LEVELS):
                    act.wait_ge(q_upper, c * (NL + 1) + (n + 2))
                    if n:
                        act.wait_ge(q_lower, c * NL + (n + 1))
                        act.wait_ge(k_upper, c * NL + (n + 1))
                        act.wait_ge(k_lower, c * NL + (n + 1))
                    else:
                        act.wait_ge(base_in, c + 2)
                    lo, _ = halves(Q, n + 1, L)
                    to, _ = halves(Q, n + 2, L)
                    nc.scalar.activation(to, lo, ACT.Copy).then_inc(q_lower, 1)
                    _, up = halves(K, n, L)
                    _, to = halves(K, n + 1, L)
                    nc.scalar.activation(to, up, ACT.Copy).then_inc(k_upper, 1)
                    if n == 1:
                        act.wait_ge(v_turned, c + 2)
                        act.wait_ge(st_mm, c + 1)
                        nc.scalar.activation(v_tok[:, :, :], heads(bV), ACT.Copy).then_inc(v_ready, 1)
                act.wait_ge(diag_ready, c + 2)
                act.wait_ge(num_done, c + 1)
                for j in range(4):
                    ins = nc.scalar.activation(pr[32 * j:32 * j + 32, :, 32 * j:32 * j + 32], diag[32 * j:32 * j + 32, :, :], ACT.Copy)
                ins.then_inc(placed, 1)

        @block.tensor
        def _(pe):
            k.credit(pe, v_turned, small_mm, big_mm, k_turned, st_mm, num_done)
            pe.wait_ge(zeroed, 2)
            with pe.Fori(0, NCH) as c:
                pe.wait_ge(v_staged, c + 2)
                pe.wait_ge(v_ready, c + 1)
                for h in range(4):
                    mm = nc.tensor.transpose(heads(bV)[:, h, :], v_st[:, h, :], k.ident[:, :])
                mm.then_inc(v_turned, 1)
                pe.wait_ge(pick, c + 1)
                for n in range(SMALL):
                    qi, ki = n, max(n - 1, 0)
                    if n == 0:
                        pe.wait_ge(base_in, c + 2)
                    else:
                        pe.wait_ge(q_upper, c * (NL + 1) + (n + 1))
                    if n >= 2:
                        pe.wait_ge(q_lower, c * NL + n)
                        pe.wait_ge(k_lower, c * NL + n)
                        pe.wait_ge(k_upper, c * NL + n)
                    for h in range(4):
                        for j in range(4):
                            out = k.psum[32 * j:32 * j + 32, n // 4, (n % 4) * 128 + h * 32:(n % 4) * 128 + h * 32 + 32]
                            mm = nc.tensor.matmul(out, K[:, ki, h, 32 * j:32 * j + 32], Q[:, qi, h, 32 * j:32 * j + 32],
                                                  start=True, stop=True)
                mm.then_inc(small_mm, 1)
                pe.wait_ge(big_stored, c + 1)
                pe.wait_ge(q_lower, c * NL + 6)
                pe.wait_ge(q_upper, c * (NL + 1) + 7)
                pe.wait_ge(k_lower, c * NL + 6)
                pe.wait_ge(k_upper, c * NL + 6)
                for h in range(4):
                    for s0 in (0, 64):
                        nc.tensor.matmul(heads(bBig)[s0:s0 + 32, h, s0 + 32:s0 + 64], K[:, 5, h, s0:s0 + 32], Q[:, 6, h, s0 + 32:s0 + 64],
                                         start=True, stop=True)
                pe.wait_ge(q_lower, c * NL + 7)
                pe.wait_ge(q_upper, c * (NL + 1) + 8)
                pe.wait_ge(k_lower, c * NL + 7)
                pe.wait_ge(k_upper, c * NL + 7)
                for h in range(4):
                    mm = nc.tensor.matmul(heads(bBig)[0:64, h, 64:128], K[:, 6, h, 0:64], Q[:, 7, h, 64:128], start=True, stop=True)
                mm.then_inc(big_mm, 1)
                pe.wait_ge(kw_ready, c + 1)
                pe.wait_ge(k_lower, c * NL + 8)
                pe.wait_ge(k_upper, c * NL + 8)
                for h in range(4):
                    mm = nc.tensor.transpose(heads(bK)[:, h, :], K[:, NL, h, :], k.ident[:, :])
                mm.then_inc(k_turned, 1)
                pe.wait_ge(v_ready, c + 2)
                pe.wait_ge(kw_ready, c + 2)
                pe.wait_ge(st_done, c + 1)
                for h in range(4):
                    mm = nc.tensor.matmul(heads(bC)[:, h, :], kw[:, h, :], v_tok[:, h, :], start=True, stop=True)
                mm.then_inc(st_mm, 1)
                pe.wait_ge(q_upper, c * (NL + 1) + 9)
                pe.wait_ge(q_lower, c * NL + 8)
                pe.wait_ge(placed, c + 2)
                pe.wait_ge(big_stored, c + 2)
                pe.wait_ge(o_stored, c + 1)
                for h in range(4):
                    nc.tensor.matmul(heads(bN)[:, h, :], pr[:, h, :], v_tok[:, h, :], start=True, stop=False)
                    mm = nc.tensor.matmul(heads(bN)[:, h, :], Q[:, NL + 1, h, :], state[:, h, :], start=False, stop=True)
                mm.then_inc(num_done, 1)


def rotate(k):
    nc = k.nc
    cos, sin, swap, a, b = k.work(k.X0, 32768, cos=[P, T], sin=[P, T], swap=[P, P], a=[P, 2, T], b=[P, 2, T])
    tab_in, swapped, with_cos, with_sin, done = k.sems("rotary", "tables_in", "swapped", "with_cos", "with_sin", "done")
    n_tiles = 2 * HEADS

    with nc.Block() as block:
        @block.sync
        def _(sp):
            for buf, name in ((swap, "swap"), (cos, "cos"), (sin, "sin")):
                at, n = TAB[name]
                sp.dma_start(buf[:, :], k.tables[:, at:at + n]).then_inc(tab_in, 16)
            sp.wait_ge(tab_in, 48)

        @block.tensor
        def _(pe):
            pe.wait_ge(tab_in, 48)

            def one(j, slot, turn):
                pe.wait_ge(with_sin, j + 1)
                for half in range(2):
                    mm = nc.tensor.matmul(k.bank(2 * slot + half), swap[:, :], k.m[:, bass.ds(j, 1), half * HALF:(half + 1) * HALF].rearrange("p a n -> p (a n)"),
                                          start=True, stop=True)
                mm.then_inc(swapped, 1)
            in_pairs(pe, 0, n_tiles, one)

        @block.gpsimd
        def _(pool):
            k.clear_before(pool)
            pool.wait_ge(tab_in, 48)
            pool.sem_inc(done, 2)

            def one(j, slot, turn):
                pool.wait_ge(done, j + 1)
                pool.tensor_tensor(a[:, slot, :], flat(k.m[:, bass.ds(j, 1), :]), cos[:, :], ALU.mult).then_inc(with_cos, 1)
            in_pairs(pool, 0, n_tiles, one)

        @block.vector
        def _(dve):
            dve.wait_ge(tab_in, 48)
            dve.sem_inc(with_sin, 2)

            def one(j, slot, turn):
                dve.wait_ge(swapped, j + 1)
                nc.vector.tensor_tensor(b[:, slot, :], k.pair(slot), sin[:, :], ALU.mult).then_inc(with_sin, 1)
                dve.wait_ge(with_sin, j + 3)
                dve.wait_ge(with_cos, j + 1)
                nc.vector.tensor_tensor(flat(k.m[:, bass.ds(j, 1), :]), a[:, slot, :], b[:, slot, :], ALU.add).then_inc(done, 1)
            in_pairs(dve, 0, n_tiles, one)


def mix_c(k):
    nc = k.nc
    q, kk, v = k.m[:, TQ:TQ + 4, :], k.m[:, TK:TK + 4, :], k.m[:, TV:TV + 4, :]
    (k_st, v_st, v_tok, pr, qs, kw, state, decay, gq, gk, gc) = k.work(
        k.X0, 32768, k_st=[P, 4, CH], v_st=[P, 4, CH], v_tok=[P, 4, DH], pr=[P, 4, CH], qs=[P, 4, CH],
        kw=[P, 4, DH], state=[P, 4, DH], decay=[P, 4, CH], gq=[P, 4, CH], gk=[P, 4, 1], gc=[P, 4, 1])
    (tab_in, zeroed, v_staged, v_ready, o_stored, k_staged, qs_ready, p_ready, kw_ready, decayed, st_done, tv_done, s_done,
     tk_done, num_done, st_mm) = k.sems(
        "c", "tables_in", "zeroed", "v_staged", "v_ready", "o_stored", "k_staged", "qs_ready", "p_ready", "kw_ready",
        "decayed", "state_done", "v_turned", "scores", "k_turned", "numerator", "state_mm")
    bS, bV, bK, bN, bC = 0, 1, 2, 3, 4

    def heads(b):
        return k.psum[:, b, :].rearrange("p (h n) -> p h n", h=4)

    with nc.Block() as block:
        @block.sync
        def _(sp):
            for buf, name in ((decay, "decay"), (gq, "gq"), (gk, "gk"), (gc, "gc")):
                at, n = TAB[name]
                sp.dma_start(buf[:, :, :].rearrange("p a n -> p (a n)"), k.tables[:, at:at + n]).then_inc(tab_in, 16)
            sp.wait_ge(tab_in, 64)

        @block.gpsimd
        def _(pool):
            k.clear_before(pool)
            k.credit(pool, qs_ready)
            pool.memset(state[:, :, :], 0.0).then_inc(zeroed, 1)
            pool.wait_ge(tab_in, 64)
            with pool.Fori(0, NCH) as c:
                pool.wait_ge(num_done, c + 1)
                pool.tensor_tensor(qs[:, :, :], chunk(q, c), gq[:, :, :], ALU.mult).then_inc(qs_ready, 1)

        @block.scalar
        def _(act):
            k.credit(act, v_staged, v_ready)
            with act.Fori(0, NCH) as c:
                act.wait_ge(tv_done, c + 1)
                nc.scalar.activation(v_st[:, :, :], chunk(v, c), ACT.Copy).then_inc(v_staged, 1)
                act.wait_ge(tv_done, c + 2)
                act.wait_ge(num_done, c + 1)
                act.wait_ge(st_mm, c + 1)
                nc.scalar.activation(v_tok[:, :, :], heads(bV), ACT.Copy).then_inc(v_ready, 1)

        @block.vector
        def _(dve):
            k.credit(dve, k_staged, p_ready, kw_ready, o_stored, decayed, st_done)
            dve.wait_ge(zeroed, 1)
            dve.wait_ge(tab_in, 64)
            with dve.Fori(0, NCH) as c:
                dve.wait_ge(s_done, c + 1)
                dve.wait_ge(tk_done, c + 1)
                nc.vector.tensor_copy(k_st[:, :, :], chunk(kk, c)).then_inc(k_staged, 1)
                dve.wait_ge(s_done, c + 2)
                dve.wait_ge(num_done, c + 1)
                nc.vector.tensor_tensor(pr[:, :, :], heads(bS), decay[:, :, :], ALU.mult).then_inc(p_ready, 1)
                dve.wait_ge(tk_done, c + 2)
                dve.wait_ge(st_mm, c + 1)
                nc.vector.tensor_tensor(kw[:, :, :], heads(bK), gk[:, :, :].to_broadcast([P, 4, DH]), ALU.mult).then_inc(kw_ready, 1)
                dve.wait_ge(num_done, c + 2)
                nc.vector.tensor_scalar(chunk(v, c), heads(bN), 1.0, None, ALU.mult).then_inc(o_stored, 1)
                nc.vector.tensor_tensor(state[:, :, :], state[:, :, :], gc[:, :, :].to_broadcast([P, 4, DH]), ALU.mult).then_inc(decayed, 1)
                dve.wait_ge(decayed, c + 2)
                dve.wait_ge(st_mm, c + 2)
                nc.vector.tensor_tensor(state[:, :, :], heads(bC), state[:, :, :], ALU.add).then_inc(st_done, 1)

        @block.tensor
        def _(pe):
            k.credit(pe, tv_done, s_done, tk_done, num_done, st_mm)
            pe.wait_ge(zeroed, 1)
            with pe.Fori(0, NCH) as c:
                pe.wait_ge(v_staged, c + 2)
                pe.wait_ge(v_ready, c + 1)
                for h in range(4):
                    mm = nc.tensor.transpose(heads(bV)[:, h, :], v_st[:, h, :], k.ident[:, :])
                mm.then_inc(tv_done, 1)
                pe.wait_ge(k_staged, c + 2)
                pe.wait_ge(p_ready, c + 1)
                for h in range(4):
                    mm = nc.tensor.matmul(heads(bS)[:, h, :], k_st[:, h, :], q[:, h, bass.ds(c * CH, CH)], start=True, stop=True)
                mm.then_inc(s_done, 1)
                pe.wait_ge(kw_ready, c + 1)
                for h in range(4):
                    mm = nc.tensor.transpose(heads(bK)[:, h, :], k_st[:, h, :], k.ident[:, :])
                mm.then_inc(tk_done, 1)
                pe.wait_ge(v_ready, c + 2)
                pe.wait_ge(qs_ready, c + 2)
                pe.wait_ge(p_ready, c + 2)
                pe.wait_ge(st_done, c + 1)
                pe.wait_ge(o_stored, c + 1)
                for h in range(4):
                    nc.tensor.matmul(heads(bN)[:, h, :], pr[:, h, :], v_tok[:, h, :], start=True, stop=False)
                    mm = nc.tensor.matmul(heads(bN)[:, h, :], qs[:, h, :], state[:, h, :], start=False, stop=True)
                mm.then_inc(num_done, 1)
                pe.wait_ge(kw_ready, c + 2)
                for h in range(4):
                    mm = nc.tensor.matmul(heads(bC)[:, h, :], kw[:, h, :], v_tok[:, h, :], start=True, stop=True)
                mm.then_inc(st_mm, 1)


def mix_d(k):
    nc = k.nc
    v = k.m[:, TV:TV + 4, :]
    u, beta, turned_a, prod = k.work(k.X0, 32768, u=[P, 2, T], beta=[P, 2, T], at=[P, 2, T], prod=[P, T + 8])
    q_st, k_st, v_st = k.work(k.M0 + TGA * T * 4, 16384, q_st=[P, 2, T], k_st=[P, T], v_st=[P, T])
    (tab_in, v_turned, v_back, q_zero, q_staged, k_staged, v_staged, z_done, sig_done, ready, scanned, a_done, a_turned,
     at_stored, av_done, y_stored) = k.sems(
        "d", "tables_in", "v_turned", "v_back", "q_zero", "q_staged", "k_staged", "v_staged", "z", "sigmoids", "ready",
        "scanned", "weights", "weights_turned", "weights_back", "av", "y_stored")
    barrier, = k.work(k.X0 + 28672 + 64, 4096, barrier=[P, P])
    NB = T // P
    PER = 2 * NB

    with nc.Block() as block:
        @block.sync
        def _(sp):
            at, n = TAB["barrier"]
            sp.dma_start(barrier[:, :], k.tables[:, at:at + n]).then_inc(tab_in, 16)
            sp.wait_ge(tab_in, 16)

        @block.scalar
        def _(act):
            k.credit(act, q_staged, sig_done, at_stored)
            for n in range(8):
                act.wait_ge(v_turned, n + 1)
                ft, g = n // 2, n % 2
                nc.scalar.activation(v[:, ft, g * HALF:(g + 1) * HALF], k.bank(n % 4), ACT.Copy).then_inc(v_back, 1)
            act.wait_ge(q_zero, 1)

            def sigmoids(hp, n):
                w, par = P * (n % NB + 1), n % 2
                act.wait_ge(z_done, hp * PER + (n + 2))
                nc.scalar.activation(u[:, par, 0:w], k.pair(par)[:, 0:w], ACT.Sigmoid, scale=-SCALE_D)
                nc.scalar.activation(beta[:, par, 0:w], k.pair(par)[:, 0:w], ACT.Sigmoid, scale=SCALE_D).then_inc(sig_done, 1)

            with act.Fori(0, HEADS) as hp:
                act.wait_ge(z_done, hp * PER + 1)
                nc.scalar.activation(q_st[0:DH_D, 0, :], flat(k.m[0:DH_D, bass.ds(hp + TQ, 1), :]), ACT.Copy)
                nc.scalar.activation(q_st[DH_D:P, 1, :], flat(k.m[DH_D:P, bass.ds(hp + TQ, 1), :]), ACT.Copy).then_inc(q_staged, 1)
                act.wait_ge(a_turned, hp * PER + 1)
                sigmoids(hp, 0)
                sigmoids(hp, 1)
                for n in range(PER):
                    w, par = P * (n % NB + 1), n % 2
                    act.wait_ge(a_turned, hp * PER + (n + 2))
                    if n >= 2:
                        act.wait_ge(av_done, hp * PER + n)
                    nc.scalar.activation(turned_a[:, par, 0:w], k.pair(2)[:, 0:w], ACT.Copy).then_inc(at_stored, 1)
                    if n + 2 < PER:
                        sigmoids(hp, n + 2)

        @block.gpsimd
        def _(pool):
            k.clear_before(pool)
            k.credit(pool, v_staged)
            pool.memset(q_st[:, :, :], 0.0).then_inc(q_zero, 1)
            pool.wait_ge(v_back, 8)
            with pool.Fori(0, HEADS) as hp:
                pool.wait_ge(av_done, hp * PER + 1)
                pool.tensor_tensor(v_st[:, :], flat(v[:, bass.ds(hp, 1), :]), k.ones[:, 0:1].to_broadcast([P, T]), ALU.mult).then_inc(v_staged, 1)

        @block.vector
        def _(dve):
            k.credit(dve, k_staged, scanned, a_done, y_stored)
            nc.vector.memset(prod[:, 0:1], 1.0).then_inc(ready, 1)
            dve.wait_ge(ready, 1)
            with dve.Fori(0, HEADS) as hp:
                dve.wait_ge(z_done, hp * PER + 1)
                nc.vector.tensor_copy(k_st[:, ::-1], flat(k.m[:, bass.ds(hp + TK, 1), :])).then_inc(k_staged, 1)
                for n in range(PER):
                    w, par = P * (n % NB + 1), n % 2
                    dve.wait_ge(sig_done, hp * PER + (n + 2))
                    dve.wait_ge(a_done, hp * PER + (n + 1))
                    nc.vector.tensor_tensor_scan(prod[:, 1:w + 1], u[:, par, 0:w], u[:, par, 0:w], 1.0, ALU.mult, ALU.bypass).then_inc(scanned, 1)
                    dve.wait_ge(scanned, hp * PER + (n + 2))
                    nc.vector.tensor_tensor(u[:, par, 0:w][:, ::-1], beta[:, par, 0:w], prod[:, 0:w], ALU.mult).then_inc(a_done, 1)
                dve.wait_ge(av_done, hp * PER + (PER + 1))
                nc.vector.tensor_scalar(flat(k.m[:, bass.ds(hp + TGB, 1), :]), k.pair(3), 1.0, None, ALU.mult).then_inc(y_stored, 1)

        @block.tensor
        def _(pe):
            k.credit(pe, z_done, a_turned, av_done)
            for n in range(8):
                ft, g = n // 2, n % 2
                if n >= 4:
                    pe.wait_ge(v_back, n - 3)
                for c in range(4):
                    at = g * HALF + c * P
                    mm = nc.tensor.transpose(k.bank(n % 4)[:, c * P:(c + 1) * P], v[:, ft, at:at + P], k.ident[:, :])
                mm.then_inc(v_turned, 1)
            pe.wait_ge(v_back, 8)
            pe.wait_ge(tab_in, 16)

            def scores(hp, n):
                tb, hh, par = n % NB, n // NB, n % 2
                w = P * (tb + 1)
                if n >= 2:
                    pe.wait_ge(sig_done, hp * PER + n)
                for a in range(0, w, HALF):
                    b = min(w, a + HALF)
                    mm = nc.tensor.matmul(k.pair(par)[:, a:b], q_st[:, hh, tb * P:(tb + 1) * P], k_st[:, T - w + a:T - w + b],
                                          start=True, stop=(a > 0))
                    if a == 0:
                        mm = nc.tensor.matmul(k.pair(par)[:, 0:P], k.ident[:, :], barrier[:, :], start=False, stop=True)
                mm.then_inc(z_done, 1)

            def turn(hp, n):
                pe.wait_ge(a_done, hp * PER + (n + 2))
                pe.wait_ge(at_stored, hp * PER + (n + 1))
                for c in range(n % NB + 1):
                    mm = nc.tensor.transpose(k.pair(2)[:, c * P:(c + 1) * P], u[:, n % 2, c * P:(c + 1) * P], k.ident[:, :])
                mm.then_inc(a_turned, 1)

            def with_v(hp, n):
                tb, hh, par = n % NB, n // NB, n % 2
                pe.wait_ge(at_stored, hp * PER + (n + 2))
                for c in range(tb + 1):
                    at = c * P + hh * DH_D
                    mm = nc.tensor.matmul(k.pair(3)[DH_D * hh:DH_D * (hh + 1), tb * P:(tb + 1) * P],
                                          v_st[:, at:at + DH_D], turned_a[:, par, c * P:(c + 1) * P],
                                          start=(c == 0), stop=(c == tb))
                mm.then_inc(av_done, 1)

            with pe.Fori(0, HEADS) as hp:
                pe.wait_ge(q_staged, hp + 2)
                pe.wait_ge(k_staged, hp + 2)
                pe.wait_ge(sig_done, hp * PER + 1)
                scores(hp, 0)
                scores(hp, 1)
                for n in range(PER):
                    turn(hp, n)
                    if n + 2 < PER:
                        scores(hp, n + 2)
                    if n == 1:
                        pe.wait_ge(v_staged, hp + 2)
                        pe.wait_ge(y_stored, hp + 1)
                    if n:
                        with_v(hp, n - 1)
                with_v(hp, PER - 1)


def hybrid_trunk(nc, xT, params, tables, w_ada, c_rows, w_units, outT, stop=None, dump=None):
    with ExitStack() as ctx:
        k = Trunk(nc, ctx, xT, params, tables, w_ada, c_rows, w_units, outT)
        steps = [
            ("start", lambda: start(k)),
            ("projA", lambda: project(k, "projA", N_PROJ_A, [
                ("conv", TQ, ("b_even", 0), None, 8),
                ("rows", None, None, None, 1),
                ("gate_sigmoid", TGA, ("b_even", 8), "mlstm_norm", 4),
                ("copy", TV, ("b_even", 12), None, 4)],
                gate_rows=(k.m[0:4, TGB, :], k.m[0:4, TGB + 1, :]), norm=(k.modA[:, 0, :], k.mod[:, 0, 0:8]))),
            ("mixA", lambda: mix_a(k)),
            ("finA", lambda: finish_heads(k, "finA", TGA, mlstm=True)),
            ("projB", lambda: project(k, "projB", N_PROJ_B, [
                ("silu", TQ, ("b_even", 16), None, 4),
                ("forget", TK, ("b_even", 20), None, 4),
                ("gate_silu", TGB, ("b_even", 28), "hgrn_norm", 4),
                ("copy", TV, ("b_even", 24), None, 4)], f_tile=k.x[:, 0:4, :], rest_of_ada=True)),
            ("mixB", lambda: mix_b(k, k.x[:, 0:4, :])),
            ("finB", lambda: finish_heads(k, "finB", TGB)),
            ("out0", lambda: out_project(k, "out0", 0)),
            ("ffn0", lambda: ffn(k, "ffn0", 0, (k.modA[:, 1, :], k.mod[:, 0, 24:32]))),
            ("projD", lambda: project(k, "projD", N_PROJ_D, [
                ("copy", TQ, ("b_odd", 16), None, 4),
                ("copy", TK, ("b_odd", 20), None, 4),
                ("copy", TV, ("b_odd", 24), None, 4)], norm=(k.modA[:, 2, :], k.mod[:, 1, 0:8]), spill=True)),
            ("mixD", lambda: mix_d(k)),
            ("projC", lambda: project(k, "projC", N_PROJ_C, [
                ("copy", TQ, ("b_odd", 0), None, 8),
                ("gate_silu", TGA, ("b_odd", 12), "ret_norm", 4),
                ("copy", TV, ("b_odd", 8), None, 4)])),
            ("rotary", lambda: rotate(k)),
            ("mixC", lambda: mix_c(k)),
            ("finC", lambda: finish_heads(k, "finC", TGA)),
            ("out1", lambda: out_project(k, "out1", 1)),
            ("ffn1", lambda: ffn(k, "ffn1", 1, (k.modA[:, 3, :], k.mod[:, 1, 24:32]))),
            ("final", lambda: final_norm(k, k.par[:, COL["norm_final"]:COL["norm_final"] + 8])),
        ]
        for name, step in steps:
            k.phase(step)
            if name == stop:
                k.phase(lambda: dump(k))
                break
        k.held.close()


def make_tables():
    t = np.zeros((P, N_TAB), np.float64)

    def put(name, a):
        at, n = TAB[name]
        t[0:a.shape[0], at:at + n] = a.reshape(a.shape[0], n)
    i = np.arange(P)
    put("ident", np.eye(P))
    put("ones", np.ones((P, P)))
    put("causal", np.where(i[:, None] <= i[None, :], 0.0, -1e30))
    lv = np.zeros((P, SMALL, 32))
    s, u = (i % 32)[:, None], np.arange(32)[None, :]
    lv[:, 0] = s == u
    for n in range(1, SMALL):
        L = 2 ** (n - 1)
        lv[:, n] = (s // (2 * L) == u // (2 * L)) & (s % (2 * L) < L) & (u % (2 * L) >= L)
    put("levels", lv)
    put("sel", np.repeat(np.eye(4)[:, :, None], P, axis=2))
    strict = (i[:, None] + i[None, :]) > P - 1
    put("barrier", np.where(strict, 0.0, -1e30))
    swap = np.zeros((P, P))
    swap[i[64:], i[64:] - 64] = -1.0
    swap[i[:64], i[:64] + 64] = 1.0
    put("swap", swap)
    gamma = np.log1p(-(2.0 ** (-5.0 - np.arange(HEADS))))
    lag = i[None, :] - i[:, None]
    put("decay", np.where(lag[:, None, :] >= 0, np.exp(np.maximum(lag, 0)[:, None, :] * gamma[None, :, None]), 0.0) * SCALE_A)
    put("gq", np.broadcast_to(np.exp((i + 1)[None, None, :] * gamma[None, :, None]), (P, HEADS, P)) * SCALE_A)
    put("gk", np.exp((P - 1 - i)[:, None] * gamma[None, :]))
    put("gc", np.broadcast_to(np.exp(P * gamma)[None, :], (P, HEADS)))
    inv = (np.float32(10000.0) ** (-np.arange(0, DH, 2, dtype=np.float32) / np.float32(DH))).astype(np.float32)
    ang = (np.arange(T, dtype=np.float32)[None, :] * inv[:, None]).astype(np.float64)
    put("cos", np.tile(np.cos(ang), (2, 1)))
    put("sin", np.tile(np.sin(ang), (2, 1)))
    return t.astype(np.float32)


def lay_out(x, c, w_ada, b_ada, norm_mix, norm_ffn, norm_final, w_in_even, b_in_even, conv_qk_w, conv_qk_b, mlstm_f_bias,
            mlstm_norm, hgrn_lb_logits, hgrn_norm, w_in_odd, b_in_odd, ret_norm, w_out, ffn_up, ffn_conv_w, ffn_conv_b, ffn_down):
    def feature_columns(a):
        a = np.asarray(a)
        return np.moveaxis(a.reshape(-1, P), 0, 1)

    def units(w):
        return w.reshape(KT, P, -1, P).transpose(2, 1, 0, 3).reshape(-1, P, KT * P)

    G = GROUP_W
    be, bo = b_in_even[0], b_in_odd[0]
    even = w_in_even[0]
    qk, va, oa = slice(0, 2 * G), slice(2 * G, 3 * G), slice(3 * G, 4 * G)
    ia, fa = slice(4 * G, 4 * G + 4), slice(4 * G + 4, 4 * G + 8)
    rest = 4 * G + 8
    qb, fb, ib, gb = (slice(rest + i * G, rest + (i + 1) * G) for i in range(4))
    rows = np.zeros((D, P), np.float32)
    rows[:, 0:4] = even[:, ia]
    rows[:, 32:36] = even[:, fa]
    odd = w_in_odd[0]
    qc, kc, vc, gc, qd, kd, vd = (slice(i * G, (i + 1) * G) for i in range(7))

    def ffn_units(layer):
        up = units(ffn_up[layer])
        dn = ffn_down[layer].reshape(GROUPS, 2, P, 2, HALF).transpose(0, 3, 2, 1, 4).reshape(GROUPS, 2, P, 2 * HALF)
        out = []
        for g in range(GROUPS + 1):
            if g < GROUPS:
                out += [up[2 * g], up[FFT + 2 * g], up[2 * g + 1], up[FFT + 2 * g + 1]]
            if g:
                out += [dn[g - 1, 0], dn[g - 1, 1]]
        return np.stack(out)

    w_units = np.concatenate([
        units(even[:, qk]), units(rows), units(even[:, oa]), units(even[:, va]),
        units(even[:, qb]), units(even[:, fb]), units(even[:, gb]), units(even[:, ib]),
        units(w_out[0]), ffn_units(0),
        units(odd[:, qd]), units(odd[:, kd]), units(odd[:, vd]),
        units(odd[:, qc]), units(odd[:, kc]), units(odd[:, gc]), units(odd[:, vc]),
        units(w_out[1]), ffn_units(1)])

    par = np.zeros((P, COL["all"]), np.float32)

    def put(name, a):
        par[0:a.shape[0], COL[name]:COL[name] + a.shape[1]] = a
    put("b_ada", feature_columns(b_ada))
    put("norm_mix", feature_columns(norm_mix))
    put("norm_ffn", feature_columns(norm_ffn))
    put("norm_final", feature_columns(norm_final))
    put("b_even", feature_columns(np.concatenate([be[qk], be[oa], be[va], be[qb], be[fb], be[ib], be[gb]])))
    gate = np.zeros((P, 1), np.float32)
    gate[0:4, 0] = be[ia]
    gate[32:36, 0] = be[fa]
    put("b_gate", gate)
    put("f_bias", mlstm_f_bias[0][:, None])
    put("conv_qk_w", feature_columns(conv_qk_w[0]))
    put("conv_qk_b", feature_columns(conv_qk_b))
    put("mlstm_norm", feature_columns(mlstm_norm))
    put("lb_logits", feature_columns(hgrn_lb_logits))
    put("hgrn_norm", feature_columns(hgrn_norm))
    put("b_odd", feature_columns(bo))
    put("ret_norm", feature_columns(ret_norm))
    fw = feature_columns(ffn_conv_w)
    n = 6 * FFT
    put("ffn_w0", fw[:, :n])
    put("ffn_w1", fw[:, n:])
    put("ffn_b", feature_columns(ffn_conv_b))
    put("eps", np.full((P, 1), EPS, np.float32))

    return {
        "xT": np.ascontiguousarray(x[0].T.reshape(KT, P, T).transpose(1, 0, 2).reshape(P, KT * T)),
        "params": par,
        "tables": make_tables(),
        "w_ada": np.ascontiguousarray(w_ada.reshape(D, 12, 4, P).transpose(1, 3, 2, 0)),
        "c_rows": np.ascontiguousarray(np.broadcast_to(c.reshape(1, D), (P, D))),
        "w_units": np.ascontiguousarray(w_units),
    }


def kernel(**inputs):
    import concourse.bacc as bacc
    from concourse.bass_utils import run_bass_kernel_spmd

    arrays = lay_out(**{n: np.asarray(a) for n, a in inputs.items()})
    nc = bacc.Bacc("TRN2", target_bir_lowering=False, num_devices=1)
    args = [nc.dram_tensor(n, a.shape, mybir.dt.from_np(a.dtype), kind="ExternalInput").ap() for n, a in arrays.items()]
    out = nc.dram_tensor("outT", (P, KT, T), F32, kind="ExternalOutput").ap()
    hybrid_trunk(nc, *args, out)
    got = run_bass_kernel_spmd(nc, [arrays], core_ids=[0]).results[0]["outT"]
    return np.ascontiguousarray(got.transpose(1, 0, 2).reshape(D, T).T).reshape(1, T, D)
```

```python
from contextlib import ExitStack

import numpy as np

import concourse.bass as bass
from concourse import mybir

F32 = mybir.dt.float32
F32R = mybir.dt.float32r
ALU = mybir.AluOpType
ACT = mybir.ActivationFunctionType
AX = mybir.AxisListType

P = 128
D = 1024
T = 1024
KT = D // P
HALF = 512
HEADS = 4
DH = 128
GROUP_W = HEADS * DH
CH = 128
NCH = T // CH
D_FF = 2816
FFT = D_FF // P
GROUPS = FFT // 2
H_D = 8
DH_D = 64
EPS = 1e-6
CONV_A = 4
FFN_CONV = 3
SCALE_A = float(DH) ** -0.5
SCALE_D = float(DH_D) ** -0.5
LEVELS = [1, 2, 4, 8, 16, 32, 64]
SMALL = 6

TQ, TK, TV, TGA, TGB = 0, 4, 8, 12, 16

N_PROJ_A, N_PROJ_B, N_PROJ_D, N_PROJ_C = 17, 16, 12, 16
N_OUT, N_FFN = 8, 66


def columns():
    sizes = [("b_ada", 96), ("norm_mix", 16), ("norm_ffn", 16), ("norm_final", 8),
             ("b_even", 32), ("b_gate", 1), ("f_bias", 1), ("conv_qk_w", 8 * CONV_A), ("conv_qk_b", 8),
             ("mlstm_norm", 4), ("lb_logits", 4), ("hgrn_norm", 4), ("b_odd", 28), ("ret_norm", 4),
             ("ffn_w0", 6 * FFT), ("ffn_w1", 6 * FFT), ("ffn_b", 4 * FFT), ("eps", 1)]
    out, at = {}, 0
    for name, n in sizes:
        out[name] = at
        at += n
    out["all"] = at
    return out


COL = columns()

TAB = {}
_at = 0
for _name, _n in (("ident", 128), ("ones", 128), ("causal", 128), ("levels", SMALL * 32), ("sel", 512),
                  ("barrier", 128), ("decay", 512), ("gq", 512), ("gk", 4), ("gc", 4),
                  ("cos", 1024), ("sin", 1024)):
    TAB[_name] = (_at, _n)
    _at += _n
N_TAB = _at


def in_pairs(eng, start, stop, body):
    turns = (stop - start) // 2
    if turns > 0:
        with eng.Fori(0, turns) as i:
            for u in range(2):
                body(i * 2 + (start + u), u, i)
    if (stop - start) % 2:
        body(stop - 1, 0, turns)


def flat(ap):
    return ap.rearrange("p a n -> p (a n)")


class Trunk:
    def __init__(self, nc, ctx, xT, params, tables, w_ada, c_rows, w_units, outT):
        self.nc, self.ctx = nc, ctx
        self.xT, self.params_d, self.tables, self.w_ada, self.c_rows, self.w_units, self.outT = xT, params, tables, w_ada, c_rows, w_units, outT
        self.x_spill = nc.dram_tensor("x_spill", (P, KT * T), F32, kind="Internal").ap()
        self.held, self.mine, self.before = ExitStack(), [], []
        self.unit = 0
        self.top = 16512
        place = self.place
        self.ident = place("ident", [P, 128], F32)
        self.ones = place("ones", [P, 128], F32)
        self.par = place("par", [P, COL["all"]], F32)
        self.mod = place("mod", [P, 2, 48], F32)
        self.modA = place("modA", [P, 4, 8], F32)
        self.lb = place("lb", [P, 3, 4], F32)
        self.small = place("small", [P, 8, 32], F32)
        self.top = 16512 + 7680
        self.w_raw = place("w_raw", [P, 2, 1024], F32)
        self.w_hi = place("w_hi", [P, 2, 1024], F32R)
        self.w_lo = place("w_lo", [P, 2, 1024], F32R)
        self.X0 = self.top
        self.x = place("x", [P, KT, T], F32)
        self.H0 = self.top
        self.hh = place("hh", [P, KT, T], F32R)
        self.hl = place("hl", [P, KT, T], F32R)
        self.M0 = self.top
        self.m = place("m", [P, 20, T], F32)
        self.psum = ctx.enter_context(nc.psum_tensor("ps", [P, 8, HALF], F32))
        self.n_place = 0
        self.acc, self.sq = self.work(self.M0 + 14 * T * 4, 12288, acc=[P, T], sq=[P, 2, T])
        self.rs, self.xr, self.hb = self.work(self.M0 + 15 * T * 4, 20480, rs=[P, T], xr=[P, 2, T], hb=[P, 2, T])

    def place(self, name, shape, dt):
        n = 4
        for s in shape[1:]:
            n *= s
        t = self.nc.alloc_sbuf_tensor_at(name, shape, dt, offset=self.top)
        self.top += (n + 31) // 32 * 32
        assert self.top <= 229368, (name, self.top)
        return t

    def work(self, start, limit, **shapes):
        keep, self.top, out = self.top, start, []
        self.n_place += 1
        for name, shape in shapes.items():
            dt = F32
            if isinstance(shape, tuple):
                shape, dt = shape
            out.append(self.place(f"{name}_{self.n_place}", shape, dt))
        assert self.top <= start + limit, (self.top - start, limit)
        self.top = keep
        return out

    def sems(self, phase, *names):
        new = [self.held.enter_context(self.nc.semaphore(f"{phase}_{n}")) for n in names]
        self.mine += new
        return new

    def phase(self, build):
        self.before, self.mine, last = self.mine, [], self.held
        self.held = ExitStack()
        build()
        last.close()

    def credit(self, eng, *sems):
        for s in sems:
            eng.sem_inc(s, 1)

    def clear_before(self, eng):
        for s in self.before:
            eng.sem_clear(s)

    def col(self, name, i=0):
        if isinstance(i, int):
            return self.par[:, COL[name] + i:COL[name] + i + 1]
        return self.par[:, bass.ds(i + COL[name], 1)]

    def pair(self, q):
        return self.psum[:, 2 * q:2 * q + 2, :].rearrange("p a n -> p (a n)")

    def bank(self, b, n=HALF):
        return self.psum[:, b, 0:n]

    def stream_sems(self, name):
        return self.sems(name, "loaded_even", "loaded_odd", "hi", "split", "unit_done")

    def load_units(self, eng, sems, n, beside=None):
        first = self.unit
        loaded, split = sems[0:2], sems[3]
        last = min(n + 2, TOTAL_UNITS - first)

        def load(j, slot, turn):
            eng.wait_ge(split, j - 1)
            place = (first + slot) % 2
            src = self.w_units[bass.ds(j + first, 1), :, :].rearrange("a p n -> p (a n)")
            eng.dma_start(self.w_raw[:, place, :], src).then_inc(loaded[slot], 16)
            if beside is not None and turn is not None:
                beside(j, slot)
        if beside is None:
            in_pairs(eng, 2, last, load)
        else:
            in_pairs(eng, 2, 10, load)
            in_pairs(eng, 10, last, lambda j, slot, turn: load(j, slot, None))
        count = last - 2
        eng.wait_ge(loaded[0], 16 * ((count + 1) // 2))
        if count > 1:
            eng.wait_ge(loaded[1], 16 * (count // 2))

    def split_units(self, eng, sems, n):
        first = self.unit
        loaded, hi, split, done = sems[0:2], sems[2], sems[3], sems[4]
        raw, w_hi, w_lo = self.w_raw, self.w_hi, self.w_lo
        one = self.ones[:, 0:1].to_broadcast([P, 1024])

        self.credit(eng, split)
        place = (first + 1) % 2
        eng.tensor_tensor(w_hi[:, place, :], raw[:, place, :], one, ALU.mult).then_inc(hi, 1)
        eng.wait_ge(hi, 1)
        eng.tensor_tensor(w_lo[:, place, :], raw[:, place, :], w_hi[:, place, :].bitcast(F32),
                          ALU.subtract).then_inc(split, 1)
        stop = min(n + 1, TOTAL_UNITS - first)

        def rest(j, slot, turn):
            place = (first + slot) % 2
            eng.wait_ge(loaded[slot], (turn + 1) * 16)
            eng.wait_ge(done, j - 1)
            eng.tensor_tensor(w_hi[:, place, :], raw[:, place, :], one, ALU.mult).then_inc(hi, 1)
            eng.wait_ge(hi, j)
            eng.tensor_tensor(w_lo[:, place, :], raw[:, place, :], w_hi[:, place, :].bitcast(F32),
                              ALU.subtract).then_inc(split, 1)
        in_pairs(eng, 2, stop, rest)

    def multiply(self, place, psum_pair, rhs_hi, rhs_lo):
        nc = self.nc
        for k in range(KT):
            w_hi = self.w_hi[:, place, k * P:(k + 1) * P]
            w_lo = self.w_lo[:, place, k * P:(k + 1) * P]
            for n, (w, r) in enumerate(((w_hi, rhs_hi), (w_hi, rhs_lo), (w_lo, rhs_hi))):
                for half in range(2):
                    mm = nc.tensor.matmul(self.bank(2 * psum_pair + half), w,
                                          r[:, k, half * HALF:(half + 1) * HALF],
                                          start=(k == 0 and n == 0), stop=(k == KT - 1 and n == 2))
        return mm


    def multiply_first(self, first, rhs_ready, split, done, order=range(KT), between=None):
        nc = self.nc
        nc.tensor.wait_ge(split, 2)
        for n_ready, k in enumerate(order):
            if between and n_ready == KT // 2:
                between()
            nc.tensor.wait_ge(rhs_ready, n_ready + 1)
            for u in range(2):
                place = (first + u) % 2
                w_hi = self.w_hi[:, place, k * P:(k + 1) * P]
                w_lo = self.w_lo[:, place, k * P:(k + 1) * P]
                for n, (w, r) in enumerate(((w_hi, self.hh), (w_hi, self.hl), (w_lo, self.hh))):
                    for half in range(2):
                        mm = nc.tensor.matmul(self.bank(2 * u + half), w, r[:, k, half * HALF:(half + 1) * HALF],
                                              start=(n_ready == 0 and n == 0), stop=(n_ready == KT - 1 and n == 2))
                if n_ready == KT - 1:
                    mm.then_inc(done, 1)

    def square_sems(self, name):
        return self.sems(name, "squared", "summed")

    def square(self, act, S, i, x):
        if not isinstance(i, int) or i >= 3:
            act.wait_ge(S[1], i - 1)
        dst = self.acc[:, :] if isinstance(i, int) and i == 0 else self.sq[:, x[1], :]
        self.nc.scalar.activation(dst, x[0], ACT.Square).then_inc(S[0], 1)

    def add_square(self, dve, S, i, slot):
        dve.wait_ge(S[0], i + 1)
        dve.wait_ge(S[1], i)
        self.nc.vector.tensor_tensor(self.acc[:, :], self.acc[:, :], self.sq[:, slot, :], ALU.add).then_inc(S[1], 1)

    def norm_sems(self, name):
        return self.sems(name, "mean", "ln", "rstd", "x_rstd", "h_hi", "h_ready")

    def norm_mean(self, N):
        for half in range(2):
            mm = self.nc.tensor.matmul(self.bank(6 + half), self.ones[:, :], self.acc[:, half * HALF:(half + 1) * HALF],
                                       start=True, stop=True)
        mm.then_inc(N[0], 1)

    def norm_rstd(self, act, N):
        act.wait_ge(N[0], 1)
        self.nc.scalar.activation(self.rs[:, :], self.pair(3), ACT.Ln, bias=self.col("eps"), scale=1.0 / D).then_inc(N[1], 1)
        act.wait_ge(N[1], 1)
        self.nc.scalar.activation(self.rs[:, :], self.rs[:, :], ACT.Exp, scale=-0.5).then_inc(N[2], 1)

    def norm_act(self, act, N, scale, shift, rstd_before=False):
        if not rstd_before:
            self.norm_rstd(act, N)
        for i in range(KT):
            act.wait_ge(N[3], i + 1)
            if i >= 2:
                act.wait_ge(N[5], i - 1)
            args = dict(scale=scale[:, i:i + 1], bias=shift[:, i:i + 1])
            self.nc.scalar.activation(self.hb[:, i % 2, :], self.xr[:, i % 2, :], ACT.Identity, **args)
            self.nc.scalar.activation(self.hh[:, i, :], self.xr[:, i % 2, :], ACT.Identity, **args).then_inc(N[4], 1)

    def norm_dve(self, dve, N, rstd_before=False):
        nc = self.nc

        def lo(i):
            dve.wait_ge(N[4], i + 1)
            nc.vector.tensor_tensor(self.hl[:, i, :], self.hb[:, i % 2, :], self.hh[:, i, :].bitcast(F32),
                                    ALU.subtract).then_inc(N[5], 1)
        if not rstd_before:
            dve.wait_ge(N[2], 1)
        for i in range(KT):
            if i >= 2:
                dve.wait_ge(N[4], i - 1)
            nc.vector.tensor_tensor(self.xr[:, i % 2, :], self.x[:, i, :], self.rs[:, :], ALU.mult).then_inc(N[3], 1)
            if i:
                lo(i - 1)
        lo(KT - 1)


TOTAL_UNITS = N_PROJ_A + N_PROJ_B + N_PROJ_D + N_PROJ_C + 2 * (N_OUT + N_FFN)


def ada_tile(k, junk, w, silu_c, out):
    return k.nc.vector.scalar_tensor_tensor(junk, w, 1.0, silu_c, ALU.mult, ALU.mult, accum_out=out)


def start(k):
    nc = k.nc
    par_in, c_in, x_in0, x_in1, ada0, ada1, ada2, ada3, units_in, c_ready, hi, split, chain = k.sems(
        "start", "par", "c", "x_in0", "x_in1", "ada_in0", "ada_in1", "ada_in2", "ada_in3", "units_in", "silu_c",
        "hi", "split", "chain")
    squared, summed, ln = k.sems("start", "squared", "summed", "ln")
    ada_in = (ada0, ada1, ada2, ada3)
    ada_w, = k.work(k.H0, 65536, ada_w=[P, 4, 4, D])
    junk, silu_c, sq = k.work(k.M0, 12 * 2048 + 4096, junk=[P, 2, D], silu_c=[P, D], sq=[P, 2, T])
    lbt, = k.work(k.M0 + 5 * T * 4, 1024, lbt=[P, 2, 4])

    with nc.Block() as block:
        @block.sync
        def _(sp):
            sp.dma_start(silu_c[:, :], k.c_rows).then_inc(c_in, 16)
            sp.dma_start(flat(k.x[:, 0:4, :]), k.xT[:, 0:4 * T]).then_inc(x_in0, 16)
            sp.dma_start(k.par[:, :], k.params_d).then_inc(par_in, 16)
            sp.dma_start(k.ident[:, :], k.tables[:, TAB["ident"][0]:TAB["ident"][0] + 128]).then_inc(par_in, 16)
            sp.dma_start(k.ones[:, :], k.tables[:, TAB["ones"][0]:TAB["ones"][0] + 128]).then_inc(par_in, 16)
            for s in range(2):
                sp.dma_start(k.w_raw[:, s, :], k.w_units[s]).then_inc(units_in, 16)
            sp.dma_start(ada_w[:, 0], k.w_ada[0]).then_inc(ada_in[0], 16)
            sp.dma_start(flat(k.x[:, 4:8, :]), k.xT[:, 4 * T:]).then_inc(x_in1, 16)
            for n in range(1, 4):
                sp.dma_start(ada_w[:, n], k.w_ada[n]).then_inc(ada_in[n], 16)

        @block.gpsimd
        def _(pool):
            k.clear_before(pool)
            pool.wait_ge(units_in, 32)
            pool.tensor_copy(k.w_hi[:, 0, :], k.w_raw[:, 0, :]).then_inc(hi, 1)
            pool.wait_ge(hi, 1)
            pool.tensor_tensor(k.w_lo[:, 0, :], k.w_raw[:, 0, :], k.w_hi[:, 0, :].bitcast(F32), ALU.subtract).then_inc(split, 1)

        @block.vector
        def _(dve):
            step = [0]

            def link(ins):
                ins.then_inc(chain, 1)
                step[0] += 1
                dve.wait_ge(chain, step[0])
            dve.wait_ge(par_in, 48)
            lg = k.par[:, COL["lb_logits"]:COL["lb_logits"] + 4]
            link(nc.vector.tensor_tensor(lbt[:, 0, :], lg, lg, ALU.subtract))
            dve.wait_ge(c_ready, 2)
            link(nc.vector.reciprocal(lbt[:, 1, :], k.lb[:, 2, :]))
            link(nc.vector.tensor_tensor(k.lb[:, 2, :], k.lb[:, 2, :], lbt[:, 1, :], ALU.mult))
            link(nc.vector.tensor_tensor(k.lb[:, 0, :], k.lb[:, 2, :], k.lb[:, 2, :], ALU.subtract))
            link(nc.vector.tensor_scalar(k.lb[:, 1, :], k.lb[:, 0, :], -1.0, 1.0, ALU.mult, ALU.add))
            for n in range(16):
                dve.wait_ge(ada_in[n // 4], 16)
                if n >= 2:
                    dve.wait_ge(chain, step[0] - 1)
                ada_tile(k, junk[:, n % 2, :], ada_w[:, n // 4, n % 4, :], silu_c[:, :], k.mod[:, 1, n:n + 1]).then_inc(chain, 1)
                step[0] += 1
            dve.wait_ge(chain, step[0])
            link(nc.vector.tensor_tensor(k.mod[:, 0, 0:16], k.mod[:, 1, 0:16], k.par[:, COL["b_ada"]:COL["b_ada"] + 16], ALU.add))
            link(nc.vector.tensor_tensor(k.mod[:, 1, 0:16], k.mod[:, 1, 0:16], k.par[:, COL["b_ada"] + 48:COL["b_ada"] + 64], ALU.add))
            for layer in range(2):
                w = k.par[:, COL["norm_mix"] + 8 * layer:COL["norm_mix"] + 8 * layer + 8]
                link(nc.vector.scalar_tensor_tensor(k.modA[:, 2 * layer, :], k.mod[:, layer, 8:16], 1.0, w, ALU.add, ALU.mult))

        @block.scalar
        def _(act):
            act.wait_ge(c_in, 16)
            nc.scalar.activation(silu_c[:, :], silu_c[:, :], ACT.Silu).then_inc(c_ready, 1)
            act.wait_ge(chain, 1)
            nc.scalar.activation(k.lb[:, 2, :], lbt[:, 0, :], ACT.Exp).then_inc(c_ready, 1)
            for i in range(KT):
                act.wait_ge(x_in0 if i < 4 else x_in1, 16)
                if i >= 2:
                    act.wait_ge(summed, i - 1)
                nc.scalar.activation(sq[:, i % 2, :], k.x[:, i, :], ACT.Square).then_inc(squared, 1)
            act.wait_ge(summed, KT)
            nc.scalar.activation(k.rs[:, :], k.pair(3), ACT.Ln, bias=k.col("eps"), scale=1.0 / D).then_inc(ln, 1)
            act.wait_ge(ln, 1)
            nc.scalar.activation(k.rs[:, :], k.rs[:, :], ACT.Exp, scale=-0.5)

        @block.tensor
        def _(pe):
            pe.wait_ge(par_in, 48)
            for i in range(KT):
                pe.wait_ge(squared, i + 1)
                for half in range(2):
                    mm = nc.tensor.matmul(k.bank(6 + half), k.ones[:, :], sq[:, i % 2, half * HALF:(half + 1) * HALF],
                                          start=(i == 0), stop=(i == KT - 1))
                mm.then_inc(summed, 1)


def final_norm(k, weight):
    nc = k.nc
    N = k.norm_sems("final")
    y_ready, stored = k.sems("final", "y", "stored")
    y, = k.work(k.H0, 32768, y=[P, KT, T])

    with nc.Block() as block:
        @block.sync
        def _(sp):
            for i in range(KT):
                sp.wait_ge(y_ready, i + 1)
                sp.dma_start(k.outT[:, i, :], y[:, i, :]).then_inc(stored, 16)
            sp.wait_ge(stored, 16 * KT)

        @block.gpsimd
        def _(pool):
            k.clear_before(pool)

        @block.tensor
        def _(pe):
            k.norm_mean(N)

        @block.scalar
        def _(act):
            k.norm_rstd(act, N)
            for i in range(KT):
                act.wait_ge(N[3], i + 1)
                nc.scalar.activation(y[:, i, :], k.xr[:, i % 2, :], ACT.Copy, scale=weight[:, i:i + 1]).then_inc(y_ready, 1)

        @block.vector
        def _(dve):
            dve.wait_ge(N[2], 1)
            for i in range(KT):
                if i >= 2:
                    dve.wait_ge(y_ready, i - 1)
                nc.vector.tensor_tensor(k.xr[:, i % 2, :], k.x[:, i, :], k.rs[:, :], ALU.mult).then_inc(N[3], 1)


class Finish:

    def __init__(self, k, name, gate_tile, mlstm=False):
        self.k, self.mlstm = k, mlstm
        self.o = k.m[:, TV:TV + 4, :]
        self.y = k.m[:, gate_tile:gate_tile + 4, :]
        self.sq, = k.work(k.M0, 8192, sq=[P, 2, NCH, DH])
        self.sq_ready, self.reduced, self.fac_ready, self.scaled, self.turned, self.stored, self.chain, self.ln = k.sems(
            name, "sq", "reduced", "factor", "scaled", "turned", "stored", "chain", "ln")

    def scalar(self, act):
        k, nc, ss, fac = self.k, self.k.nc, self.k.small[:, 3, :], self.k.small[:, 4, :]
        for h in range(4):
            if h >= 2:
                act.wait_ge(self.reduced, h - 1)
            nc.scalar.activation(self.sq[:, h % 2], self.o[:, h, :].rearrange("p (c n) -> p c n", c=NCH), ACT.Square).then_inc(self.sq_ready, 1)
        if self.mlstm:
            act.wait_ge(self.chain, 5)
        else:
            act.wait_ge(self.reduced, 4)
        nc.scalar.activation(fac, ss, ACT.Ln, bias=k.col("eps"), scale=1.0 / DH).then_inc(self.ln, 1)
        act.wait_ge(self.ln, 1)
        nc.scalar.activation(fac, fac, ACT.Exp, scale=-0.5).then_inc(self.fac_ready, 1)

    def vector(self, dve):
        k, nc, o = self.k, self.k.nc, self.o
        ss, fac, r = k.small[:, 3, :], k.small[:, 4, :], k.small[:, 5, :]
        den, em = k.small[:, 1, :], k.small[:, 2, :]
        step = [0]

        def link(ins):
            ins.then_inc(self.chain, 1)
            step[0] += 1
            dve.wait_ge(self.chain, step[0])
        for h in range(4):
            dve.wait_ge(self.sq_ready, h + 1)
            nc.vector.tensor_reduce(ss[:, h * NCH:(h + 1) * NCH], self.sq[:, h % 2], axis=AX.X, op=ALU.add).then_inc(self.reduced, 1)
        dve.wait_ge(self.reduced, 4)
        if self.mlstm:
            link(nc.vector.scalar_tensor_tensor(den, den, -1.0, den, ALU.mult, ALU.max))
            link(nc.vector.tensor_tensor(r.rearrange("p (h c) -> p c h", h=4), den.rearrange("p (c h) -> p c h", h=4),
                                         em.rearrange("p (c h) -> p c h", h=4), ALU.max))
            link(nc.vector.reciprocal(r, r))
            link(nc.vector.tensor_tensor(ss, ss, r, ALU.mult))
            link(nc.vector.tensor_tensor(ss, ss, r, ALU.mult))
        dve.wait_ge(self.fac_ready, 1)
        if self.mlstm:
            link(nc.vector.tensor_tensor(fac, fac, r, ALU.mult))
        for h in range(4):
            oh = o[:, h, :].rearrange("p (c n) -> p c n", c=NCH)
            f = fac[:, h * NCH:(h + 1) * NCH].rearrange("p (c n) -> p c n", n=1).to_broadcast([P, NCH, DH])
            nc.vector.tensor_tensor(oh, oh, f, ALU.mult).then_inc(self.scaled, 1)
            if h:
                self.gated(dve, h - 1)
        self.gated(dve, 3)

    def gated(self, dve, h):
        for g in range(2):
            dve.wait_ge(self.turned, 2 * h + g + 1)
            yh = self.y[:, h, g * HALF:(g + 1) * HALF]
            self.k.nc.vector.tensor_tensor(yh, self.k.bank(4 + (2 * h + g) % 4), yh, ALU.mult).then_inc(self.stored, 1)

    def tensor(self, pe):
        k = self.k
        for n in range(8):
            h, g = n // 2, n % 2
            pe.wait_ge(self.scaled, h + 1)
            if n >= 4:
                pe.wait_ge(self.stored, n - 3)
            for c in range(4):
                at = g * HALF + c * P
                mm = k.nc.tensor.transpose(k.bank(4 + n % 4)[:, c * P:(c + 1) * P], self.o[:, h, at:at + P], k.ident[:, :])
            mm.then_inc(self.turned, 1)


def project(k, name, n_units, segments, gate_rows=None, f_tile=None, norm=None, spill=False, rest_of_ada=False, rstd_before=False, finish=None):
    nc = k.nc
    S = k.stream_sems(name)
    done = S[4]
    free, conv_read, tap_done, conv_done, negated = k.sems(
        name, "psum_free", "conv_read", "tap_done", "conv_done", "negated")
    N = k.norm_sems(name) if norm else None
    spilled, ada_in0, ada_in1, ada_read, ada_prod, ada_done = k.sems(name, "x_spilled", "ada_in0", "ada_in1", "ada_read", "ada_prod", "ada_done")
    c_in, c_ready = k.sems(name, "c_in", "silu_c")
    rows_f, chain = k.sems(name, "row_act", "chain")
    fin = Finish(k, *finish) if finish else None
    rotary = any(kind == "rotary" for kind, *_ in segments)
    turn_in, swapped, with_sin, with_cos, rotated = k.sems(name, "cos_sin_in", "swapped", "with_sin", "with_cos", "rotated")
    cos, sin, other, a_cos = k.work(k.X0, 20480, cos=[P, T], sin=[P, T], other=[P, 2, T], a_cos=[P, T]) if rotary else [None] * 4
    lf, reset = k.work(k.X0 + 16384, 8192, lf=[4, T], reset=[4, T])
    silu_c = k.m[:, TGB, :]
    ada_in = (ada_in0, ada_in1)
    ada_w = (k.x[:, 4:8, :], k.m[:, TV:TV + 4, :])
    pbuf, cbuf = k.work(k.X0, 16384, p=[P, 2, T], cv=[P, 2, T]) if name.endswith("A") else (None, None)
    first = k.unit

    with nc.Block() as block:
        @block.sync
        def _(sp):
            if spill:
                sp.dma_start(k.x_spill, flat(k.x[:, :, :])).then_inc(spilled, 16)

            if rest_of_ada:
                sp.dma_start(silu_c, k.c_rows).then_inc(c_in, 16)

            if rotary:
                for buf, table in ((cos, "cos"), (sin, "sin")):
                    at, n = TAB[table]
                    sp.dma_start(buf[:, :], k.tables[:, at:at + n]).then_inc(turn_in, 16)

            def ada_load(j, slot):
                if slot == 1:
                    sp.wait_ge(fin.turned, 8)
                sp.wait_ge(ada_read, j - 1)
                sp.dma_start(ada_w[slot].rearrange("p a n -> p (a n)"),
                             k.w_ada[bass.ds(j + 2, 1)].rearrange("z p a n -> p (z a n)")).then_inc(ada_in[slot], 16)
            k.load_units(sp, S, n_units, ada_load if rest_of_ada else None)
            if spill:
                sp.wait_ge(spilled, 16)

        @block.gpsimd
        def _(pool):
            k.clear_before(pool)
            k.split_units(pool, S, n_units)

        @block.tensor
        def _(pe):
            if norm:
                if not rstd_before:
                    k.norm_mean(N)
                k.multiply_first(first, N[5], S[3], done)

            def unit(j, slot, turn):
                pe.wait_ge(S[3], j + 1)
                pe.wait_ge(free, j + 1)
                k.multiply((first + slot) % 2, slot, k.hh, k.hl).then_inc(done, 1)
            if fin:
                unit(0, 0, 0)
                fin.tensor(pe)
                unit(1, 1, 0)
            in_pairs(pe, 2 if norm or fin else 0, n_units, unit)

        @block.scalar
        def _(act):
            if norm:
                k.norm_act(act, N, *norm, rstd_before)
            if fin:
                fin.scalar(act)
            if rest_of_ada:
                act.wait_ge(c_in, 16)
                nc.scalar.activation(silu_c, silu_c, ACT.Silu).then_inc(c_ready, 1)
            act.sem_inc(free, 2)
            act.sem_inc(conv_read, 2)
            at = 0
            for kind, tile, bias, weight, n in segments:
                def unit(j, slot, turn, kind=kind, tile=tile, bias=bias, at=at):
                    ps = k.pair((at + slot) % 2)
                    act.wait_ge(done, j + (at + 1))
                    dst = flat(k.m[:, bass.ds(j + tile, 1), :])
                    b = k.col(bias[0], j + bias[1])
                    if kind == "conv":
                        nc.scalar.activation(pbuf[:, slot, :], ps, ACT.Identity, bias=b).then_inc(free, 1)
                        act.wait_ge(conv_done, j + 1)
                        nc.scalar.activation(dst, cbuf[:, slot, :], ACT.Silu).then_inc(conv_read, 1)
                    elif kind == "copy":
                        nc.scalar.activation(dst, ps, ACT.Identity, bias=b).then_inc(free, 1)
                    elif kind == "rotary":
                        nc.scalar.activation(dst, ps, ACT.Identity, bias=b).then_inc(free, 1)
                        act.wait_ge(free, j + (at + 3))
                        act.wait_ge(rotated, j + 1)
                        lower, upper = (flat(k.m[rows, bass.ds(j + tile, 1), :]) for rows in (slice(0, DH // 2), slice(DH // 2, DH)))
                        nc.scalar.activation(other[0:DH // 2, slot, :], upper, ACT.Copy)
                        nc.scalar.activation(other[DH // 2:DH, slot, :], lower, ACT.Copy).then_inc(swapped, 1)
                    elif kind == "silu":
                        nc.scalar.activation(dst, ps, ACT.Silu, bias=b).then_inc(free, 1)
                    elif kind == "gate_sigmoid":
                        nc.scalar.activation(dst, ps, ACT.Sigmoid, bias=b).then_inc(free, 1)
                    elif kind == "gate_silu":
                        nc.scalar.activation(dst, ps, ACT.Silu, bias=b).then_inc(free, 1)
                    elif kind == "forget":
                        nc.scalar.activation(flat(f_tile[:, bass.ds(j, 1), :]), ps, ACT.Sigmoid, bias=b)
                        nc.scalar.activation(dst, ps, ACT.Sigmoid, scale=-1.0,
                                             bias=k.small[:, 0, bass.ds(j, 1)]).then_inc(free, 1)
                if kind == "rows":
                    act.wait_ge(done, at + 1)
                    ps = k.pair(at % 2)
                    g0 = COL["b_gate"]
                    nc.scalar.activation(gate_rows[0], ps[0:4, :], ACT.Identity, bias=k.par[0:4, g0:g0 + 1])
                    nc.scalar.activation(gate_rows[1], ps[32:36, :], ACT.Identity, bias=k.par[32:36, g0:g0 + 1]).then_inc(free, 1)
                    act.wait_ge(chain, 3)
                    nc.scalar.activation(lf[:, :], gate_rows[1], ACT.Abs).then_inc(rows_f, 1)
                    act.wait_ge(rows_f, 1)
                    nc.scalar.activation(lf[:, :], lf[:, :], ACT.Exp, scale=-1.0).then_inc(rows_f, 1)
                    act.wait_ge(rows_f, 2)
                    nc.scalar.activation(lf[:, :], lf[:, :], ACT.Ln, bias=1.0).then_inc(rows_f, 1)
                else:
                    if kind == "forget":
                        act.wait_ge(negated, 1)
                    if tile in (TGB, TV) and rest_of_ada:
                        act.wait_ge(ada_read, 10)
                    in_pairs(act, 0, n, unit)
                at += n

        @block.vector
        def _(dve):
            if norm:
                k.norm_dve(dve, N, rstd_before)
            if fin:
                fin.vector(dve)
                dve.wait_ge(fin.stored, 8)
            for kind, tile, bias, weight, n in segments:
                if kind == "forget":
                    b0 = COL[bias[0]] + bias[1]
                    nc.vector.tensor_scalar(k.small[:, 0, 0:4], k.par[:, b0:b0 + 4], -1.0, None, ALU.mult).then_inc(negated, 1)
            if rest_of_ada:
                dve.wait_ge(c_ready, 1)
                dve.sem_inc(ada_read, 2)
                dve.sem_inc(ada_prod, 2)
                with dve.Fori(0, 4) as i:
                    for slot in range(2):
                        dve.wait_ge(ada_in[slot], i * 16 + 16)
                        for a in range(4):
                            n = i * 8 + (4 * slot + a)
                            dve.wait_ge(ada_prod, n + 1)
                            ada_tile(k, k.pair(2 + a % 2), ada_w[slot][:, a, :], silu_c, k.mod[:, 1, bass.ds(n + 16, 1)]).then_inc(ada_prod, 1)
                        dve.wait_ge(ada_prod, i * 8 + (4 * slot + 6))
                        dve.sem_inc(ada_read, 1)
                for layer in range(2):
                    b = COL["b_ada"] + 48 * layer
                    nc.vector.tensor_tensor(k.mod[:, layer, 16:48], k.mod[:, 1, 16:48], k.par[:, b + 16:b + 48], ALU.add).then_inc(ada_done, 1)
                    dve.wait_ge(ada_done, layer * 2 + 1)
                    w = k.par[:, COL["norm_ffn"] + 8 * layer:COL["norm_ffn"] + 8 * layer + 8]
                    nc.vector.scalar_tensor_tensor(k.modA[:, 2 * layer + 1, :], k.mod[:, layer, 32:40], 1.0, w, ALU.add, ALU.mult).then_inc(ada_done, 1)
                    dve.wait_ge(ada_done, layer * 2 + 2)
            at = 0
            for kind, tile, bias, weight, n in segments:
                if kind == "conv":
                    def conv(j, slot, turn):
                        c = cbuf[:, slot, :]
                        dve.wait_ge(free, j + 3)
                        dve.wait_ge(conv_read, j + 1)
                        nc.vector.tensor_scalar(c, pbuf[:, slot, :], k.col("conv_qk_w", j + 8 * (CONV_A - 1)),
                                                k.col("conv_qk_b", j), ALU.mult, ALU.add).then_inc(tap_done, 1)
                        for lag in range(1, CONV_A):
                            dve.wait_ge(tap_done, j * (CONV_A - 1) + lag)
                            nc.vector.scalar_tensor_tensor(
                                cbuf[:, slot, lag:T], pbuf[:, slot, 0:T - lag], k.col("conv_qk_w", j + 8 * (CONV_A - 1 - lag)),
                                cbuf[:, slot, lag:T], ALU.mult, ALU.add).then_inc(conv_done if lag == CONV_A - 1 else tap_done, 1)
                    in_pairs(dve, 0, n, conv)
                elif kind == "rows":
                    i_row, F_row, m_row, G_row = gate_rows
                    step = [0]

                    def link(ins):
                        ins.then_inc(chain, 1)
                        step[0] += 1
                        dve.wait_ge(chain, step[0])
                    fb = COL["f_bias"]
                    link(nc.vector.memset(reset[:, :], 1.0))
                    link(nc.vector.memset(reset[:, 0:T:CH], 0.0))
                    dve.wait_ge(free, at + 3)
                    link(nc.vector.tensor_scalar(F_row, F_row, k.par[0:4, fb:fb + 1], None, ALU.add))
                    dve.wait_ge(rows_f, 3)
                    link(nc.vector.scalar_tensor_tensor(lf[:, :], F_row, 0.0, lf[:, :], ALU.min, ALU.subtract))
                    link(nc.vector.tensor_tensor_scan(m_row, lf[:, :], i_row, 0.0, ALU.add, ALU.max))
                    link(nc.vector.tensor_tensor_scan(F_row, reset[:, :], lf[:, :], 0.0, ALU.mult, ALU.add))
                    link(nc.vector.tensor_tensor(i_row, i_row, F_row, ALU.subtract))
                    link(nc.vector.tensor_tensor(G_row, F_row, m_row, ALU.subtract))
                elif kind == "rotary":
                    def turn_pair(j, slot, turn, tile=tile):
                        x = flat(k.m[:, bass.ds(j + tile, 1), :])
                        dve.wait_ge(swapped, j + 1)
                        nc.vector.tensor_tensor(other[:, slot, :], other[:, slot, :], sin[:, :], ALU.mult).then_inc(with_sin, 1)
                        dve.wait_ge(rotated, j + 2)
                        nc.vector.tensor_tensor(a_cos[:, :], x, cos[:, :], ALU.mult).then_inc(with_cos, 1)
                        dve.wait_ge(with_sin, j + 1)
                        dve.wait_ge(with_cos, j + 1)
                        nc.vector.tensor_tensor(x, a_cos[:, :], other[:, slot, :], ALU.add).then_inc(rotated, 1)
                    dve.sem_inc(rotated, 2)
                    dve.wait_ge(turn_in, 32)
                    in_pairs(dve, 0, n, turn_pair)
                elif kind in ("gate_sigmoid", "gate_silu"):
                    def gate(j, slot, turn, tile=tile, weight=weight, at=at):
                        dst = flat(k.m[:, bass.ds(j + tile, 1), :])
                        dve.wait_ge(free, j + (at + 3))
                        nc.vector.tensor_scalar(dst, dst, k.col(weight, j), None, ALU.mult)
                    in_pairs(dve, 0, n, gate)
                elif kind == "forget":
                    def forget(j, slot, turn, tile=tile, at=at):
                        f = flat(f_tile[:, bass.ds(j, 1), :])
                        dst = flat(k.m[:, bass.ds(j + tile, 1), :])
                        dve.wait_ge(free, j + (at + 3))
                        nc.vector.tensor_scalar(f, f, k.lb[:, 1, bass.ds(j, 1)], k.lb[:, 0, bass.ds(j, 1)], ALU.mult, ALU.add)
                        nc.vector.tensor_scalar(dst, dst, k.lb[:, 1, bass.ds(j, 1)], None, ALU.mult)
                    in_pairs(dve, 0, n, forget)
                at += n
    k.unit += n_units


def out_project(k, name, layer, finish, order):
    nc = k.nc
    S = k.stream_sems(name)
    done = S[4]
    free, hi_done, y_split, x_in = k.sems(name, "psum_free", "y_hi", "y_split", "x_back")
    Q = k.square_sems(name)
    fin = Finish(k, *finish)
    x_home = k.xT if layer == 0 else k.x_spill
    first = k.unit
    gate = k.mod[:, layer, 16:24]

    with nc.Block() as block:
        @block.sync
        def _(sp):
            sp.dma_start(flat(k.x[:, :, :]), x_home).then_inc(x_in, 16)
            k.load_units(sp, S, N_OUT)

        @block.gpsimd
        def _(pool):
            k.clear_before(pool)
            k.split_units(pool, S, N_OUT)

        @block.scalar
        def _(act):
            for n, i in enumerate(order):
                if n == 4:
                    fin.scalar(act)
                if n >= 4:
                    act.wait_ge(fin.stored, 2 * (n - 4) + 2)
                nc.scalar.activation(k.hh[:, i, :], k.m[:, TGA + i, :], ACT.Copy).then_inc(hi_done, 1)
            act.wait_ge(y_split, KT)

            def unit(j, slot, turn):
                act.wait_ge(free, j + 3)
                x = k.x[:, j, :] if isinstance(j, int) else flat(k.x[:, bass.ds(j, 1), :])
                k.square(act, Q, j, (x, slot))
            unit(0, 0, 0)
            unit(1, 1, 0)
            in_pairs(act, 2, N_OUT, unit)

        @block.tensor
        def _(pe):
            k.multiply_first(first, y_split, S[3], done, order, lambda: fin.tensor(pe))

            def unit(j, slot, turn):
                pe.wait_ge(S[3], j + 1)
                pe.wait_ge(free, j + 1)
                k.multiply((first + slot) % 2, slot, k.hh, k.hl).then_inc(done, 1)
            in_pairs(pe, 2, N_OUT, unit)

        @block.vector
        def _(dve):
            dve.sem_inc(free, 2)
            k.credit(dve, Q[1])
            for n, i in enumerate(order):
                if n == 4:
                    fin.vector(dve)
                dve.wait_ge(hi_done, n + 1)
                nc.vector.tensor_tensor(k.hl[:, i, :], k.m[:, TGA + i, :], k.hh[:, i, :].bitcast(F32),
                                        ALU.subtract).then_inc(y_split, 1)
            dve.wait_ge(x_in, 16)

            def unit(j, slot, turn):
                x = flat(k.x[:, bass.ds(j, 1), :])
                dve.wait_ge(done, j + 1)
                nc.vector.scalar_tensor_tensor(x, k.pair(slot), gate[:, bass.ds(j, 1)], x, ALU.mult, ALU.add).then_inc(free, 1)
                k.add_square(dve, Q, j, slot)
            dve.wait_ge(done, 1)
            nc.vector.scalar_tensor_tensor(k.x[:, 0, :], k.pair(0), gate[:, 0:1], k.x[:, 0, :], ALU.mult, ALU.add).then_inc(free, 1)
            dve.wait_ge(done, 2)
            nc.vector.scalar_tensor_tensor(k.x[:, 1, :], k.pair(1), gate[:, 1:2], k.x[:, 1, :], ALU.mult, ALU.add).then_inc(free, 1)
            k.add_square(dve, Q, 1, 1)
            in_pairs(dve, 2, N_OUT, unit)
    k.unit += N_OUT


def ffn(k, name, layer, norm):
    nc = k.nc
    S = k.stream_sems(name)
    done = S[4]
    newest, tap1, tap_done, silu_done, prod, hi_done, split_done, down_done, down_free = k.sems(
        name, "newest_tap", "tap1", "taps_done", "silu_done", "product", "a_hi", "a_split", "down_done", "down_free")
    N, Q = k.norm_sems(name), k.square_sems(name)
    a_hi, a_lo, conv, sg = k.work(k.M0, 14 * T * 4, a_hi=([P, 2, 2, T], F32R), a_lo=([P, 2, 2, T], F32R),
                                  cv=[P, 4, T], sg=[P, 2, T])
    first = k.unit
    gate = k.mod[:, layer, 40:48]

    def cols(kind, g, u):
        tile = g * 2 + (u // 2 + (u % 2) * FFT)
        if kind == 3:
            return k.col("ffn_b", tile + 2 * FFT * layer)
        at = kind * 2 * FFT + FFN_CONV * 2 * FFT * layer
        return k.col("ffn_w0", tile + at)

    with nc.Block() as block:
        @block.sync
        def _(sp):
            k.load_units(sp, S, N_FFN)

        @block.gpsimd
        def _(pool):
            k.clear_before(pool)
            k.split_units(pool, S, N_FFN)

        @block.tensor
        def _(pe):
            def up(g, unit0, units=range(4)):
                for u in units:
                    pe.wait_ge(S[3], unit0 + (u + 1))
                    pe.wait_ge(tap_done, g * 4 + (u + 1))
                    k.multiply((first + u) % 2, u % 2, k.hh, k.hl).then_inc(done, 1)

            def down(g, parity, unit0):
                pe.wait_ge(split_done, g * 2 + 2)
                for u in range(2):
                    place = (first + u) % 2
                    pe.wait_ge(S[3], unit0 + (u + 1))
                    for o in range(4):
                        pe.wait_ge(down_free, g * 8 + (4 * u + o + 1))
                        for kk in range(2):
                            w_hi = k.w_hi[:, place, kk * HALF + o * P:kk * HALF + (o + 1) * P]
                            w_lo = k.w_lo[:, place, kk * HALF + o * P:kk * HALF + (o + 1) * P]
                            for n, (w, r) in enumerate(((w_hi, a_hi), (w_hi, a_lo), (w_lo, a_hi))):
                                for half in range(2):
                                    mm = nc.tensor.matmul(k.bank(4 + 2 * (o % 2) + half), w,
                                                          r[:, parity, kk, half * HALF:(half + 1) * HALF],
                                                          start=(kk == 0 and n == 0), stop=(kk == 1 and n == 2))
                        mm.then_inc(done if o == 3 else down_done, 1)

            k.norm_mean(N)
            k.multiply_first(first, N[5], S[3], done)
            up(0, 0, (2, 3))
            with pe.Fori(0, (GROUPS - 1) // 2) as i:
                for v in range(2):
                    g = i * 2 + (1 + v)
                    up(g, i * 12 + (6 * v + 4))
                    down(i * 2 + v, v, i * 12 + (6 * v + 8))
            down(GROUPS - 1, (GROUPS - 1) % 2, N_FFN - 2)

        @block.scalar
        def _(act):
            def group(g, parity, unit0):
                for u in range(4):
                    act.wait_ge(done, unit0 + (u + 1))
                    act.wait_ge(split_done, g * 2)
                    nc.scalar.activation(conv[:, u, :], k.pair(u % 2), ACT.Identity, bias=cols(3, g, u),
                                         scale=cols(2, g, u)).then_inc(newest, 1)
                    if u % 2:
                        act.wait_ge(tap_done, g * 4 + (u + 3))
                        nc.scalar.activation(sg[:, u // 2, :], conv[:, u, :], ACT.Silu).then_inc(silu_done, 1)
                        act.wait_ge(prod, g * 2 + (u // 2 + 1))
                        nc.scalar.activation(a_hi[:, parity, u // 2, :], conv[:, u - 1, :], ACT.Copy).then_inc(hi_done, 1)

            k.norm_act(act, N, *norm)
            group(0, 0, 0)
            with act.Fori(0, (GROUPS - 1) // 2) as i:
                for v in range(2):
                    group(i * 2 + (1 + v), (1 + v) % 2, i * 12 + (6 * v + 4))
            for o in range(KT):
                act.wait_ge(down_free, 2 + (GROUPS - 1) * KT + o + 1)
                k.square(act, Q, o, (k.x[:, o, :], o % 2))

        @block.vector
        def _(dve):
            def up(g, parity, down=None):
                for u in range(4):
                    ps = k.pair(u % 2)
                    dve.wait_ge(newest, g * 4 + (u + 1))
                    nc.vector.scalar_tensor_tensor(conv[:, u, 1:T], ps[:, 0:T - 1], cols(1, g, u), conv[:, u, 1:T],
                                                   ALU.mult, ALU.add).then_inc(tap1, 1)
                    dve.wait_ge(tap1, g * 4 + (u + 1))
                    nc.vector.scalar_tensor_tensor(conv[:, u, 2:T], ps[:, 0:T - 2], cols(0, g, u), conv[:, u, 2:T],
                                                   ALU.mult, ALU.add).then_inc(tap_done, 1)
                    if u % 2:
                        if down and u == 3:
                            down(0)
                        dve.wait_ge(silu_done, g * 2 + (u // 2 + 1))
                        nc.vector.tensor_tensor(conv[:, u - 1, :], conv[:, u - 1, :], sg[:, u // 2, :],
                                                ALU.mult).then_inc(prod, 1)
                        if down and u == 3:
                            down(1)
                        dve.wait_ge(hi_done, g * 2 + (u // 2 + 1))
                        nc.vector.tensor_tensor(a_lo[:, parity, u // 2, :], conv[:, u - 1, :],
                                                a_hi[:, parity, u // 2, :].bitcast(F32), ALU.subtract).then_inc(split_done, 1)

            def add_down(g, unit0, o):
                if o % 4 == 3:
                    dve.wait_ge(done, unit0 + (o // 4 + 1))
                else:
                    dve.wait_ge(down_done, g * 6 + (o // 4 * 3 + o % 4 + 1))
                nc.vector.scalar_tensor_tensor(k.x[:, o, :], k.pair(2 + o % 2), gate[:, o:o + 1], k.x[:, o, :],
                                               ALU.mult, ALU.add).then_inc(down_free, 1)
            k.norm_dve(dve, N)
            k.credit(dve, Q[1])
            dve.sem_inc(tap_done, 2)
            dve.sem_inc(down_free, 2)
            up(0, 0)
            with dve.Fori(0, (GROUPS - 1) // 2) as i:
                for v in range(2):
                    def down(o, v=v):
                        add_down(i * 2 + v, i * 12 + (6 * v + 8), o)
                    up(i * 2 + (1 + v), (1 + v) % 2, down)
                    for o in range(2, KT):
                        down(o)
            for o in range(KT):
                add_down(GROUPS - 1, N_FFN - 2, o)
                if o >= 2:
                    k.add_square(dve, Q, o - 1, (o - 1) % 2)
            k.add_square(dve, Q, KT - 1, (KT - 1) % 2)
    k.unit += N_FFN


def chunk(ap4, c):
    return ap4[:, :, bass.ds(c * CH, CH)]


def mix_a(k):
    nc = k.nc
    q, kk, v = k.m[:, TQ:TQ + 4, :], k.m[:, TK:TK + 4, :], k.m[:, TV:TV + 4, :]
    rows = k.m[0:4, TGB:TGB + 4, :]
    (k_st, v_st, vaug, pr, qs, kw, dx, wi, state, sel, causal, acol, m_prev) = k.work(
        k.X0, 32768, k_st=[P, 4, CH], v_st=[P, 4, CH], vaug=[P, 4, DH + 1], pr=[P, 4, CH], qs=[P, 4, CH],
        kw=[P, 4, DH], dx=[P, 4, CH], wi=[P, 4, CH], state=[P, 4, DH + 1], sel=[4, 4, P], causal=[P, CH],
        acol=[P, NCH, 4], mprev=[P, 4, NCH])
    (tab_in, m_zero, cols_mm, cols_done, zeroed) = k.sems("a_cols", "tables_in", "m_zero", "cols_mm", "cols", "zeroed")
    (v_staged, vaug_ready, d_ready, wi_ready, o_stored, k_staged, x_ready, qs_ready, p_ready, kw_ready,
     st_done, g_done, tv_done, s_done, tk_done, num_done, st_mm) = k.sems(
        "a", "v_staged", "vaug", "d_ready", "wi_ready", "o_stored", "k_staged", "x_ready", "qs_ready", "p_ready",
        "kw_ready", "state_done", "g_rows", "v_turned", "scores", "k_turned", "numerator", "state_mm")
    den, em = k.small[:, 1, :], k.small[:, 2, :]
    i_row, m_row, G_row = rows[:, 0, :], rows[:, 2, :], rows[:, 3, :]
    bG, bS, bV, bK = 0, 1, 2, 3
    num = k.psum[:, 4:6, :].rearrange("p a (b n) -> p (a b) n", b=2)
    st = k.psum[:, 6:8, :].rearrange("p a (b n) -> p (a b) n", b=2)

    def heads(b):
        return k.psum[:, b, :].rearrange("p (h n) -> p h n", h=4)

    with nc.Block() as block:
        @block.sync
        def _(sp):
            a, n = TAB["sel"]
            sp.dma_start(sel[:, :, :].rearrange("p a n -> p (a n)"), k.tables[0:4, a:a + n]).then_inc(tab_in, 16)
            a, n = TAB["causal"]
            sp.dma_start(causal[:, :], k.tables[:, a:a + n]).then_inc(tab_in, 16)
            sp.wait_ge(tab_in, 32)

        @block.gpsimd
        def _(pool):
            k.clear_before(pool)
            pool.memset(state[:, :, :], 0.0).then_inc(zeroed, 1)
            pool.memset(vaug[:, :, DH:DH + 1], 1.0).then_inc(zeroed, 1)

        @block.scalar
        def _(act):
            k.credit(act, v_staged, vaug_ready, d_ready, wi_ready, o_stored)
            act.wait_ge(cols_mm, 1)
            act.wait_ge(m_zero, 1)
            nc.scalar.activation(em, k.psum[:, 1, 0:32], ACT.Exp, scale=-1.0)
            nc.scalar.activation(m_prev[:, :, 1:NCH], k.psum[:, 2, 0:32].rearrange("p (h c) -> p h c", h=4)[:, :, 0:NCH - 1],
                                 ACT.Copy).then_inc(cols_done, 1)

            def store(c):
                act.wait_ge(num_done, c + 2)
                nc.scalar.activation(den[:, bass.ds(c * 4, 4)], num[:, :, DH:DH + 1].rearrange("p h a -> p (h a)"), ACT.Copy)
                nc.scalar.activation(chunk(v, c), num[:, :, 0:DH], ACT.Copy).then_inc(o_stored, 1)

            def step(c, before):
                act.wait_ge(tv_done, c + 1)
                nc.scalar.activation(v_st[:, :, :], chunk(v, c), ACT.Copy).then_inc(v_staged, 1)
                act.wait_ge(x_ready, c + 2)
                nc.scalar.activation(dx[:, :, :], dx[:, :, :], ACT.Exp).then_inc(d_ready, 1)
                if before is not None:
                    store(before)
                act.wait_ge(tv_done, c + 2)
                act.wait_ge(st_mm, c + 1)
                nc.scalar.activation(vaug[:, :, 0:DH], heads(bV), ACT.Copy).then_inc(vaug_ready, 1)
                act.wait_ge(st_done, c + 1)
                act.wait_ge(g_done, c + 2)
                for h in range(4):
                    ins = nc.scalar.activation(wi[:, h, :], heads(bG)[:, h, :], ACT.Exp, bias=m_prev[:, h, bass.ds(c, 1)])
                ins.then_inc(wi_ready, 1)

            step(0, None)
            with act.Fori(0, NCH - 1) as i:
                step(i + 1, i)
            store(NCH - 1)

        @block.vector
        def _(dve):
            k.credit(dve, k_staged, x_ready, qs_ready, p_ready, kw_ready, st_done)
            nc.vector.memset(m_prev[:, :, :], 0.0).then_inc(m_zero, 1)
            dve.wait_ge(cols_mm, 1)
            nc.vector.tensor_copy(acol[:, :, :], k.psum[:, 0, 0:32].rearrange("p (c h) -> p c h", h=4)).then_inc(cols_done, 1)
            dve.wait_ge(cols_done, 2)
            dve.wait_ge(zeroed, 2)
            dve.wait_ge(tab_in, 32)

            def state_after(c):
                dve.wait_ge(num_done, c + 2)
                dve.wait_ge(st_mm, c + 2)
                for h in range(4):
                    ins = nc.vector.scalar_tensor_tensor(state[:, h, :], state[:, h, :], wi[:, h, CH - 1:CH], st[:, h, 0:DH + 1],
                                                         ALU.mult, ALU.add)
                ins.then_inc(st_done, 1)

            def step(c, before):
                dve.wait_ge(s_done, c + 1)
                dve.wait_ge(tk_done, c + 1)
                nc.vector.tensor_copy(k_st[:, :, :], chunk(kk, c)).then_inc(k_staged, 1)
                dve.wait_ge(g_done, c + 2)
                dve.wait_ge(kw_ready, c + 1)
                for h in range(4):
                    ins = nc.vector.scalar_tensor_tensor(dx[:, h, :], heads(bG)[:, h, :], acol[:, bass.ds(c, 1), h:h + 1].rearrange("p a n -> p (a n)"),
                                                         causal[:, :], ALU.add, ALU.add)
                ins.then_inc(x_ready, 1)
                if before is not None:
                    state_after(before)
                dve.wait_ge(wi_ready, c + 2)
                dve.wait_ge(num_done, c + 1)
                nc.vector.scalar_tensor_tensor(qs[:, :, :], chunk(q, c), SCALE_A, wi[:, :, :], ALU.mult, ALU.mult).then_inc(qs_ready, 1)
                dve.wait_ge(d_ready, c + 2)
                dve.wait_ge(s_done, c + 2)
                nc.vector.scalar_tensor_tensor(pr[:, :, :], heads(bS), SCALE_A, dx[:, :, :], ALU.mult, ALU.mult).then_inc(p_ready, 1)
                dve.wait_ge(tk_done, c + 2)
                dve.wait_ge(st_mm, c + 1)
                nc.vector.tensor_tensor(kw[:, :, :], heads(bK), dx[:, :, CH - 1:CH].to_broadcast([P, 4, DH]), ALU.mult).then_inc(kw_ready, 1)

            step(0, None)
            with dve.Fori(0, NCH - 1) as i:
                step(i + 1, i)
            state_after(NCH - 1)

        @block.tensor
        def _(pe):
            k.credit(pe, g_done, tv_done, s_done, tk_done, num_done, st_mm)
            pe.wait_ge(tab_in, 32)
            for c in range(NCH):
                nc.tensor.matmul(k.psum[:, 0, 4 * c:4 * c + 4], i_row[:, c * CH:(c + 1) * CH], k.ident[0:4, 0:4], start=True, stop=True)
                nc.tensor.matmul(k.psum[:, 1, 4 * c:4 * c + 4], m_row[:, c * CH:(c + 1) * CH], k.ident[0:4, 0:4], start=True, stop=True)
            for h in range(4):
                mm = nc.tensor.matmul(k.psum[:, 2, NCH * h:NCH * (h + 1)], sel[:, h, :], m_row[:, CH - 1:T:CH], start=True, stop=True)
            mm.then_inc(cols_mm, 1)
            pe.wait_ge(cols_done, 2)
            pe.wait_ge(zeroed, 2)

            def gates(c):
                pe.wait_ge(x_ready, c + 1)
                pe.wait_ge(wi_ready, c + 1)
                for h in range(4):
                    mm = nc.tensor.matmul(heads(bG)[:, h, :], sel[:, h, :], G_row[:, bass.ds(c * CH, CH)], start=True, stop=True)
                mm.then_inc(g_done, 1)

            def step(c, after):
                pe.wait_ge(v_staged, c + 2)
                pe.wait_ge(vaug_ready, c + 1)
                for h in range(4):
                    mm = nc.tensor.transpose(heads(bV)[:, h, :], v_st[:, h, :], k.ident[:, :])
                mm.then_inc(tv_done, 1)
                pe.wait_ge(k_staged, c + 2)
                pe.wait_ge(p_ready, c + 1)
                for h in range(4):
                    mm = nc.tensor.matmul(heads(bS)[:, h, :], k_st[:, h, :], q[:, h, bass.ds(c * CH, CH)], start=True, stop=True)
                mm.then_inc(s_done, 1)
                pe.wait_ge(kw_ready, c + 1)
                for h in range(4):
                    mm = nc.tensor.transpose(heads(bK)[:, h, :], k_st[:, h, :], k.ident[:, :])
                mm.then_inc(tk_done, 1)
                if after is not None:
                    gates(after)
                pe.wait_ge(vaug_ready, c + 2)
                pe.wait_ge(qs_ready, c + 2)
                pe.wait_ge(p_ready, c + 2)
                pe.wait_ge(st_done, c + 1)
                pe.wait_ge(o_stored, c + 1)
                for h in range(4):
                    nc.tensor.matmul(num[:, h, 0:DH + 1], pr[:, h, :], vaug[:, h, :], start=True, stop=False)
                    mm = nc.tensor.matmul(num[:, h, 0:DH + 1], qs[:, h, :], state[:, h, :], start=False, stop=True)
                mm.then_inc(num_done, 1)
                pe.wait_ge(kw_ready, c + 2)
                for h in range(4):
                    mm = nc.tensor.matmul(st[:, h, 0:DH + 1], kw[:, h, :], vaug[:, h, :], start=True, stop=True)
                mm.then_inc(st_mm, 1)

            gates(0)
            with pe.Fori(0, NCH - 1) as c:
                step(c, c + 1)
            step(NCH - 1, None)


def mix_b(k, f_slot):
    nc = k.nc
    q, kk, v = k.m[:, TQ:TQ + 4, :], k.m[:, TK:TK + 4, :], k.m[:, TV:TV + 4, :]
    NL = len(LEVELS)
    Q, K, B, v_st, v_tok, kw, pr, state, levels, picked, diag = k.work(
        k.H0, 65536, Q=[P, NL + 2, 4, CH], K=[P, NL + 1, 4, CH], B=[P, NL + 1, 2 * CH], v_st=[P, 4, CH], v_tok=[P, 4, DH],
        kw=[P, 4, DH], pr=[P, 4, CH], state=[P, 4, DH], levels=[P, SMALL, 32], picked=[P, SMALL, 4, 32], diag=[P, 4, 32])
    (tab_in, zeroed, v_staged, v_turned, v_ready, base_in, q_lower, q_upper, k_upper, k_lower, blocks, small_mm, big_mm,
     pick, diag_ready, placed, big_stored, k_turned, kw_ready, num_done, o_stored, st_mm, st_done) = k.sems(
        "b", "tables_in", "zeroed", "v_staged", "v_turned", "v_ready", "base_in", "q_lower", "q_upper", "k_upper", "k_lower",
        "blocks", "small_mm", "big_mm", "picked", "diag_ready", "placed", "big_stored", "k_turned", "kw_ready", "num_done",
        "o_stored", "state_mm", "state_done")
    bBig, bV, bK, bN, bC = 2, 3, 4, 5, 6

    def heads(b):
        return k.psum[:, b, :].rearrange("p (h n) -> p h n", h=4)

    def halves(ap, n, L):
        x = ap[:, n].rearrange("p h t -> p (h t)").rearrange("p (b u l) -> p b u l", u=2, l=L)
        return x[:, :, 0, :], x[:, :, 1, :]

    def decays(c, n, L):
        if n == 0:
            f = chunk(f_slot, c).rearrange("p h (b u) -> p h b u", u=2)
            return f[:, :, :, 0:1], f[:, :, :, 1:2]
        x = B[:, n, 0:4 * CH // L].rearrange("p (b u l) -> p b u l", u=2, l=1)
        return x[:, :, 0, :], x[:, :, 1, :]

    def spread(d, n, L):
        return d if n == 0 else d.to_broadcast([P, 2 * CH // L, L])

    def shaped(x, n):
        return x.rearrange("p (h b) l -> p h b l", h=4) if n == 0 else x

    with nc.Block() as block:
        @block.sync
        def _(sp):
            a, n = TAB["levels"]
            sp.dma_start(levels[:, :, :].rearrange("p a n -> p (a n)"), k.tables[:, a:a + n]).then_inc(tab_in, 16)
            sp.wait_ge(tab_in, 16)

        @block.gpsimd
        def _(pool):
            k.clear_before(pool)
            k.credit(pool, k_lower)
            pool.memset(state[:, :, :], 0.0).then_inc(zeroed, 1)
            pool.memset(pr[:, :, :], 0.0).then_inc(zeroed, 1)
            with pool.Fori(0, NCH) as c:
                for n, L in enumerate(LEVELS):
                    if n == 0:
                        pool.wait_ge(base_in, c + 2)
                        pool.wait_ge(k_turned, c + 1)
                    else:
                        pool.wait_ge(k_lower, c * NL + (n + 1))
                        pool.wait_ge(k_upper, c * NL + (n + 1))
                        pool.wait_ge(blocks, c * NL + (n + 1))
                    lo, _ = halves(K, n, L)
                    to, _ = halves(K, n + 1, L)
                    _, d = decays(c, n, L)
                    pool.tensor_tensor(shaped(to, n), shaped(lo, n), spread(d, n, L), ALU.mult).then_inc(k_lower, 1)

        @block.vector
        def _(dve):
            k.credit(dve, q_upper, blocks, pick, diag_ready, big_stored, kw_ready, o_stored, st_done)
            dve.wait_ge(tab_in, 16)
            dve.wait_ge(zeroed, 2)
            def outputs(c):
                dve.wait_ge(num_done, c + 2)
                nc.vector.tensor_scalar(chunk(v, c), heads(bN), 1.0, None, ALU.mult).then_inc(o_stored, 1)
                dve.wait_ge(st_mm, c + 2)
                for h in range(4):
                    ins = nc.vector.scalar_tensor_tensor(state[:, h, :], state[:, h, :], B[:, NL, h:h + 1], heads(bC)[:, h, :],
                                                         ALU.mult, ALU.add)
                ins.then_inc(st_done, 1)

            def step(c, before):
                dve.wait_ge(big_mm, c + 1)
                dve.wait_ge(k_lower, c * NL + 1)
                nc.vector.tensor_tensor(Q[:, 1], chunk(q, c), chunk(f_slot, c), ALU.mult).then_inc(q_upper, 1)
                for n, L in enumerate(LEVELS):
                    if n == 3 and before is not None:
                        outputs(before)
                    dve.wait_ge(q_upper, c * (NL + 1) + (n + 2))
                    if n:
                        dve.wait_ge(q_lower, c * NL + (n + 1))
                        dve.wait_ge(blocks, c * NL + (n + 1))
                    _, up = halves(Q, n + 1, L)
                    _, to = halves(Q, n + 2, L)
                    d, d2 = decays(c, n, L)
                    nc.vector.tensor_tensor(shaped(to, n), shaped(up, n), spread(d, n, L), ALU.mult).then_inc(q_upper, 1)
                    out = B[:, n + 1, 0:2 * CH // L].rearrange("p (b l) -> p b l", l=1)
                    nc.vector.tensor_tensor(shaped(out, n), d, d2, ALU.mult).then_inc(blocks, 1)
                dve.wait_ge(small_mm, c + 2)
                ps = k.psum[:, 0:2, :].rearrange("p a n -> p (a n)")
                for a, b in ((0, 4), (4, SMALL)):
                    ins = nc.vector.tensor_tensor(
                        picked[:, a:b], ps[:, a * 128:b * 128].rearrange("p (l h t) -> p l h t", h=4, t=32),
                        levels[:, a:b].rearrange("p l (h t) -> p l h t", h=1).to_broadcast([P, b - a, 4, 32]), ALU.mult)
                ins.then_inc(pick, 1)
                dve.wait_ge(pick, c + 2)
                dve.wait_ge(placed, c + 1)
                nc.vector.tensor_reduce(diag[:, :, :].rearrange("p h t -> p (h t)"),
                                        picked[:, :, :, :].rearrange("p l h t -> p (h t) l"), axis=AX.X, op=ALU.add).then_inc(diag_ready, 1)
                dve.wait_ge(big_mm, c + 2)
                for j in range(3):
                    ins = nc.vector.tensor_copy(pr[32 * j:32 * j + 32, :, 32 * (j + 1):CH], heads(bBig)[32 * j:32 * j + 32, :, 32 * (j + 1):CH])
                ins.then_inc(big_stored, 1)
                dve.wait_ge(k_turned, c + 2)
                dve.wait_ge(st_mm, c + 1)
                nc.vector.tensor_copy(kw[:, :, :], heads(bK)).then_inc(kw_ready, 1)

            step(0, None)
            with dve.Fori(0, NCH - 1) as i:
                step(i + 1, i)
            outputs(NCH - 1)

        @block.scalar
        def _(act):
            k.credit(act, base_in, v_staged, q_lower, k_upper, v_ready, placed)
            with act.Fori(0, NCH) as c:
                act.wait_ge(big_mm, c + 1)
                act.wait_ge(k_lower, c * NL + 1)
                nc.scalar.activation(K[:, 0], chunk(kk, c), ACT.Copy)
                nc.scalar.activation(Q[:, 0], chunk(q, c), ACT.Copy).then_inc(base_in, 1)
                act.wait_ge(v_turned, c + 1)
                nc.scalar.activation(v_st[:, :, :], chunk(v, c), ACT.Copy).then_inc(v_staged, 1)
                act.wait_ge(k_turned, c + 1)
                for n, L in enumerate(LEVELS):
                    act.wait_ge(q_upper, c * (NL + 1) + (n + 2))
                    if n:
                        act.wait_ge(q_lower, c * NL + (n + 1))
                        act.wait_ge(k_upper, c * NL + (n + 1))
                        act.wait_ge(k_lower, c * NL + (n + 1))
                    else:
                        act.wait_ge(base_in, c + 2)
                    if n == NL - 1:
                        act.wait_ge(num_done, c + 1)
                    lo, _ = halves(Q, n + 1, L)
                    to, _ = halves(Q, n + 2, L)
                    nc.scalar.activation(to, lo, ACT.Copy).then_inc(q_lower, 1)
                    _, up = halves(K, n, L)
                    _, to = halves(K, n + 1, L)
                    nc.scalar.activation(to, up, ACT.Copy).then_inc(k_upper, 1)
                    if n == 4:
                        act.wait_ge(v_turned, c + 2)
                        act.wait_ge(num_done, c + 1)
                        act.wait_ge(st_mm, c + 1)
                        nc.scalar.activation(v_tok[:, :, :], heads(bV), ACT.Copy).then_inc(v_ready, 1)
                act.wait_ge(diag_ready, c + 2)
                act.wait_ge(num_done, c + 1)
                for j in range(4):
                    ins = nc.scalar.activation(pr[32 * j:32 * j + 32, :, 32 * j:32 * j + 32], diag[32 * j:32 * j + 32, :, :], ACT.Copy)
                ins.then_inc(placed, 1)

        @block.tensor
        def _(pe):
            k.credit(pe, v_turned, small_mm, big_mm, k_turned, st_mm, num_done)
            pe.wait_ge(zeroed, 2)
            with pe.Fori(0, NCH) as c:
                pe.wait_ge(v_staged, c + 2)
                pe.wait_ge(v_ready, c + 1)
                for h in range(4):
                    mm = nc.tensor.transpose(heads(bV)[:, h, :], v_st[:, h, :], k.ident[:, :])
                mm.then_inc(v_turned, 1)
                pe.wait_ge(pick, c + 1)
                for n in range(SMALL):
                    qi, ki = n, max(n - 1, 0)
                    if n == 0:
                        pe.wait_ge(base_in, c + 2)
                    else:
                        pe.wait_ge(q_upper, c * (NL + 1) + (n + 1))
                    if n >= 2:
                        pe.wait_ge(q_lower, c * NL + n)
                        pe.wait_ge(k_lower, c * NL + n)
                        pe.wait_ge(k_upper, c * NL + n)
                    for h in range(4):
                        for j in range(4):
                            out = k.psum[32 * j:32 * j + 32, n // 4, (n % 4) * 128 + h * 32:(n % 4) * 128 + h * 32 + 32]
                            mm = nc.tensor.matmul(out, K[:, ki, h, 32 * j:32 * j + 32], Q[:, qi, h, 32 * j:32 * j + 32],
                                                  start=True, stop=True)
                mm.then_inc(small_mm, 1)
                pe.wait_ge(big_stored, c + 1)
                pe.wait_ge(q_lower, c * NL + 6)
                pe.wait_ge(q_upper, c * (NL + 1) + 7)
                pe.wait_ge(k_lower, c * NL + 6)
                pe.wait_ge(k_upper, c * NL + 6)
                for h in range(4):
                    for s0 in (0, 64):
                        nc.tensor.matmul(heads(bBig)[s0:s0 + 32, h, s0 + 32:s0 + 64], K[:, 5, h, s0:s0 + 32], Q[:, 6, h, s0 + 32:s0 + 64],
                                         start=True, stop=True)
                pe.wait_ge(q_lower, c * NL + 7)
                pe.wait_ge(q_upper, c * (NL + 1) + 8)
                pe.wait_ge(k_lower, c * NL + 7)
                pe.wait_ge(k_upper, c * NL + 7)
                for h in range(4):
                    mm = nc.tensor.matmul(heads(bBig)[0:64, h, 64:128], K[:, 6, h, 0:64], Q[:, 7, h, 64:128], start=True, stop=True)
                mm.then_inc(big_mm, 1)
                pe.wait_ge(kw_ready, c + 1)
                pe.wait_ge(k_lower, c * NL + 8)
                pe.wait_ge(k_upper, c * NL + 8)
                for h in range(4):
                    mm = nc.tensor.transpose(heads(bK)[:, h, :], K[:, NL, h, :], k.ident[:, :])
                mm.then_inc(k_turned, 1)
                pe.wait_ge(v_ready, c + 2)
                pe.wait_ge(q_upper, c * (NL + 1) + 9)
                pe.wait_ge(q_lower, c * NL + 8)
                pe.wait_ge(placed, c + 2)
                pe.wait_ge(big_stored, c + 2)
                pe.wait_ge(o_stored, c + 1)
                pe.wait_ge(st_done, c + 1)
                for h in range(4):
                    nc.tensor.matmul(heads(bN)[:, h, :], pr[:, h, :], v_tok[:, h, :], start=True, stop=False)
                    mm = nc.tensor.matmul(heads(bN)[:, h, :], Q[:, NL + 1, h, :], state[:, h, :], start=False, stop=True)
                mm.then_inc(num_done, 1)
                pe.wait_ge(kw_ready, c + 2)
                pe.wait_ge(st_done, c + 1)
                for h in range(4):
                    mm = nc.tensor.matmul(heads(bC)[:, h, :], kw[:, h, :], v_tok[:, h, :], start=True, stop=True)
                mm.then_inc(st_mm, 1)


def mix_c(k):
    nc = k.nc
    q, kk, v = k.m[:, TQ:TQ + 4, :], k.m[:, TK:TK + 4, :], k.m[:, TV:TV + 4, :]
    (k_st, v_st, v_tok, pr, qs, kw, state, decay, gq, gk, gc) = k.work(
        k.X0, 32768, k_st=[P, 4, CH], v_st=[P, 4, CH], v_tok=[P, 4, DH], pr=[P, 4, CH], qs=[P, 4, CH],
        kw=[P, 4, DH], state=[P, 4, DH], decay=[P, 4, CH], gq=[P, 4, CH], gk=[P, 4, 1], gc=[P, 4, 1])
    (tab_in, zeroed, v_staged, v_ready, o_stored, k_staged, qs_ready, p_ready, kw_ready, decayed, st_done, tv_done, s_done,
     tk_done, num_done, st_mm) = k.sems(
        "c", "tables_in", "zeroed", "v_staged", "v_ready", "o_stored", "k_staged", "qs_ready", "p_ready", "kw_ready",
        "decayed", "state_done", "v_turned", "scores", "k_turned", "numerator", "state_mm")
    bS, bV, bK, bN, bC = 0, 1, 2, 3, 4

    def heads(b):
        return k.psum[:, b, :].rearrange("p (h n) -> p h n", h=4)

    with nc.Block() as block:
        @block.sync
        def _(sp):
            for buf, name in ((decay, "decay"), (gq, "gq"), (gk, "gk"), (gc, "gc")):
                at, n = TAB[name]
                sp.dma_start(buf[:, :, :].rearrange("p a n -> p (a n)"), k.tables[:, at:at + n]).then_inc(tab_in, 16)
            sp.wait_ge(tab_in, 64)

        @block.gpsimd
        def _(pool):
            k.clear_before(pool)
            k.credit(pool, qs_ready)
            pool.memset(state[:, :, :], 0.0).then_inc(zeroed, 1)
            pool.wait_ge(tab_in, 64)
            with pool.Fori(0, NCH) as c:
                pool.wait_ge(num_done, c + 1)
                pool.tensor_tensor(qs[:, :, :], chunk(q, c), gq[:, :, :], ALU.mult).then_inc(qs_ready, 1)

        @block.scalar
        def _(act):
            k.credit(act, v_staged, v_ready)
            with act.Fori(0, NCH) as c:
                act.wait_ge(tv_done, c + 1)
                nc.scalar.activation(v_st[:, :, :], chunk(v, c), ACT.Copy).then_inc(v_staged, 1)
                act.wait_ge(tv_done, c + 2)
                act.wait_ge(num_done, c + 1)
                act.wait_ge(st_mm, c + 1)
                nc.scalar.activation(v_tok[:, :, :], heads(bV), ACT.Copy).then_inc(v_ready, 1)

        @block.vector
        def _(dve):
            k.credit(dve, k_staged, p_ready, kw_ready, o_stored, decayed, st_done)
            dve.wait_ge(zeroed, 1)
            dve.wait_ge(tab_in, 64)

            def outputs(c):
                dve.wait_ge(num_done, c + 2)
                nc.vector.tensor_scalar(chunk(v, c), heads(bN), 1.0, None, ALU.mult).then_inc(o_stored, 1)
                nc.vector.tensor_tensor(state[:, :, :], state[:, :, :], gc[:, :, :].to_broadcast([P, 4, DH]), ALU.mult).then_inc(decayed, 1)
                dve.wait_ge(decayed, c + 2)
                dve.wait_ge(st_mm, c + 2)
                nc.vector.tensor_tensor(state[:, :, :], heads(bC), state[:, :, :], ALU.add).then_inc(st_done, 1)

            def step(c, before):
                dve.wait_ge(s_done, c + 1)
                dve.wait_ge(tk_done, c + 1)
                nc.vector.tensor_copy(k_st[:, :, :], chunk(kk, c)).then_inc(k_staged, 1)
                if before is not None:
                    outputs(before)
                dve.wait_ge(s_done, c + 2)
                dve.wait_ge(num_done, c + 1)
                nc.vector.tensor_tensor(pr[:, :, :], heads(bS), decay[:, :, :], ALU.mult).then_inc(p_ready, 1)
                dve.wait_ge(tk_done, c + 2)
                dve.wait_ge(st_mm, c + 1)
                nc.vector.tensor_tensor(kw[:, :, :], heads(bK), gk[:, :, :].to_broadcast([P, 4, DH]), ALU.mult).then_inc(kw_ready, 1)

            step(0, None)
            with dve.Fori(0, NCH - 1) as i:
                step(i + 1, i)
            outputs(NCH - 1)

        @block.tensor
        def _(pe):
            k.credit(pe, tv_done, s_done, tk_done, num_done, st_mm)
            pe.wait_ge(zeroed, 1)
            with pe.Fori(0, NCH) as c:
                pe.wait_ge(v_staged, c + 2)
                pe.wait_ge(v_ready, c + 1)
                for h in range(4):
                    mm = nc.tensor.transpose(heads(bV)[:, h, :], v_st[:, h, :], k.ident[:, :])
                mm.then_inc(tv_done, 1)
                pe.wait_ge(k_staged, c + 2)
                pe.wait_ge(p_ready, c + 1)
                for h in range(4):
                    mm = nc.tensor.matmul(heads(bS)[:, h, :], k_st[:, h, :], q[:, h, bass.ds(c * CH, CH)], start=True, stop=True)
                mm.then_inc(s_done, 1)
                pe.wait_ge(kw_ready, c + 1)
                for h in range(4):
                    mm = nc.tensor.transpose(heads(bK)[:, h, :], k_st[:, h, :], k.ident[:, :])
                mm.then_inc(tk_done, 1)
                pe.wait_ge(v_ready, c + 2)
                pe.wait_ge(qs_ready, c + 2)
                pe.wait_ge(p_ready, c + 2)
                pe.wait_ge(st_done, c + 1)
                pe.wait_ge(o_stored, c + 1)
                for h in range(4):
                    nc.tensor.matmul(heads(bN)[:, h, :], pr[:, h, :], v_tok[:, h, :], start=True, stop=False)
                    mm = nc.tensor.matmul(heads(bN)[:, h, :], qs[:, h, :], state[:, h, :], start=False, stop=True)
                mm.then_inc(num_done, 1)
                pe.wait_ge(kw_ready, c + 2)
                for h in range(4):
                    mm = nc.tensor.matmul(heads(bC)[:, h, :], kw[:, h, :], v_tok[:, h, :], start=True, stop=True)
                mm.then_inc(st_mm, 1)


def mix_d(k):
    nc = k.nc
    v = k.m[:, TV:TV + 4, :]
    u, beta, turned_a, prod = k.work(k.X0, 32768, u=[P, 2, T], beta=[P, 2, T], at=[P, 2, T], prod=[P, T + 8])
    q_st, k_st, v_st = k.work(k.M0 + TGA * T * 4, 16384, q_st=[P, 2, T], k_st=[P, T], v_st=[P, T])
    (tab_in, v_turned, v_back, q_zero, q_staged, k_staged, v_staged, z_done, sig_done, ready, scanned, a_done, a_turned,
     at_stored, av_done, y_stored) = k.sems(
        "d", "tables_in", "v_turned", "v_back", "q_zero", "q_staged", "k_staged", "v_staged", "z", "sigmoids", "ready",
        "scanned", "weights", "weights_turned", "weights_back", "av", "y_stored")
    barrier, = k.work(k.X0 + 28672 + 64, 4096, barrier=[P, P])
    NB = T // P
    PER = 2 * NB
    row_block = list(range(NB)) + list(range(NB))[::-1]

    with nc.Block() as block:
        @block.sync
        def _(sp):
            at, n = TAB["barrier"]
            sp.dma_start(barrier[:, :], k.tables[:, at:at + n]).then_inc(tab_in, 16)
            sp.wait_ge(tab_in, 16)

        @block.scalar
        def _(act):
            k.credit(act, q_staged, sig_done, at_stored)
            for n in range(8):
                act.wait_ge(v_turned, n + 1)
                ft, g = n // 2, n % 2
                nc.scalar.activation(v[:, ft, g * HALF:(g + 1) * HALF], k.bank(n % 4), ACT.Copy).then_inc(v_back, 1)
            act.wait_ge(q_zero, 1)

            def sigmoids(hp, n):
                w, par = P * (row_block[n] + 1), n % 2
                act.wait_ge(z_done, hp * PER + (n + 2))
                nc.scalar.activation(u[:, par, 0:w], k.pair(par)[:, 0:w], ACT.Sigmoid, scale=-SCALE_D)
                nc.scalar.activation(beta[:, par, 0:w], k.pair(par)[:, 0:w], ACT.Sigmoid, scale=SCALE_D).then_inc(sig_done, 1)

            with act.Fori(0, HEADS) as hp:
                act.wait_ge(z_done, hp * PER + 1)
                nc.scalar.activation(q_st[0:DH_D, 0, :], flat(k.m[0:DH_D, bass.ds(hp + TQ, 1), :]), ACT.Copy)
                nc.scalar.activation(q_st[DH_D:P, 1, :], flat(k.m[DH_D:P, bass.ds(hp + TQ, 1), :]), ACT.Copy).then_inc(q_staged, 1)
                act.wait_ge(a_turned, hp * PER + 1)
                sigmoids(hp, 0)
                sigmoids(hp, 1)
                for n in range(PER):
                    w, par = P * (row_block[n] + 1), n % 2
                    act.wait_ge(a_turned, hp * PER + (n + 2))
                    if n >= 2:
                        act.wait_ge(av_done, hp * PER + n)
                    nc.scalar.activation(turned_a[:, par, 0:w], k.pair(2)[:, 0:w], ACT.Copy).then_inc(at_stored, 1)
                    if n + 2 < PER:
                        sigmoids(hp, n + 2)

        @block.gpsimd
        def _(pool):
            k.clear_before(pool)
            k.credit(pool, v_staged)
            pool.memset(q_st[:, :, :], 0.0).then_inc(q_zero, 1)
            pool.wait_ge(v_back, 8)
            with pool.Fori(0, HEADS) as hp:
                pool.wait_ge(av_done, hp * PER + 1)
                pool.tensor_tensor(v_st[:, :], flat(v[:, bass.ds(hp, 1), :]), k.ones[:, 0:1].to_broadcast([P, T]), ALU.mult).then_inc(v_staged, 1)

        @block.vector
        def _(dve):
            k.credit(dve, k_staged, scanned, a_done, y_stored)
            nc.vector.memset(prod[:, 0:1], 1.0).then_inc(ready, 1)
            dve.wait_ge(ready, 1)
            with dve.Fori(0, HEADS) as hp:
                dve.wait_ge(z_done, hp * PER + 1)
                nc.vector.tensor_copy(k_st[:, ::-1], flat(k.m[:, bass.ds(hp + TK, 1), :])).then_inc(k_staged, 1)
                for n in range(PER):
                    w, par = P * (row_block[n] + 1), n % 2
                    dve.wait_ge(sig_done, hp * PER + (n + 2))
                    dve.wait_ge(a_done, hp * PER + (n + 1))
                    nc.vector.tensor_tensor_scan(prod[:, 1:w + 1], u[:, par, 0:w], u[:, par, 0:w], 1.0, ALU.mult, ALU.bypass).then_inc(scanned, 1)
                    dve.wait_ge(scanned, hp * PER + (n + 2))
                    nc.vector.tensor_tensor(u[:, par, 0:w][:, ::-1], beta[:, par, 0:w], prod[:, 0:w], ALU.mult).then_inc(a_done, 1)
                dve.wait_ge(av_done, hp * PER + (PER + 1))
                nc.vector.tensor_scalar(flat(k.m[:, bass.ds(hp + TGB, 1), :]), k.pair(3), 1.0, None, ALU.mult).then_inc(y_stored, 1)

        @block.tensor
        def _(pe):
            k.credit(pe, z_done, a_turned, av_done)
            for n in range(8):
                ft, g = n // 2, n % 2
                if n >= 4:
                    pe.wait_ge(v_back, n - 3)
                for c in range(4):
                    at = g * HALF + c * P
                    mm = nc.tensor.transpose(k.bank(n % 4)[:, c * P:(c + 1) * P], v[:, ft, at:at + P], k.ident[:, :])
                mm.then_inc(v_turned, 1)
            pe.wait_ge(v_back, 8)
            pe.wait_ge(tab_in, 16)

            def scores(hp, n):
                tb, hh, par = row_block[n], n // NB, n % 2
                w = P * (tb + 1)
                if n >= 2:
                    pe.wait_ge(sig_done, hp * PER + n)
                for a in range(0, w, HALF):
                    b = min(w, a + HALF)
                    mm = nc.tensor.matmul(k.pair(par)[:, a:b], q_st[:, hh, tb * P:(tb + 1) * P], k_st[:, T - w + a:T - w + b],
                                          start=True, stop=(a > 0))
                    if a == 0:
                        mm = nc.tensor.matmul(k.pair(par)[:, 0:P], k.ident[:, :], barrier[:, :], start=False, stop=True)
                mm.then_inc(z_done, 1)

            def turn(hp, n):
                pe.wait_ge(a_done, hp * PER + (n + 2))
                pe.wait_ge(at_stored, hp * PER + (n + 1))
                for c in range(row_block[n] + 1):
                    mm = nc.tensor.transpose(k.pair(2)[:, c * P:(c + 1) * P], u[:, n % 2, c * P:(c + 1) * P], k.ident[:, :])
                mm.then_inc(a_turned, 1)

            def with_v(hp, n):
                tb, hh, par = row_block[n], n // NB, n % 2
                pe.wait_ge(at_stored, hp * PER + (n + 2))
                for c in range(tb + 1):
                    at = c * P + hh * DH_D
                    mm = nc.tensor.matmul(k.pair(3)[DH_D * hh:DH_D * (hh + 1), tb * P:(tb + 1) * P],
                                          v_st[:, at:at + DH_D], turned_a[:, par, c * P:(c + 1) * P],
                                          start=(c == 0), stop=(c == tb))
                mm.then_inc(av_done, 1)

            with pe.Fori(0, HEADS) as hp:
                pe.wait_ge(q_staged, hp + 2)
                pe.wait_ge(k_staged, hp + 2)
                pe.wait_ge(sig_done, hp * PER + 1)
                scores(hp, 0)
                scores(hp, 1)
                for n in range(PER):
                    turn(hp, n)
                    if n + 2 < PER:
                        scores(hp, n + 2)
                    if n == 1:
                        pe.wait_ge(v_staged, hp + 2)
                        pe.wait_ge(y_stored, hp + 1)
                    if n:
                        with_v(hp, n - 1)
                with_v(hp, PER - 1)


def hybrid_trunk(nc, xT, params, tables, w_ada, c_rows, w_units, outT, stop=None, dump=None):
    with ExitStack() as ctx:
        k = Trunk(nc, ctx, xT, params, tables, w_ada, c_rows, w_units, outT)
        steps = [
            ("start", lambda: start(k)),
            ("projA", lambda: project(k, "projA", N_PROJ_A, [
                ("conv", TQ, ("b_even", 0), None, 8),
                ("rows", None, None, None, 1),
                ("gate_sigmoid", TGA, ("b_even", 8), "mlstm_norm", 4),
                ("copy", TV, ("b_even", 12), None, 4)],
                gate_rows=tuple(k.m[0:4, TGB + r, :] for r in range(4)), norm=(k.modA[:, 0, :], k.mod[:, 0, 0:8]), rstd_before=True)),
            ("mixA", lambda: mix_a(k)),
            ("projB", lambda: project(k, "projB", N_PROJ_B, [
                ("silu", TQ, ("b_even", 16), None, 4),
                ("forget", TK, ("b_even", 20), None, 4),
                ("gate_silu", TGB, ("b_even", 28), "hgrn_norm", 4),
                ("copy", TV, ("b_even", 24), None, 4)], f_tile=k.x[:, 0:4, :], rest_of_ada=True, finish=("finA", TGA, True))),
            ("mixB", lambda: mix_b(k, k.x[:, 0:4, :])),
            ("out0", lambda: out_project(k, "out0", 0, ("finB", TGB), (0, 1, 2, 3, 4, 5, 6, 7))),
            ("ffn0", lambda: ffn(k, "ffn0", 0, (k.modA[:, 1, :], k.mod[:, 0, 24:32]))),
            ("projD", lambda: project(k, "projD", N_PROJ_D, [
                ("copy", TQ, ("b_odd", 16), None, 4),
                ("copy", TK, ("b_odd", 20), None, 4),
                ("copy", TV, ("b_odd", 24), None, 4)], norm=(k.modA[:, 2, :], k.mod[:, 1, 0:8]), spill=True)),
            ("mixD", lambda: mix_d(k)),
            ("projC", lambda: project(k, "projC", N_PROJ_C, [
                ("rotary", TQ, ("b_odd", 0), None, 8),
                ("gate_silu", TGA, ("b_odd", 12), "ret_norm", 4),
                ("copy", TV, ("b_odd", 8), None, 4)])),
            ("mixC", lambda: mix_c(k)),
            ("out1", lambda: out_project(k, "out1", 1, ("finC", TGA), (4, 5, 6, 7, 0, 1, 2, 3))),
            ("ffn1", lambda: ffn(k, "ffn1", 1, (k.modA[:, 3, :], k.mod[:, 1, 24:32]))),
            ("final", lambda: final_norm(k, k.par[:, COL["norm_final"]:COL["norm_final"] + 8])),
        ]
        for name, step in steps:
            k.phase(step)
            if name == stop:
                k.phase(lambda: dump(k))
                break
        k.held.close()


def make_tables():
    t = np.zeros((P, N_TAB), np.float64)

    def put(name, a):
        at, n = TAB[name]
        t[0:a.shape[0], at:at + n] = a.reshape(a.shape[0], n)
    i = np.arange(P)
    put("ident", np.eye(P))
    put("ones", np.ones((P, P)))
    put("causal", np.where(i[:, None] <= i[None, :], 0.0, -1e30))
    lv = np.zeros((P, SMALL, 32))
    s, u = (i % 32)[:, None], np.arange(32)[None, :]
    lv[:, 0] = s == u
    for n in range(1, SMALL):
        L = 2 ** (n - 1)
        lv[:, n] = (s // (2 * L) == u // (2 * L)) & (s % (2 * L) < L) & (u % (2 * L) >= L)
    put("levels", lv)
    put("sel", np.repeat(np.eye(4)[:, :, None], P, axis=2))
    strict = (i[:, None] + i[None, :]) > P - 1
    put("barrier", np.where(strict, 0.0, -1e30))
    gamma = np.log1p(-(2.0 ** (-5.0 - np.arange(HEADS))))
    lag = i[None, :] - i[:, None]
    put("decay", np.where(lag[:, None, :] >= 0, np.exp(np.maximum(lag, 0)[:, None, :] * gamma[None, :, None]), 0.0) * SCALE_A)
    put("gq", np.broadcast_to(np.exp((i + 1)[None, None, :] * gamma[None, :, None]), (P, HEADS, P)) * SCALE_A)
    put("gk", np.exp((P - 1 - i)[:, None] * gamma[None, :]))
    put("gc", np.broadcast_to(np.exp(P * gamma)[None, :], (P, HEADS)))
    inv = (np.float32(10000.0) ** (-np.arange(0, DH, 2, dtype=np.float32) / np.float32(DH))).astype(np.float32)
    ang = (np.arange(T, dtype=np.float32)[None, :] * inv[:, None]).astype(np.float64)
    put("cos", np.tile(np.cos(ang), (2, 1)))
    put("sin", np.concatenate([-np.sin(ang), np.sin(ang)]))
    return t.astype(np.float32)


def lay_out(x, c, w_ada, b_ada, norm_mix, norm_ffn, norm_final, w_in_even, b_in_even, conv_qk_w, conv_qk_b, mlstm_f_bias,
            mlstm_norm, hgrn_lb_logits, hgrn_norm, w_in_odd, b_in_odd, ret_norm, w_out, ffn_up, ffn_conv_w, ffn_conv_b, ffn_down):
    def feature_columns(a):
        a = np.asarray(a)
        return np.moveaxis(a.reshape(-1, P), 0, 1)

    def units(w):
        return w.reshape(KT, P, -1, P).transpose(2, 1, 0, 3).reshape(-1, P, KT * P)

    G = GROUP_W
    be, bo = b_in_even[0], b_in_odd[0]
    even = w_in_even[0]
    qk, va, oa = slice(0, 2 * G), slice(2 * G, 3 * G), slice(3 * G, 4 * G)
    ia, fa = slice(4 * G, 4 * G + 4), slice(4 * G + 4, 4 * G + 8)
    rest = 4 * G + 8
    qb, fb, ib, gb = (slice(rest + i * G, rest + (i + 1) * G) for i in range(4))
    rows = np.zeros((D, P), np.float32)
    rows[:, 0:4] = even[:, ia]
    rows[:, 32:36] = even[:, fa]
    odd = w_in_odd[0]
    qc, kc, vc, gc, qd, kd, vd = (slice(i * G, (i + 1) * G) for i in range(7))

    def ffn_units(layer):
        up = units(ffn_up[layer])
        dn = ffn_down[layer].reshape(GROUPS, 2, P, 2, HALF).transpose(0, 3, 2, 1, 4).reshape(GROUPS, 2, P, 2 * HALF)
        out = []
        for g in range(GROUPS + 1):
            if g < GROUPS:
                out += [up[2 * g], up[FFT + 2 * g], up[2 * g + 1], up[FFT + 2 * g + 1]]
            if g:
                out += [dn[g - 1, 0], dn[g - 1, 1]]
        return np.stack(out)

    w_units = np.concatenate([
        units(even[:, qk]), units(rows), units(even[:, oa]), units(even[:, va]),
        units(even[:, qb]), units(even[:, fb]), units(even[:, gb]), units(even[:, ib]),
        units(w_out[0]), ffn_units(0),
        units(odd[:, qd]), units(odd[:, kd]), units(odd[:, vd]),
        units(odd[:, qc]), units(odd[:, kc]), units(odd[:, gc]), units(odd[:, vc]),
        units(w_out[1]), ffn_units(1)])

    par = np.zeros((P, COL["all"]), np.float32)

    def put(name, a):
        par[0:a.shape[0], COL[name]:COL[name] + a.shape[1]] = a
    put("b_ada", feature_columns(b_ada))
    put("norm_mix", feature_columns(norm_mix))
    put("norm_ffn", feature_columns(norm_ffn))
    put("norm_final", feature_columns(norm_final))
    put("b_even", feature_columns(np.concatenate([be[qk], be[oa], be[va], be[qb], be[fb], be[ib], be[gb]])))
    gate = np.zeros((P, 1), np.float32)
    gate[0:4, 0] = be[ia]
    gate[32:36, 0] = be[fa]
    put("b_gate", gate)
    put("f_bias", mlstm_f_bias[0][:, None])
    put("conv_qk_w", feature_columns(conv_qk_w[0]))
    put("conv_qk_b", feature_columns(conv_qk_b))
    put("mlstm_norm", feature_columns(mlstm_norm))
    put("lb_logits", feature_columns(hgrn_lb_logits))
    put("hgrn_norm", feature_columns(hgrn_norm))
    put("b_odd", feature_columns(bo))
    put("ret_norm", feature_columns(ret_norm))
    fw = feature_columns(ffn_conv_w)
    n = 6 * FFT
    put("ffn_w0", fw[:, :n])
    put("ffn_w1", fw[:, n:])
    put("ffn_b", feature_columns(ffn_conv_b))
    put("eps", np.full((P, 1), EPS, np.float32))

    return {
        "xT": np.ascontiguousarray(x[0].T.reshape(KT, P, T).transpose(1, 0, 2).reshape(P, KT * T)),
        "params": par,
        "tables": make_tables(),
        "w_ada": np.ascontiguousarray(w_ada.reshape(D, 12, 4, P).transpose(1, 3, 2, 0)),
        "c_rows": np.ascontiguousarray(np.broadcast_to(c.reshape(1, D), (P, D))),
        "w_units": np.ascontiguousarray(w_units),
    }


def kernel(**inputs):
    import concourse.bacc as bacc
    from concourse.bass_utils import run_bass_kernel_spmd

    arrays = lay_out(**{n: np.asarray(a) for n, a in inputs.items()})
    nc = bacc.Bacc("TRN2", target_bir_lowering=False, num_devices=1)
    args = [nc.dram_tensor(n, a.shape, mybir.dt.from_np(a.dtype), kind="ExternalInput").ap() for n, a in arrays.items()]
    out = nc.dram_tensor("outT", (P, KT, T), F32, kind="ExternalOutput").ap()
    hybrid_trunk(nc, *args, out)
    got = run_bass_kernel_spmd(nc, [arrays], core_ids=[0]).results[0]["outT"]
    return np.ascontiguousarray(got.transpose(1, 0, 2).reshape(D, T).T).reshape(1, T, D)
```
